# Optimizing a Trainium2 kernel written in Bass

```python
import math
import jax, jax.numpy as jnp
from jax import lax
import numpy as np

D_MODEL = 1024
BATCH = 1
SEQ = 512
DEPTH = 1

PLE_DIM = 256
HEAD_DIM = 64
MOBA_HEADS = 8
MOBA_BLOCK = 256
MOBA_TOPK = 3
MOBA_Q_CHUNK = 32
NSA_HEADS = 8
NSA_KV_GROUPS = 2
NSA_HPG = NSA_HEADS // NSA_KV_GROUPS
NSA_CMP_LEN = 32
NSA_CMP_STRIDE = 16
NSA_CMP_HIDDEN = 2 * HEAD_DIM
NSA_SEL_BLOCK = 64
NSA_SEL_TOPN = 16
NSA_WINDOW = 512
NSA_Q_CHUNK = 64
WIN_Q_BLOCK = 128
REL_BUCKETS = 32
REL_MAX_DIST = 128
N_ATTN_HEADS = MOBA_HEADS + NSA_HEADS
MOBA_WIDTH = MOBA_HEADS * HEAD_DIM
NSA_WIDTH = NSA_HEADS * HEAD_DIM
NSA_KV_WIDTH = NSA_KV_GROUPS * HEAD_DIM
NSA_GATE_COLS = 3 * NSA_HEADS
MERGE_COLS = 2 * D_MODEL
IN_SIZES = (MOBA_WIDTH, MOBA_WIDTH, MOBA_WIDTH, NSA_WIDTH) + (NSA_KV_WIDTH,) * 6 + (NSA_GATE_COLS, MERGE_COLS)
IN_COLS = 3 * MOBA_WIDTH + NSA_WIDTH + 6 * NSA_KV_WIDTH + NSA_GATE_COLS + MERGE_COLS
D_FF = 128 * (-(-8 * D_MODEL // (3 * 128)))
CONV_W = 3
RMS_EPS = 1e-6
SCALE = HEAD_DIM ** -0.5

kernel_name = 'hybrid_moba_nsa_convffn_ple'

def rms_norm(x, gain):
    x32 = x.astype(jnp.float32)
    y = x32 * lax.rsqrt(jnp.mean(x32 * x32, axis=-1, keepdims=True) + RMS_EPS)
    return y.astype(x.dtype) * gain

def rel_bucket(dist):
    n = jnp.maximum(jnp.asarray(dist, jnp.int32), 0)
    max_exact = REL_BUCKETS // 2
    nf = jnp.maximum(n, 1).astype(jnp.float32)
    large = max_exact + (jnp.log(nf / max_exact) / math.log(REL_MAX_DIST / max_exact)
                         * (REL_BUCKETS - max_exact)).astype(jnp.int32)
    return jnp.where(n < max_exact, n, jnp.minimum(large, REL_BUCKETS - 1))

def masked_softmax_safe(logits, mask):
    z = jnp.where(mask, logits, -jnp.inf)
    m = jnp.max(z, axis=-1, keepdims=True)
    e = jnp.exp(z - jnp.where(jnp.isfinite(m), m, 0.0))
    s = jnp.sum(e, axis=-1, keepdims=True)
    return e / jnp.where(s > 0, s, 1.0)

def to_heads(t, n):
    B, S, _ = t.shape
    return t.reshape(B, S, n, HEAD_DIM).transpose(0, 2, 1, 3)

def causal_dwconv(u, w, b):
    c = u.shape[-1]
    y = lax.conv_general_dilated(u, w[:, None, :], window_strides=(1,), padding=[(CONV_W - 1, 0)],
                                 dimension_numbers=('NWC', 'WIO', 'NWC'), feature_group_count=c)
    return y + b

def compress_blocks(t, pos, w1, w2):
    B, G, S, dh = t.shape
    nc = (S - NSA_CMP_LEN) // NSA_CMP_STRIDE + 1
    idx = np.arange(nc)[:, None] * NSA_CMP_STRIDE + np.arange(NSA_CMP_LEN)[None, :]
    blk = (t[:, :, idx] + pos).reshape(B, G, nc, NSA_CMP_LEN * dh)
    return jax.nn.gelu(blk @ w1) @ w2

def moba_attention(q, k, v, tab):
    B, H, S, dh = q.shape
    L, C = MOBA_BLOCK, MOBA_Q_CHUNK
    nb = -(-S // L)
    sp = nb * L
    padw = ((0, 0), (0, 0), (0, sp - S), (0, 0))
    qp, kp, vp = jnp.pad(q, padw), jnp.pad(k, padw), jnp.pad(v, padw)
    kb = kp.reshape(B, H, nb, L, dh)
    vb = vp.reshape(B, H, nb, L, dh)
    n_real = jnp.asarray(np.minimum(S - np.arange(nb) * L, L), k.dtype)
    kmean = kb.sum(axis=3) / n_real[:, None]
    qblk = jnp.arange(sp) // L
    past = jnp.arange(nb)[None, :] < qblk[:, None]
    gate = jnp.einsum('bhsd,bhnd->bhsn', qp, kmean).astype(jnp.float32)
    gate = jnp.where(past, gate, -jnp.inf)
    ksel = min(MOBA_TOPK, max(nb - 1, 1))
    _, sel = lax.top_k(gate, ksel)
    sel_ok = sel < qblk[:, None]
    nc = sp // C

    def chunks(t):
        return jnp.moveaxis(t.reshape(B, H, nc, C, *t.shape[3:]), 2, 0)

    bi = jnp.arange(B)[:, None, None, None]
    hi = jnp.arange(H)[None, :, None, None]
    hi5 = hi[..., None]

    def query_block(args):
        qc, ic, okc, c0 = args
        tpos = c0 + jnp.arange(C)
        own = c0 // L
        k_own = lax.dynamic_index_in_dim(kb, own, axis=2, keepdims=False)
        v_own = lax.dynamic_index_in_dim(vb, own, axis=2, keepdims=False)
        kpos_own = own * L + jnp.arange(L)
        l_own = (jnp.einsum('bhcd,bhkd->bhck', qc, k_own).astype(jnp.float32) * SCALE
                 + tab[:, rel_bucket(tpos[:, None] - kpos_own[None, :])].astype(jnp.float32))
        l_own = jnp.where(kpos_own[None, :] <= tpos[:, None], l_own, -jnp.inf)
        k_g = kb[bi, hi, ic]
        v_g = vb[bi, hi, ic]
        kpos_g = ic[..., None] * L + jnp.arange(L)
        l_g = (jnp.einsum('bhcd,bhcnkd->bhcnk', qc, k_g).astype(jnp.float32) * SCALE
               + tab[hi5, rel_bucket(tpos[:, None, None] - kpos_g)].astype(jnp.float32))
        l_g = jnp.where(okc[..., None], l_g, -jnp.inf).reshape(B, H, C, ksel * L)
        probs = jax.nn.softmax(jnp.concatenate([l_own, l_g], axis=-1), axis=-1).astype(v.dtype)
        p_own = probs[..., :L]
        p_g = probs[..., L:].reshape(B, H, C, ksel, L)
        return (jnp.einsum('bhck,bhkd->bhcd', p_own, v_own)
                + jnp.einsum('bhcnk,bhcnkd->bhcd', p_g, v_g))

    starts = jnp.arange(nc, dtype=jnp.int32) * C
    out = lax.map(query_block, (chunks(qp), chunks(sel), chunks(sel_ok), starts))
    return jnp.moveaxis(out, 0, 2).reshape(B, H, sp, dh)[:, :, :S]

def nsa_attention(q, k_cmp_raw, v_cmp_raw, k_slc, v_slc, k_win, v_win, gate_logits, k_gain,
                  cmp_k, cmp_v, tab):
    B, G, R, S, dh = q.shape
    f32 = jnp.float32
    tpos = jnp.arange(S)
    kc = rms_norm(compress_blocks(k_cmp_raw, *cmp_k), k_gain[0])
    vc = compress_blocks(v_cmp_raw, *cmp_v)
    n_cmp = kc.shape[2]
    c_end = jnp.arange(n_cmp) * NSA_CMP_STRIDE + NSA_CMP_LEN - 1
    l_cmp = (jnp.einsum('bgrsd,bgnd->bgrsn', q, kc).astype(f32) * SCALE
             + tab[:, :, rel_bucket(tpos[:, None] - c_end[None, :])].astype(f32))
    p_cmp = masked_softmax_safe(l_cmp, c_end[None, :] <= tpos[:, None])
    o_cmp = jnp.einsum('bgrsn,bgnd->bgrsd', p_cmp.astype(vc.dtype), vc)
    SB = NSA_SEL_BLOCK
    n_sel = S // SB
    ci = np.arange(n_cmp)[:, None] * NSA_CMP_STRIDE
    sj = np.arange(n_sel)[None, :] * SB
    overlap = jnp.asarray(((ci < sj + SB) & (ci + NSA_CMP_LEN > sj)).astype(np.float32))
    imp = jnp.einsum('bgrsn,nj->bgsj', p_cmp, overlap)
    j = jnp.arange(n_sel)[None, :]
    own = (tpos // SB)[:, None]
    imp = jnp.where((j == 0) | (j == own) | (j == own - 1), jnp.inf, imp)
    imp = jnp.where(j > own, -jnp.inf, imp)
    ntop = min(NSA_SEL_TOPN, n_sel)
    _, sel = lax.top_k(imp, ntop)
    sel_ok = sel <= own
    ksb = rms_norm(k_slc, k_gain[1]).reshape(B, G, n_sel, SB, dh)
    vsb = v_slc.reshape(B, G, n_sel, SB, dh)
    C = NSA_Q_CHUNK
    nc = S // C
    q_ch = jnp.moveaxis(q.reshape(B, G, R, nc, C, dh), 3, 0)
    sel_ch = jnp.moveaxis(sel.reshape(B, G, nc, C, ntop), 2, 0)
    ok_ch = jnp.moveaxis(sel_ok.reshape(B, G, nc, C, ntop), 2, 0)
    bi = jnp.arange(B)[:, None, None, None]
    gi = jnp.arange(G)[None, :, None, None]
    gi6 = jnp.arange(G)[None, :, None, None, None, None]
    ri6 = jnp.arange(R)[None, None, :, None, None, None]

    def query_block(args):
        qc, ic, okc, c0 = args
        tq = c0 + jnp.arange(C)
        k_g = ksb[bi, gi, ic]
        v_g = vsb[bi, gi, ic]
        kpos = ic[..., None] * SB + jnp.arange(SB)
        mask = okc[..., None] & (kpos <= tq[:, None, None])
        bias = tab[gi6, ri6, rel_bucket(tq[:, None, None] - kpos)[:, :, None]]
        lg = jnp.einsum('bgrcd,bgcnkd->bgrcnk', qc, k_g).astype(f32) * SCALE + bias.astype(f32)
        lg = jnp.where(mask[:, :, None], lg, -jnp.inf).reshape(B, G, R, C, ntop * SB)
        probs = jax.nn.softmax(lg, axis=-1).astype(v_g.dtype).reshape(B, G, R, C, ntop, SB)
        return jnp.einsum('bgrcnk,bgcnkd->bgrcd', probs, v_g)

    o_slc = lax.map(query_block, (q_ch, sel_ch, ok_ch, jnp.arange(nc, dtype=jnp.int32) * C))
    o_slc = jnp.moveaxis(o_slc, 0, 3).reshape(B, G, R, S, dh)
    QB = WIN_Q_BLOCK
    nq = S // QB
    nw = NSA_WINDOW // QB
    kw_len = (nw + 1) * QB
    padw = ((0, 0), (0, 0), (NSA_WINDOW, 0), (0, 0))
    kwp = jnp.pad(rms_norm(k_win, k_gain[2]), padw).reshape(B, G, nq + nw, QB, dh)
    vwp = jnp.pad(v_win, padw).reshape(B, G, nq + nw, QB, dh)
    widx = np.arange(nq)[:, None] + np.arange(nw + 1)[None, :]
    kband = kwp[:, :, widx].reshape(B, G, nq, kw_len, dh)
    vband = vwp[:, :, widx].reshape(B, G, nq, kw_len, dh)
    dist = np.arange(QB)[:, None] + NSA_WINDOW - np.arange(kw_len)[None, :]
    kabs = np.arange(nq)[:, None, None] * QB - NSA_WINDOW + np.arange(kw_len)[None, None, :]
    wmask = (dist >= 0) & (dist < NSA_WINDOW) & (kabs >= 0)
    lw = (jnp.einsum('bgrnqd,bgnkd->bgrnqk', q.reshape(B, G, R, nq, QB, dh), kband).astype(f32) * SCALE
          + tab[:, :, rel_bucket(dist)][:, :, None].astype(f32))
    pw = jax.nn.softmax(jnp.where(wmask, lw, -jnp.inf), axis=-1).astype(vband.dtype)
    o_win = jnp.einsum('bgrnqk,bgnkd->bgrnqd', pw, vband).reshape(B, G, R, S, dh)
    gates = jax.nn.sigmoid(gate_logits).reshape(B, S, 3, G, R).transpose(2, 0, 3, 4, 1)[..., None]
    o = gates[0] * o_cmp + gates[1] * o_slc + gates[2] * o_win
    return o.transpose(0, 3, 1, 2, 4).reshape(B, S, G * R * dh)

def setup_inputs(seed: int = 0) -> dict:
    key = jax.random.key(seed)
    ks = jax.random.split(key, 32)
    f32 = jnp.float32
    L, dh = DEPTH, HEAD_DIM

    def nrm(k, shape, fan_in):
        return jax.random.normal(k, shape, f32) * fan_in ** -0.5

    def gain(k, shape):
        return 1.0 + 0.05 * jax.random.normal(k, shape, f32)

    return {
        'x': jax.random.normal(ks[0], (BATCH, SEQ, D_MODEL), f32),
        'p': jax.random.normal(ks[1], (DEPTH, BATCH, SEQ, PLE_DIM), f32),
        'rel_bias': 0.5 * jax.random.normal(ks[2], (N_ATTN_HEADS, REL_BUCKETS), f32),
        'attn_norm': gain(ks[3], (L, D_MODEL)),
        'w_in': nrm(ks[4], (L, D_MODEL, IN_COLS), D_MODEL),
        'moba_q_gain': gain(ks[5], (L, dh)),
        'moba_k_gain': gain(ks[6], (L, dh)),
        'nsa_q_gain': gain(ks[7], (L, dh)),
        'nsa_k_gain': gain(ks[8], (L, 3, dh)),
        'cmp_pos_k': 0.1 * jax.random.normal(ks[9], (L, NSA_CMP_LEN, dh), f32),
        'cmp_w1_k': nrm(ks[10], (L, NSA_CMP_LEN * dh, NSA_CMP_HIDDEN), NSA_CMP_LEN * dh),
        'cmp_w2_k': nrm(ks[11], (L, NSA_CMP_HIDDEN, dh), NSA_CMP_HIDDEN),
        'cmp_pos_v': 0.1 * jax.random.normal(ks[12], (L, NSA_CMP_LEN, dh), f32),
        'cmp_w1_v': nrm(ks[13], (L, NSA_CMP_LEN * dh, NSA_CMP_HIDDEN), NSA_CMP_LEN * dh),
        'cmp_w2_v': nrm(ks[14], (L, NSA_CMP_HIDDEN, dh), NSA_CMP_HIDDEN),
        'w_br_moba': nrm(ks[15], (L, MOBA_WIDTH, D_MODEL), MOBA_WIDTH),
        'w_br_nsa': nrm(ks[16], (L, NSA_WIDTH, D_MODEL), NSA_WIDTH),
        'w_o': nrm(ks[17], (L, D_MODEL, D_MODEL), D_MODEL),
        'ffn_norm': gain(ks[18], (L, D_MODEL)),
        'w_up': nrm(ks[19], (L, D_MODEL, 2 * D_FF), D_MODEL),
        'conv_w': nrm(ks[20], (L, CONV_W, 2 * D_FF), CONV_W),
        'conv_b': 0.02 * jax.random.normal(ks[21], (L, 2 * D_FF), f32),
        'w_down': nrm(ks[22], (L, D_FF, D_MODEL), D_FF),
        'w_ple_gate': nrm(ks[23], (L, D_MODEL, D_MODEL), D_MODEL),
        'w_ple': nrm(ks[24], (L, PLE_DIM, D_MODEL), PLE_DIM),
    }

def reference(x, p, rel_bias, attn_norm, w_in, moba_q_gain, moba_k_gain, nsa_q_gain, nsa_k_gain,
              cmp_pos_k, cmp_w1_k, cmp_w2_k, cmp_pos_v, cmp_w1_v, cmp_w2_v,
              w_br_moba, w_br_nsa, w_o, ffn_norm, w_up, conv_w, conv_b, w_down, w_ple_gate, w_ple):
    B, S, _ = x.shape
    G, R = NSA_KV_GROUPS, NSA_HPG
    tab_moba = rel_bias[:MOBA_HEADS]
    tab_nsa = rel_bias[MOBA_HEADS:].reshape(G, R, REL_BUCKETS)
    cuts = np.cumsum(IN_SIZES)[:-1].tolist()
    for i in range(DEPTH):
        h = rms_norm(x, attn_norm[i])
        (mq, mk, mv, nsq, kc, vc, ksl, vsl, kwn, vwn, ngate, mgate) = jnp.split(h @ w_in[i], cuts, axis=-1)
        q_a = rms_norm(to_heads(mq, MOBA_HEADS), moba_q_gain[i])
        k_a = rms_norm(to_heads(mk, MOBA_HEADS), moba_k_gain[i])
        y_a = moba_attention(q_a, k_a, to_heads(mv, MOBA_HEADS), tab_moba)
        y_a = y_a.transpose(0, 2, 1, 3).reshape(B, S, MOBA_WIDTH)
        q_b = rms_norm(nsq.reshape(B, S, G, R, HEAD_DIM).transpose(0, 2, 3, 1, 4), nsa_q_gain[i])
        y_b = nsa_attention(q_b, to_heads(kc, G), to_heads(vc, G), to_heads(ksl, G), to_heads(vsl, G),
                            to_heads(kwn, G), to_heads(vwn, G), ngate, nsa_k_gain[i],
                            (cmp_pos_k[i], cmp_w1_k[i], cmp_w2_k[i]),
                            (cmp_pos_v[i], cmp_w1_v[i], cmp_w2_v[i]), tab_nsa)
        g_a, g_b = jnp.split(jax.nn.sigmoid(mgate), 2, axis=-1)
        x = x + (g_a * (y_a @ w_br_moba[i]) + g_b * (y_b @ w_br_nsa[i])) @ w_o[i]
        u = causal_dwconv(rms_norm(x, ffn_norm[i]) @ w_up[i], conv_w[i], conv_b[i])
        u_act, u_lin = jnp.split(u, 2, axis=-1)
        x = x + (jax.nn.gelu(u_act) * u_lin) @ w_down[i]
        x = x + jax.nn.sigmoid(x @ w_ple_gate[i]) * (p[i] @ w_ple[i])
    return x


_drawn_inputs = setup_inputs


def setup_inputs(seed=0):
    import zlib

    import numpy as np

    out = dict(_drawn_inputs(seed))
    spreads = {}
    factors = {'attn_norm': 4.821,
     'moba_q_gain': 8.0,
     'moba_k_gain': 8.0,
     'nsa_q_gain': 8.0,
     'nsa_k_gain': 8.0,
     'cmp_pos_k': 8.0,
     'cmp_pos_v': 3.751,
     'conv_b': 13.478,
     'ffn_norm': 5.563}
    for name, (base, spread) in spreads.items():
        noise = np.random.default_rng([zlib.crc32(name.encode()), seed]).standard_normal(out[name].shape)
        drawn = base * np.exp(spread * noise) if base else spread * noise
        out[name] = __import__('jax').numpy.asarray(drawn.astype(out[name].dtype))
    for name, factor in factors.items():
        out[name] = (out[name] * factor).astype(out[name].dtype)
    return out
```

```python
from contextlib import ExitStack

import numpy as np

import concourse.bass as bass
from concourse import mybir

ALU = mybir.AluOpType
ACT = mybir.ActivationFunctionType
F32 = mybir.dt.float32
F32R = mybir.dt.float32r
I32 = mybir.dt.int32
AX = mybir.AxisListType.X

P = 128
S, D, DH = 512, 1024, 64
NT, KT = S // P, D // P
DFF, PLE = 2816, 256
NF = DFF // P
HM = HN = 8
GR = 2
CMP_LEN, CMP_STRIDE = 32, 16
NCMP = (S - CMP_LEN) // CMP_STRIDE + 1
CW = 384
C_MQ, C_MK, C_NQ, C_KC, C_KS, C_NG, C_MG = 0, 512, 1536, 2048, 2304, 2816, 2840
NPAIR = 8
NGATE = 2 * D // P
EPS = 1e-6
BIG = 1e30
PITCH = 640


def bucket_edges():
    n = np.arange(S)
    nf = np.maximum(n, 1).astype(np.float32)
    large = 16 + (np.log(nf / np.float32(16)) / np.float32(np.log(128 / 16)) * np.float32(16)).astype(np.int32)
    b = np.where(n < 16, n, np.minimum(large, 31))
    return [(int(np.min(n[b == k])), int(np.max(n[b == k])) + 1) for k in range(32)]


def attention_steps():
    steps, u = [], 0
    for n in range(NPAIR):
        for e in range(2):
            for br in (["own"] if n < 4 else ["slc", "win", "cmp"]):
                tiles = range(1) if br == "cmp" else range(NT)
                for i in tiles:
                    steps.append(dict(n=n, e=e, br=br, i=i, u=u, last=(i == tiles[-1]), first=False, k=0))
                u += 1
        steps[-1]["pair_last"] = True
    k = 0
    for t, s in enumerate(steps):
        new = t == 0 or steps[t - 1]["n"] != s["n"]
        k = 0 if new else k + 1
        s["k"], s["first"] = k, new
    return steps


def layer(nc, A, out):
    STEPS = attention_steps()
    T = len(STEPS)
    first_t = [next(t for t, s in enumerate(STEPS) if s["n"] == n) for n in range(NPAIR)]
    last_t = [max(t for t, s in enumerate(STEPS) if s["n"] == n) for n in range(NPAIR)]
    NSTEP = [last_t[n] - first_t[n] + 1 for n in range(NPAIR)]
    unit_last_t = {s["u"]: t for t, s in enumerate(STEPS) if s["last"]}

    def ucols(w):
        return 2 * P + 24 if w == 0 else (P if w in (6, 8) else CW)

    def udmas(w):
        return {0: 2, 5: 3, 7: 3}.get(w, 1)

    def nvec(w):
        return 2 if w in (6, 8) else 4

    W_UNITS = 9
    USES = []
    USES += [("cst", None, k) for k in range(3)]
    USES += [("trh", None, kt) for kt in range(KT)]
    USES += [("proj", 0, tt) for tt in range(NT)]
    USES += [("vec", 0, x) for x in range(4)]
    USES += [("proj", 1, tt) for tt in range(NT)]
    USES += [("cmph", None, kv) for kv in range(2)]
    USES += [("cmpo", None, 0)]
    USES += [("cmpt", None, 0)]
    USES += [("vec", 1, x) for x in range(4)]
    for n in range(NPAIR):
        if n < 7:
            USES += [("proj", n + 2, tt) for tt in range(NT)]
        if n < 4:
            USES += [("gate", None, 2 * n)]
            USES += [("vec", n + 2, x) for x in range(4)]
            USES += [("gate", None, 2 * n + 1)]
        else:
            USES += [("gate", None, 2 * n)]
            if n < 7:
                USES += [("vec", n + 2, x) for x in range(nvec(n + 2))]
            USES += [("gate", None, 2 * n + 1)]
    use_index = {u: r for r, u in enumerate(USES)}
    vec_base = {}
    acc = 0
    for w in range(W_UNITS):
        vec_base[w] = acc
        acc += nvec(w)

    CHUNKS = []
    for mg in range(2):
        CHUNKS += [("bra", mg, kt) for kt in range(4)] + [("brb", mg, kt) for kt in range(4)]
    for mg in range(2):
        CHUNKS += [("wo", mg, kt) for kt in range(KT)]
    for ng in range(2):
        CHUNKS += [("ple", ng, kt) for kt in range(2)]
    for u in range(NF // 2):
        CHUNKS += [("up", u, kt) for kt in range(KT)]
    for mg in range(2):
        CHUNKS += [("dn", mg, kt) for kt in range(NF)]
    for ng in range(2):
        CHUNKS += [("pg", ng, kt) for kt in range(KT)]
    NC = len(CHUNKS)
    cidx = {c: i for i, c in enumerate(CHUNKS)}
    RING = 8

    x_d = A["x"].rearrange("b (t p) d -> (b t) p d", p=P)
    o_d = out.rearrange("b (t p) d -> (b t) p d", p=P)
    p_d = A["p"].rearrange("l b (t p) d -> (l b t) p d", p=P)
    win = A["w_in"].rearrange("l (k p) n -> (l k) p n", p=P)
    brm = A["w_br_moba"].rearrange("l (k p) n -> (l k) p n", p=P)
    brn = A["w_br_nsa"].rearrange("l (k p) n -> (l k) p n", p=P)
    wo_d = A["w_o"].rearrange("l (k p) n -> (l k) p n", p=P)
    up_d = A["w_up"].rearrange("l (k p) (h n) -> (l k) p h n", p=P, h=2)
    dn_d = A["w_down"].rearrange("l (k p) n -> (l k) p n", p=P)
    pg_d = A["w_ple_gate"].rearrange("l (k p) n -> (l k) p n", p=P)
    pl_d = A["w_ple"].rearrange("l (k p) n -> (l k) p n", p=P)
    w1_d = [A["cmp_w1_k"].rearrange("l (c p) h -> p (l c) h", p=P), A["cmp_w1_v"].rearrange("l (c p) h -> p (l c) h", p=P)]

    skew_d = nc.dram_tensor("skew", [16, P * PITCH], F32, kind="Internal").ap()
    gate_d = nc.dram_tensor("gates", [NGATE, P, S], F32, kind="Internal").ap()
    y_d = nc.dram_tensor("ys", [NPAIR, P, S], F32, kind="Internal").ap()
    pp_d = nc.dram_tensor("pps", [2 * NT, P, S], F32, kind="Internal").ap()

    with ExitStack() as ctx:
        def sem(n):
            return ctx.enter_context(nc.semaphore(n))

        R = ctx.enter_context(nc.sbuf_tensor("split_arena", [P, 38912], F32R))
        F = ctx.enter_context(nc.sbuf_tensor("plain_arena", [P, 14280], F32))
        PS = ctx.enter_context(nc.psum_tensor("banks", [P, 8, 512], F32))

        def r3(o, a, b):
            return R[:, o:o + a * b].rearrange("p (a b) -> p a b", a=a)

        def f3(o, a, b):
            return F[:, o:o + a * b].rearrange("p (a b) -> p a b", a=a)

        hTh, hTl = r3(0, KT, S), r3(4096, KT, S)
        Wh, Wl = r3(8192, KT, CW), r3(8192 + KT * CW, KT, CW)
        Gh, Gl = r3(14336, KT, P), r3(15360, KT, P)
        PTh = R[:, 16384:20480].rearrange("p (u j q) -> p u j q", u=2, j=NT)
        PTl = R[:, 20480:24576].rearrange("p (u j q) -> p u j q", u=2, j=NT)
        QQ = R[:, 24576:26624].rearrange("p (s e q) -> p s e q", s=2, e=2)
        Kh = R[:, 26624:28672].rearrange("p (s e q) -> p s e q", s=2, e=2)
        Kl = R[:, 28672:30720].rearrange("p (s e q) -> p s e q", s=2, e=2)
        Vh = R[:, 30720:33792].rearrange("p (s t c) -> p s t c", s=4, t=NT)
        Vl = R[:, 33792:36864].rearrange("p (s t c) -> p s t c", s=4, t=NT)
        VCh, VCl = r3(36864, 2, 192), r3(37248, 2, 192)
        KCh, KCl = r3(37632, 2, 32), r3(37696, 2, 32)
        yTh, yTl = r3(0, KT, S), r3(4096, KT, S)
        h2h, h2l = r3(0, KT, S), r3(4096, KT, S)
        W2h, W2l = r3(8192, RING, 512), r3(12288, RING, 512)
        mTh, mTl = r3(16384, KT, S), r3(20480, KT, S)
        pTh, pTl = r3(36864, 2, S), r3(37888, 2, S)
        gTh, gTl = r3(16384, NF, S), r3(16384 + NF * S, NF, S)

        raw = f3(0, KT, CW)
        graw = f3(3072, KT, P)
        strip = F[:, 4096:6144].rearrange("p (s e c) -> p s e c", s=2, e=2)
        prob = f3(6144, 4, S)
        xnat = f3(4096, NT, D)
        tcmp = f3(6144, 4, S)
        qkv = f3(8192, NT, CW)
        sq = F[:, 9728:10752].rearrange("p (t c) -> p t c", t=NT)
        qn = F[:, 9728:11776].rearrange("p (t v c) -> p t v c", t=NT, v=4)
        bp = f3(9728, 2, 1024)
        ystage = F[:, 11776:12288]
        gstage = F[:, 12288:12800]
        w1b = f3(11776, 8, P)
        rtab = F[0:16, 8192:8192 + PITCH]
        rbt = F[0:16, 8900:8932]
        rows = f3(9216, 3, P)
        ytmp = f3(8192, 7, S)
        raw2 = f3(0, RING, 512)
        x1T = f3(4096, KT, S)
        xs = F[:, 8192:9216]
        gb = f3(9216, 2, S)
        ga = f3(10240, 4, S)
        spare = F[:, 12288:12800]
        sumsq = F[:, 12288:12800]
        sqt = f3(8192, 2, S)
        rdiag = F[:, 9216:9728]
        rbc = F[:, 9728:10240]
        hst = f3(10240, 2, S)
        ppst = [F[:, o:o + S] for o in (11264, 11776, 8192, 8704)]
        ya, yl = f3(8192, 2, S), f3(10240, 2, S)
        x2n = f3(8192, NT, D)
        thb = f3(4096, 4, S)
        ppb = f3(6144, 4, S)
        ident = F[:, 12800:12928]
        ones = F[:, 12928:13056]
        cst = F[:, 13056:13296]
        gsig = F[:, 13296:13392].rearrange("p (t c) -> p t c", t=NT)
        st = F[:, 13392:13520]
        rq = F[:, 13520:13600]
        sc_c = f3(13600, NT, 32)
        hid = F[:, 13728:13852]
        kcn = F[:, 13852:13852 + 256].rearrange("p (g c) -> p g c", g=2)
        w2c = F[:, 14108:14236].rearrange("p (v c) -> p v c", v=2)
        neg8 = st[:, 100:102]
        mneg, rsum = st[:, 0:4], st[:, 4:8]
        rsum_c, mneg_c = st[:, 8:12], st[:, 12:16]
        ssx = st[:, 16:20]
        ss = st[:, 20:36]
        s_k = st[:, 36:38]

        CONVB, POSK, POSV, GQ, CONVW = 16, 60, 76, 92, 98

        x_in = [sem(f"x_in{i}") for i in range(NT)]
        const_in = sem("const_in")
        raw_in = [sem(f"raw_in{k}") for k in range(KT)]
        graw_in = sem("graw_in")
        strip_in = [sem("strip_in0"), sem("strip_in1")]
        skew_out = sem("skew_out")
        w1_in = sem("w1_in")
        y_out, g_out = sem("y_out"), sem("g_out")
        y_in = sem("y_in")
        pool_const = sem("pool_const")
        rtab_done = sem("rtab_done")
        x_sq = sem("x_sq")
        h_nat = sem("h_nat")
        bank_filled = sem("bank_filled")
        hT_hi, hT_lo = sem("hT_hi"), sem("hT_lo")
        cst_done = sem("cst_done")
        w_hi, w_lo = sem("w_hi"), sem("w_lo")
        g_hi, g_lo = sem("g_hi"), sem("g_lo")
        qkv_done = sem("qkv_done")
        sq_done = sem("sq_done")
        rstd_done = sem("rstd_done")
        norm_done = sem("norm_done")
        vec_hi, vec_lo = sem("vec_hi"), sem("vec_lo")
        v_hi, v_lo = sem("v_hi"), sem("v_lo")
        gate_tanh = sem("gate_tanh")
        gsig_tanh, gsig_done = sem("gsig_tanh"), sem("gsig_done")
        tcmp_a, tcmp_b = sem("tcmp_a"), sem("tcmp_b")
        bp_done = sem("bp_done")
        hid_done = sem("hid_done")
        cmp_sq = sem("cmp_sq")
        kcn_done = sem("kcn_done")
        vc_hi, vc_lo = sem("vc_hi"), sem("vc_lo")
        kc_hi, kc_lo = sem("kc_hi"), sem("kc_lo")
        score, biased, exped, scaled = sem("score"), sem("biased"), sem("exped"), sem("scaled")
        turned, pt_hi, pt_lo = sem("turned"), sem("pt_hi"), sem("pt_lo")
        pv_done = sem("pv_done")
        y_evac = sem("y_evac")
        chain = sem("dve_chain")
        yt_hi, yt_lo = sem("yt_hi"), sem("yt_lo")
        raw2_in = [sem(f"raw2_in{k}") for k in range(RING)]
        w2_hi, w2_lo, chunk_done = sem("w2_hi"), sem("w2_lo"), sem("chunk_done")
        xs_in, xs_tr, xT_done = sem("xs_in"), sem("xs_tr"), sem("xT_done")
        p_tr, pT_hi, pT_lo = sem("p_tr"), sem("pT_hi"), sem("pT_lo")
        ga_in, gb_in = [sem(f"ga_in{i}") for i in range(4)], [sem(f"gb_in{i}") for i in range(2)]
        brA_done, brB_done, br_sum = sem("brA_done"), sem("brB_done"), sem("br_sum")
        mT_hi, mT_lo = sem("mT_hi"), sem("mT_lo")
        x1_done, x1_sq, ssq_done = sem("x1_done"), sem("x1_sq"), sem("ssq_done")
        tok_sum, rdiag_done, bc_mm, bc_done = sem("tok_sum"), sem("rdiag_done"), sem("bc_mm"), sem("bc_done")
        h2_f, h2_hi, h2_lo = sem("h2_f"), sem("h2_hi"), sem("h2_lo")
        pp_ev, pp_out = sem("pp_ev"), [sem(f"pp_out{i}") for i in range(4)]
        ya_bias, yl_bias = sem("ya_bias"), sem("yl_bias")
        ya_conv, yl_conv = sem("ya_conv"), sem("yl_conv")
        gelu_done, glu_done, gT_hi, gT_lo = sem("gelu_done"), sem("glu_done"), sem("gT_hi"), sem("gT_lo")
        x2_done, x2_hi, x2_lo = sem("x2_done"), sem("x2_hi"), sem("x2_lo")
        x2_tr, x2n_done = sem("x2_tr"), sem("x2n_done")
        pp_in, th_done, th_mul, o_done, o_out = sem("pp_in"), sem("th_done"), sem("th_mul"), sem("o_done"), sem("o_out")

        def wait_free(eng, r):
            if r < 2:
                return
            kind, w, x = USES[r - 2]
            if kind == "trh":
                eng.wait_ge(hT_lo, x + 1)
            elif kind == "cst":
                eng.wait_ge(cst_done, x + 1)
            elif kind == "proj":
                eng.wait_ge(qkv_done, 4 * w + x + 1)
            elif kind == "vec":
                if w == 0:
                    eng.wait_ge(tcmp_b, x + 1)
                else:
                    eng.wait_ge(vec_lo, vec_base[w] + x + 1 - 4)
            elif kind == "gate":
                eng.wait_ge(gate_tanh, x + 1)
            elif kind == "cmph":
                eng.wait_ge(hid_done, x + 1)
            elif kind == "cmpo":
                eng.wait_ge(vc_lo, 1)
                eng.wait_ge(kcn_done, 1)
            elif kind == "cmpt":
                eng.wait_ge(kc_lo, 1)

        def bank(use):
            return use_index[use] % 2

        def kslot(n, e, br):
            if n < 4:
                return n % 2, e
            return (n - 4) // 2, (0 if br == "slc" else 1)

        def vslot(n, br):
            if n < 4:
                return n % 2
            return 2 * (1 - (n - 4) // 2) + (0 if br == "slc" else 1)

        def vec_dst(w, x):
            n = w - 1
            if x < 2:
                return "q", n % 2, x
            return ("k", n % 2, x - 2) if n < 4 else ("k", (n - 4) // 2, x - 2)

        def ple_bank(ng, tt):
            return tt if ng == 0 else (5, 6, 7, 0)[tt]

        def up_bank(u):
            return 4 * ((u + 1) % 2)

        def cat(br):
            return {"cmp": 0, "slc": 1, "win": 2}[br]

        block = ctx.enter_context(nc.Block())

        @block.sync
        def _(sp):
            for tt in range(NT):
                sp.dma_start(xnat[:, tt, :], x_d[tt]).then_inc(x_in[tt], 16)
            sp.dma_start(rbt, A["rel_bias"]).then_inc(const_in, 16)
            blocks = [(0, 8, A["attn_norm"]), (8, 8, A["ffn_norm"]), (CONVB, 44, A["conv_b"])]
            for r0, n, src in blocks:
                sp.dma_start(rows[r0:r0 + n, 0, :], src.rearrange("l (r c) -> (l r) c", c=P)).then_inc(const_in, 16)
            for r0, src in ((POSK, A["cmp_pos_k"]), (POSV, A["cmp_pos_v"])):
                sp.dma_start(rows[r0:r0 + 16, 0, :], src.rearrange("l (r a) c -> (l r) (a c)", a=2)).then_inc(const_in, 16)
            for a in range(2):
                for r0, n, src in ((GQ, 1, A["moba_q_gain"]), (GQ + 1, 1, A["moba_k_gain"]), (GQ + 2, 1, A["nsa_q_gain"]),
                                   (GQ + 3, 3, A["nsa_k_gain"].rearrange("l b c -> (l b) c"))):
                    sp.dma_start(rows[r0:r0 + n, 0, a * DH:(a + 1) * DH], src).then_inc(const_in, 16)
            cw = A["conv_w"].rearrange("l w (r c) -> (l w r) c", c=P)
            sp.dma_start(rows[:, 1, :], cw[0:P, :]).then_inc(const_in, 16)
            sp.dma_start(rows[0:4, 2, :], cw[P:P + 4, :]).then_inc(const_in, 16)
            for v, nm in enumerate(("cmp_w2_k", "cmp_w2_v")):
                sp.dma_start(w2c[:, v, :], A[nm].rearrange("l k n -> (l k) n")).then_inc(const_in, 16)

            def load_unit(w):
                for kt in range(KT):
                    if w > 0:
                        sp.wait_ge(w_lo, KT * (w - 1) + kt + 1)
                    if w == 0:
                        sp.dma_start(raw[:, kt, 0:256], win[kt][:, C_KC:C_KC + 256]).then_inc(raw_in[kt], 16)
                        sp.dma_start(raw[:, kt, 256:280], win[kt][:, C_NG:C_NG + 24]).then_inc(raw_in[kt], 16)
                    elif w <= 4:
                        n = w - 1
                        src = win[kt][:, 0:1536].rearrange("p (a c) -> p a c", a=3)[:, :, n * P:(n + 1) * P]
                        sp.dma_start(raw[:, kt, :].rearrange("p (a c) -> p a c", a=3), src).then_inc(raw_in[kt], 16)
                    else:
                        n = w - 5
                        sp.dma_start(raw[:, kt, 0:P], win[kt][:, C_NQ + n * P:C_NQ + (n + 1) * P]).then_inc(raw_in[kt], 16)
                        if n % 2 == 0:
                            g = n // 2
                            src = win[kt][:, C_KS:C_KS + 512].rearrange("p (b v c) -> p v b c", b=2, v=2)
                            dst = raw[:, kt, P:P + 256].rearrange("p (v b c) -> p v b c", v=2, b=2)
                            for v in range(2):
                                sp.dma_start(dst[:, v], src[:, v, :, g * DH:(g + 1) * DH]).then_inc(raw_in[kt], 16)

            def load_strips(n):
                if n >= 2:
                    sp.wait_ge(biased, last_t[n - 2] + 1)
                for e in range(2):
                    h = 2 * n + e
                    src = bass.AP(tensor=skew_d.tensor, offset=h * P * PITCH + P - 1, ap=[[PITCH - 1, P], [1, S]])
                    sp.dma_start(strip[:, n % 2, e, :], src).then_inc(strip_in[n % 2], 16)

            def load_gate_weights(j):
                if j > 0:
                    sp.wait_ge(g_lo, j)
                sp.dma_start(graw[:, :, :], A["w_in"].rearrange("l (k p) n -> p (l k) n", p=P)[
                    :, :, C_MG + j * P:C_MG + (j + 1) * P]).then_inc(graw_in, 16)

            def spill_gate(j):
                sp.wait_ge(gate_tanh, j + 1)
                sp.dma_start(gate_d[j], gstage).then_inc(g_out, 16)

            def spill_y(n):
                sp.wait_ge(y_evac, n + 1)
                sp.dma_start(y_d[n], ystage).then_inc(y_out, 16)

            load_unit(0)
            sp.wait_ge(rtab_done, 1)
            d3 = bass.AP(tensor=skew_d.tensor, offset=0, ap=[[P * PITCH, 16], [PITCH, P], [1, PITCH]])
            s3 = bass.AP(tensor=rtab.tensor, offset=rtab.offset, ap=[rtab.ap[0], [0, P], [1, PITCH]])
            sp.dma_start(d3, s3).then_inc(skew_out, 16)
            sp.dma_start(graw[:, :, :], w1_d[0][:, 0:8, :]).then_inc(w1_in, 16)
            sp.dma_start(w1b[:, :, :], w1_d[0][:, 8:16, :]).then_inc(w1_in, 16)
            load_unit(1)
            sp.wait_ge(bank_filled, use_index[("cmph", None, 0)] + 1)
            sp.dma_start(graw[:, :, :], w1_d[1][:, 0:8, :]).then_inc(w1_in, 16)
            sp.dma_start(w1b[:, :, :], w1_d[1][:, 8:16, :]).then_inc(w1_in, 16)
            sp.wait_ge(skew_out, 16)
            sp.wait_ge(bank_filled, use_index[("cmph", None, 0)] + 1)
            load_strips(0)
            load_unit(2)
            sp.wait_ge(bank_filled, use_index[("cmph", None, 1)] + 1)
            load_gate_weights(0)
            for n in range(NPAIR):
                if n + 1 < NPAIR:
                    load_strips(n + 1)
                if n + 3 < W_UNITS:
                    load_unit(n + 3)
                if n > 0:
                    spill_gate(2 * n - 1)
                load_gate_weights(2 * n + 1)
                if n > 0:
                    spill_y(n - 1)
                spill_gate(2 * n)
                if 2 * n + 2 < NGATE:
                    load_gate_weights(2 * n + 2)
            sp.wait_ge(y_out, 16 * 7)
            for n in range(7):
                sp.dma_start(ytmp[:, n, :], y_d[n]).then_inc(y_in, 16)

            def load_chunk(c):
                kind, a, kt = CHUNKS[c]
                if c >= RING:
                    sp.wait_ge(w2_lo, c - RING + 1)
                dst = raw2[:, c % RING, :]
                n0, n1 = a * 512, (a + 1) * 512
                src = {"bra": lambda: brm[kt][:, n0:n1], "brb": lambda: brn[kt][:, n0:n1], "wo": lambda: wo_d[kt][:, n0:n1],
                       "ple": lambda: pl_d[kt][:, n0:n1], "dn": lambda: dn_d[kt][:, n0:n1], "pg": lambda: pg_d[kt][:, n0:n1],
                       "up": lambda: up_d[kt][:, :, a * 256:(a + 1) * 256]}[kind]()
                if kind == "up":
                    dst = dst.rearrange("p (h c) -> p h c", h=2)
                sp.dma_start(dst, src).then_inc(raw2_in[c % RING], 16)

            def load_gates_a(mg):
                for m in range(4):
                    if mg:
                        sp.wait_ge(mT_lo, m + 1)
                    sp.dma_start(ga[:, m, :], gate_d[4 * mg + m]).then_inc(ga_in[m], 16)

            def load_gate_b(k):
                if k >= 2:
                    sp.wait_ge(br_sum, k - 1)
                sp.dma_start(gb[:, k % 2, :], gate_d[8 + k]).then_inc(gb_in[k % 2], 16)

            def load_x(tt):
                if tt:
                    sp.wait_ge(xs_tr, tt)
                sp.dma_start(xs, x_d[tt]).then_inc(xs_in, 16)

            sp.wait_ge(w_lo, KT * W_UNITS)
            for c in range(6):
                load_chunk(c)
            sp.wait_ge(g_lo, NGATE)
            for c in range(6, RING):
                load_chunk(c)
            spill_gate(NGATE - 1)
            sp.wait_ge(g_out, 16 * NGATE)
            sp.wait_ge(yt_lo, 7)
            load_x(0)
            for k in range(2):
                load_gate_b(k)
            load_gates_a(0)
            load_x(1)
            for c in range(RING, NC):
                load_chunk(c)
                if c == 22:
                    load_gate_b(2)
                    load_gate_b(3)
                    load_gates_a(1)
                    load_gate_b(4)
                    load_gate_b(5)
                if c == 23:
                    load_x(2)
                if c == 30:
                    load_gate_b(6)
                    load_gate_b(7)
                if c == 31:
                    load_x(3)
                if c == 33:
                    sp.wait_ge(xs_tr, 4)
                    for tt in range(NT):
                        sp.dma_start(xs[:, tt * PLE:(tt + 1) * PLE], p_d[tt]).then_inc(xs_in, 16)
                if c in (47, 49):
                    for k in (range(0, 2) if c == 47 else range(2, 8)):
                        sp.wait_ge(pp_ev, k + 1)
                        sp.dma_start(pp_d[k], ppst[k % 4]).then_inc(pp_out[k % 4], 16)
            for k in range(4):
                sp.wait_ge(pp_out[k], 32)
            sp.wait_ge(x2_tr, 8)
            sp.wait_ge(x2_lo, 8)
            for k in range(4):
                sp.dma_start(ppb[:, k % 4, :], pp_d[k]).then_inc(pp_in, 16)
            for k in range(8):
                sp.wait_ge(o_done, k + 1)
                ng, tt = k // 4, k % 4
                sp.dma_start(o_d[tt][:, ng * 512:(ng + 1) * 512], x2n[:, tt, ng * 512:(ng + 1) * 512]).then_inc(o_out, 16)
                if k < 4:
                    sp.dma_start(ppb[:, k % 4, :], pp_d[k + 4]).then_inc(pp_in, 16)
            sp.wait_ge(o_out, 16 * 8)

        @block.gpsimd
        def _(pool):
            pool.memset(ident, 0.0).then_inc(pool_const, 1)
            pool.memset(ones, 1.0).then_inc(pool_const, 1)
            pool.memset(neg8[:, 0:1], -(DH ** -0.5)).then_inc(pool_const, 1)
            pool.wait_ge(pool_const, 1)
            pool.affine_select(out=ident, in_=ident, compare_op=ALU.not_equal, fill=1.0, base=0,
                               pattern=[[-1, P]], channel_multiplier=1).then_inc(pool_const, 1)
            for t_ in (Vh, Vl):
                pool.memset(t_[:, :, :, DH:2 * DH].bitcast(F32), 0.0).then_inc(pool_const, 1)
            for t_ in (VCh, VCl, KCh, KCl):
                pool.memset(t_.bitcast(F32), 0.0).then_inc(pool_const, 1)
            pool.memset(rtab, BIG).then_inc(pool_const, 1)
            pool.wait_ge(const_in, 16 * 18)
            pool.wait_ge(pool_const, 11)
            for b, (lo, hi) in enumerate(bucket_edges()):
                ins = pool.tensor_scalar(rtab[:, S - hi:S - lo], rbt[:, b:b + 1].broadcast_to([16, hi - lo]), -1.0, None, ALU.mult)
            ins.then_inc(rtab_done, 1)

            def split_unit(w, kts):
                c = ucols(w)
                for kt in kts:
                    pool.wait_ge(w_hi, KT * w + kt + 1)
                    pool.tensor_tensor(Wl[:, kt, 0:c], raw[:, kt, 0:c], Wh[:, kt, 0:c].bitcast(F32), ALU.subtract).then_inc(w_lo, 1)

            def split_gate(j):
                pool.wait_ge(g_hi, j + 1)
                pool.tensor_tensor(Gl, graw, Gh.bitcast(F32), ALU.subtract).then_inc(g_lo, 1)

            def v_low(w):
                n = w - 1
                pool.wait_ge(v_hi, w if n <= 4 else 6)
                if n < 4:
                    o = Vl[:, n % 2].rearrange("p t (a c) -> p t a c", a=3)[:, :, 0:3:2, :]
                    hi = Vh[:, n % 2].rearrange("p t (a c) -> p t a c", a=3)[:, :, 0:3:2, :]
                    i = qkv[:, :, 256:384].rearrange("p t (a c) -> p t a c", a=2)
                    pool.tensor_tensor(o, i, hi.bitcast(F32), ALU.subtract).then_inc(v_lo, 1)
                else:
                    for b in range(2):
                        s = vslot(n, ("slc", "win")[b])
                        for a in (0, 2):
                            ins = pool.tensor_tensor(Vl[:, s, :, a * DH:(a + 1) * DH], qkv[:, :, 256 + b * DH:256 + (b + 1) * DH],
                                                     Vh[:, s, :, a * DH:(a + 1) * DH].bitcast(F32), ALU.subtract)
                    ins.then_inc(v_lo, 1)

            def normalise(w):
                k = nvec(w)
                pool.wait_ge(rstd_done, w)
                for tt in range(NT):
                    i = qkv[:, tt, 0:k * DH].rearrange("p (v c) -> p v c", v=k)
                    for a in range(2):
                        ins = pool.tensor_tensor(qn[:, tt, 0:k, a * DH:(a + 1) * DH], i,
                                                 rq[:, 4 * tt:4 * tt + k].unsqueeze(2).broadcast_to([P, k, DH]), ALU.mult)
                ins.then_inc(norm_done, 1)

            split_unit(0, range(KT))
            pool.wait_ge(qkv_done, NT)
            pool.wait_ge(cst_done, 3)
            for tt in range(NT):
                for a in range(2):
                    ins = pool.tensor_copy(qn[:, tt, :, a * DH:(a + 1) * DH], qkv[:, tt, 0:256].rearrange("p (v c) -> p v c", v=4))
            ins.then_inc(norm_done, 1)
            split_unit(1, range(KT))
            for kv in range(2):
                for g in range(2):
                    pool.wait_ge(tcmp_b, 2 * kv + g + 1)
                pool.wait_ge(tcmp_a, 2 * kv + 2)
                pool.wait_ge(bank_filled, use_index[("vec", 0, 3)] + 1)
                for half in range(2):
                    o = bp[:, kv, 0:992].rearrange("p (g l n) -> p g l n", g=2, l=16)
                    pos = cst[:, (POSV if kv else POSK) + 8 * half:(POSV if kv else POSK) + 8 * half + 8]
                    for g in range(2):
                        tk = tcmp[:, 2 * kv + g, 16 * half:16 * half + 496].rearrange("p (n l) -> p l n", l=16)[:, 0:16:2, :]
                        ins = pool.tensor_tensor(o[:, g, 8 * half:8 * half + 8, :], tk,
                                                 pos.unsqueeze(2).broadcast_to([P, 8, NCMP]), ALU.add)
                ins.then_inc(bp_done, 1)
            normalise(1)
            v_low(1)
            split_unit(2, range(KT))
            split_gate(0)
            for n in range(NPAIR):
                w = n + 2
                if n < 7:
                    normalise(w)
                    if w not in (6, 8):
                        v_low(w)
                if n + 3 < W_UNITS:
                    split_unit(n + 3, range(0, 4))
                split_gate(2 * n + 1)
                if n + 3 < W_UNITS:
                    split_unit(n + 3, range(4, 8))
                if 2 * n + 2 < NGATE:
                    split_gate(2 * n + 2)

            def y_low(n):
                pool.wait_ge(yt_hi, n + 1)
                pool.tensor_tensor(yTl[:, n, :], ytmp[:, n, :], yTh[:, n, :].bitcast(F32), ALU.subtract).then_inc(yt_lo, 1)

            def split_chunk(c):
                pool.wait_ge(w2_hi, c + 1)
                pool.tensor_tensor(W2l[:, c % RING, :], raw2[:, c % RING, :], W2h[:, c % RING, :].bitcast(F32),
                                   ALU.subtract).then_inc(w2_lo, 1)

            for n in range(7):
                y_low(n)
            for c in range(NC):
                split_chunk(c)
                for mg in range(2):
                    for m in range(4):
                        if c == cidx[("wo", mg, KT - 1)] + 7:
                            kt = 4 * mg + m
                            pool.wait_ge(x1_sq, kt + 1)
                            if kt == 0:
                                pool.tensor_copy(sumsq, sqt[:, 0, :]).then_inc(ssq_done, 1)
                            else:
                                pool.wait_ge(ssq_done, kt)
                                pool.tensor_tensor(sumsq, sumsq, sqt[:, kt % 2, :], ALU.add).then_inc(ssq_done, 1)
                if c == cidx[("ple", 1, 0)] + 7:
                    for kt in range(KT):
                        pool.wait_ge(h2_hi, kt + 1)
                        pool.tensor_tensor(h2l[:, kt, :], hst[:, kt % 2, :], h2h[:, kt, :].bitcast(F32), ALU.subtract).then_inc(h2_lo, 1)
                for mg in range(2):
                    if c == cidx[("dn", mg, NF - 1)] + 7:
                        for m in range(4):
                            kt = 4 * mg + m
                            pool.wait_ge(x2_hi, kt + 1)
                            pool.tensor_tensor(h2l[:, kt, :], x1T[:, kt, :], h2h[:, kt, :].bitcast(F32), ALU.subtract).then_inc(x2_lo, 1)

        @block.scalar
        def _(act):
            for tt in range(NT):
                act.wait_ge(x_in[tt], 16)
                nc.scalar.activation(R[:, 8192 + tt * D:8192 + (tt + 1) * D], xnat[:, tt, :], ACT.Square, accum_out=ssx[:, tt:tt + 1]).then_inc(x_sq, 1)

            def split_unit(w, kts):
                c = ucols(w)
                for kt in kts:
                    act.wait_ge(raw_in[kt], 16 * sum(udmas(v) for v in range(w + 1)))
                    if w > 0:
                        act.wait_ge(bank_filled, use_index[("proj", w - 1, NT - 1)] + 1)
                    else:
                        act.wait_ge(x_sq, NT)
                    nc.scalar.activation(Wh[:, kt, 0:c], raw[:, kt, 0:c], ACT.Copy).then_inc(w_hi, 1)

            def split_gate(j):
                act.wait_ge(graw_in, 16 * (j + 1))
                if j > 0:
                    act.wait_ge(bank_filled, use_index[("gate", None, j - 1)] + 1)
                nc.scalar.activation(Gh, graw, ACT.Copy).then_inc(g_hi, 1)

            def take_proj(w, tt):
                r = use_index[("proj", w, tt)]
                act.wait_ge(bank_filled, r + 1)
                if w == 1:
                    act.wait_ge(norm_done, 1)
                    act.wait_ge(gsig_tanh, 1)
                if w > 1 and tt == 0:
                    act.wait_ge(norm_done, w)
                    if w - 1 not in (6, 8):
                        act.wait_ge(v_lo, min(w - 1, 5) if w - 1 < 7 else 6)
                nc.scalar.activation(qkv[:, tt, 0:ucols(w)], PS[:, r % 2, 0:ucols(w)], ACT.Copy).then_inc(qkv_done, 1)

            def squares(w):
                k = nvec(w)
                act.wait_ge(qkv_done, 4 * w + 4)
                if w == 1:
                    act.wait_ge(bank_filled, use_index[("cmph", None, 1)] + 1)
                else:
                    act.wait_ge(bank_filled, use_index[("vec", w - 1, nvec(w - 1) - 1)] + 1)
                nc.scalar.activation(sq[:, :, 0:k * DH], qkv[:, :, 0:k * DH], ACT.Square).then_inc(sq_done, 1)

            def v_high(w):
                n = w - 1
                if n < 4:
                    if n >= 2:
                        act.wait_ge(pv_done, 2 * n - 2)
                    o = Vh[:, n % 2].rearrange("p t (a c) -> p t a c", a=3)[:, :, 0:3:2, :]
                    nc.scalar.activation(o, qkv[:, :, 256:384].rearrange("p t (a c) -> p t a c", a=2), ACT.Copy).then_inc(v_hi, 1)
                else:
                    if n == 6:
                        act.wait_ge(pv_done, 8)
                    for b in range(2):
                        s = vslot(n, ("slc", "win")[b])
                        for a in (0, 2):
                            ins = nc.scalar.activation(Vh[:, s, :, a * DH:(a + 1) * DH], qkv[:, :, 256 + b * DH:256 + (b + 1) * DH], ACT.Copy)
                    ins.then_inc(v_hi, 1)

            def vec_high(w, x):
                n = w - 1
                r = use_index[("vec", w, x)]
                act.wait_ge(bank_filled, r + 1)
                kind, s, e = vec_dst(w, x)
                if kind == "q":
                    if n >= 2:
                        act.wait_ge(score, last_t[n - 2] + 1)
                    g = cst[:, GQ + (0 if n < 4 else 2):GQ + (0 if n < 4 else 2) + 1]
                    dst = QQ[:, s, e, :]
                else:
                    if n >= 2:
                        act.wait_ge(score, last_t[min(n - 2, 3)] + 1)
                    g = cst[:, GQ + 1:GQ + 2] if n < 4 else cst[:, GQ + 4 + e:GQ + 5 + e]
                    dst = Kh[:, s, e, :]
                nc.scalar.activation(dst, PS[:, r % 2, :], ACT.Copy, scale=g).then_inc(vec_hi, 1)

            def exp(t):
                s = STEPS[t]
                act.wait_ge(biased, t + 1)
                if s["br"] == "cmp":
                    nc.scalar.activation(prob[:, t % 4, 0:P], sc_c.rearrange("p a b -> p (a b)"), ACT.Exp, scale=-1.0).then_inc(exped, 1)
                else:
                    nk = P * (s["i"] + 1)
                    nc.scalar.activation(prob[:, t % 4, 0:nk], prob[:, t % 4, 0:nk], ACT.Exp, bias=mneg[:, t % 4:t % 4 + 1],
                                         scale=-1.0, accum_out=rsum[:, t % 4:t % 4 + 1]).then_inc(exped, 1)

            def pt_high(t):
                s = STEPS[t]
                act.wait_ge(turned, t + 1)
                if s["u"] >= 2:
                    act.wait_ge(pv_done, s["u"] - 1)
                if s["br"] == "cmp":
                    nc.scalar.activation(PTh[0:32, s["u"] % 2, 0, :], PS[0:32, 4 + t % 2, :], ACT.Copy).then_inc(pt_hi, 1)
                else:
                    i = s["i"]
                    nc.scalar.activation(PTh[:, s["u"] % 2, 0:i + 1, P * i:P * (i + 1)],
                                         PS[:, 4 + t % 2, 0:P * (i + 1)].rearrange("p (j q) -> p j q", j=i + 1), ACT.Copy).then_inc(pt_hi, 1)

            def take_gate(j):
                r = use_index[("gate", None, j)]
                act.wait_ge(bank_filled, r + 1)
                if j > 0:
                    act.wait_ge(g_out, 16 * j)
                else:
                    act.wait_ge(bank_filled, use_index[("cmph", None, 1)] + 1)
                nc.scalar.activation(gstage, PS[:, r % 2, :], ACT.Tanh, scale=0.5).then_inc(gate_tanh, 1)

            def split_chunk(c):
                act.wait_ge(raw2_in[c % RING], 16 * (c // RING + 1))
                if c >= RING:
                    act.wait_ge(chunk_done, c - RING + 1)
                if c == 0:
                    act.wait_ge(bank_filled, len(USES))
                nc.scalar.activation(W2h[:, c % RING, :], raw2[:, c % RING, :], ACT.Copy).then_inc(w2_hi, 1)

            split_unit(0, range(KT))
            for k, nr in enumerate((98, P, 4)):
                r = use_index[("cst", None, k)]
                act.wait_ge(bank_filled, r + 1)
                o0 = (0, CONVW, CONVW + P)[k]
                nc.scalar.activation(cst[:, o0:o0 + nr], PS[:, r % 2, 0:nr], ACT.Copy).then_inc(cst_done, 1)
            act.wait_ge(cst_done, 3)
            for kt in range(KT):
                r = use_index[("trh", None, kt)]
                act.wait_ge(bank_filled, r + 1)
                nc.scalar.activation(hTh[:, kt, :], PS[:, r % 2, :], ACT.Copy, scale=cst[:, kt:kt + 1]).then_inc(hT_hi, 1)
            for tt in range(NT):
                if tt == 0:
                    act.wait_ge(rtab_done, 1)
                    act.wait_ge(skew_out, 16)
                    act.wait_ge(cst_done, 3)
                take_proj(0, tt)
            act.wait_ge(qkv_done, 4)
            nc.scalar.activation(gsig, qkv[:, :, 256:280], ACT.Tanh, scale=0.5).then_inc(gsig_tanh, 1)
            for x in range(4):
                r = use_index[("vec", 0, x)]
                act.wait_ge(bank_filled, r + 1)
                nc.scalar.activation(tcmp[0:DH, x, :], PS[0:DH, r % 2, :], ACT.Copy).then_inc(tcmp_a, 1)
            split_unit(1, range(KT))
            for tt in range(NT):
                take_proj(1, tt)
            for kv in range(2):
                r = use_index[("cmph", None, kv)]
                act.wait_ge(bank_filled, r + 1)
                nc.scalar.activation(hid[:, kv * 62:kv * 62 + 62], PS[:, r % 2, 0:62], ACT.Gelu_apprx_tanh).then_inc(hid_done, 1)
            r = use_index[("cmpo", None, 0)]
            act.wait_ge(bank_filled, r + 1)
            vps = PS[0:NCMP, r % 2, P:2 * P].rearrange("p (g c) -> p g c", g=2)
            act.wait_ge(pool_const, 11)
            act.wait_ge(kcn_done, 1)
            for g in range(2):
                for a in (0, 2):
                    ins = nc.scalar.activation(VCh[0:NCMP, g, a * DH:(a + 1) * DH], vps[:, g, :], ACT.Copy)
            ins.then_inc(vc_hi, 1)
            r = use_index[("cmpt", None, 0)]
            act.wait_ge(bank_filled, r + 1)
            for g in range(2):
                ins = nc.scalar.activation(KCh[:, g, 0:NCMP], PS[:, r % 2, 32 * g:32 * g + NCMP], ACT.Copy, scale=cst[:, GQ + 3:GQ + 4])
            ins.then_inc(kc_hi, 1)
            squares(1)
            v_high(1)
            split_unit(2, range(KT))
            for x in range(4):
                vec_high(1, x)
            split_gate(0)

            for t in range(T + 2):
                if t < T:
                    exp(t)
                    s = STEPS[t]
                    n, k, w = s["n"], s["k"], s["n"] + 2
                    moba = n < 4
                    if k == 0 and n > 0 and n <= 4:
                        take_gate(2 * n - 1)
                    if k == 1 and n > 0 and n <= 4:
                        split_gate(2 * n)
                    if n < 7 and 1 <= k <= 4:
                        take_proj(w, k - 1)
                    if n < 7 and k == 4:
                        squares(w)
                        if w not in (6, 8):
                            v_high(w)
                    if moba:
                        if n + 3 < W_UNITS and 4 <= k < 8:
                            split_unit(n + 3, (2 * (k - 4), 2 * (k - 4) + 1))
                        if k == 5:
                            take_gate(2 * n)
                            split_gate(2 * n + 1)
                            vec_high(w, 0)
                            vec_high(w, 1)
                        if k == 6:
                            vec_high(w, 2)
                            vec_high(w, 3)
                    else:
                        if k == 6:
                            take_gate(2 * n)
                            split_gate(2 * n + 1)
                        if n + 3 < W_UNITS and 5 <= k < 13:
                            split_unit(n + 3, (k - 5,))
                        if n < 7 and k == 8:
                            vec_high(w, 0)
                            vec_high(w, 1)
                        if n < 7 and k == 9 and nvec(w) == 4:
                            vec_high(w, 2)
                            vec_high(w, 3)
                        if k == 13:
                            take_gate(2 * n + 1)
                            if 2 * n + 2 < NGATE:
                                split_gate(2 * n + 2)
                        if n == 7 and k == 14:
                            act.wait_ge(bank_filled, len(USES))
                            act.wait_ge(y_in, 16 * 7)
                            for m in range(7):
                                nc.scalar.activation(yTh[:, m, :], ytmp[:, m, :], ACT.Copy).then_inc(yt_hi, 1)
                        if n == 7 and k in (15, 16):
                            for c in range(4 * (k - 15), 4 * (k - 15) + 4):
                                split_chunk(c)
                if 1 <= t <= T:
                    pt_high(t - 1)

            act.wait_ge(pv_done, STEPS[-1]["u"] + 1)
            nc.scalar.activation(yTh[:, 7, :], PS[:, 6, :], ACT.Copy).then_inc(yt_hi, 1)

            def take_x(tt):
                for half in range(2):
                    b = (4 + 2 * (tt % 2)) + half
                    act.wait_ge(xs_tr, tt + 1)
                    nc.scalar.activation(x1T[:, 4 * half:4 * half + 4, P * tt:P * (tt + 1)],
                                         PS[:, b, :].rearrange("p (k q) -> p k q", k=4), ACT.Copy).then_inc(xT_done, 1)

            def conv_bias(f):
                u, q = f // 2, f % 2
                act.wait_ge(chunk_done, cidx[("up", u, KT - 1)] + 1)
                for half, (dst, sm) in enumerate(((ya, ya_bias), (yl, yl_bias))):
                    b = up_bank(u) + 2 * half + q
                    if f == 0 and half == 0:
                        act.wait_ge(h2_lo, KT)
                        act.wait_ge(h2_f, KT)
                        for k in range(4):
                            act.wait_ge(pp_out[k], 32)
                    if f >= 2:
                        act.wait_ge(gT_lo, f - 1)
                    col = half * NF + f
                    nc.scalar.activation(dst[:, f % 2, :], PS[:, b, :], ACT.Identity, scale=cst[:, CONVW + 88 + col:CONVW + 89 + col],
                                         bias=cst[:, CONVB + col:CONVB + col + 1]).then_inc(sm, 1)

            def gelu(f):
                act.wait_ge(ya_conv, f + 1)
                nc.scalar.activation(ya[:, f % 2, :], ya[:, f % 2, :], ACT.Gelu_apprx_tanh).then_inc(gelu_done, 1)

            def g_high(f):
                act.wait_ge(glu_done, f + 1)
                if f == 0:
                    act.wait_ge(chunk_done, cidx[("ple", 1, 1)] + 1)
                nc.scalar.activation(gTh[:, f, :], ya[:, f % 2, :], ACT.Copy).then_inc(gT_hi, 1)

            def take_pp(k):
                act.wait_ge(chunk_done, cidx[("ple", k // 4, 1)] + 1)
                if k == 2:
                    act.wait_ge(ssq_done, KT)
                if k >= 4:
                    act.wait_ge(pp_out[k % 4], 16)
                nc.scalar.activation(ppst[k % 4], PS[:, ple_bank(k // 4, k % 4), :], ACT.Copy, scale=0.5).then_inc(pp_ev, 1)

            take_x(0)
            take_x(1)
            for c in range(RING, NC + 10):
                e = c - RING
                kind, a, kt = CHUNKS[e] if e < NC else (None, 0, 0)
                if kind == "brb" and kt == 3:
                    for m in range(4):
                        i = 4 * a + m
                        act.wait_ge(br_sum, i + 1)
                        nc.scalar.activation(mTh[:, i, :], ga[:, m, :], ACT.Copy, scale=0.5).then_inc(mT_hi, 1)
                if kind == "wo" and a == 0 and kt == 5:
                    take_x(2)
                    take_x(3)
                    for k in range(2):
                        act.wait_ge(p_tr, k + 1)
                        nc.scalar.activation(pTh[:, k, :], PS[:, 4 + k, :], ACT.Copy).then_inc(pT_hi, 1)
                if kind == "wo" and kt == KT - 1:
                    for m in range(4):
                        i = 4 * a + m
                        act.wait_ge(x1_done, i + 1)
                        if i >= 2:
                            act.wait_ge(ssq_done, i - 1)
                        nc.scalar.activation(sqt[:, i % 2, :], x1T[:, i, :], ACT.Square).then_inc(x1_sq, 1)
                if kind == "ple" and (a, kt) == (0, 1):
                    take_pp(0)
                    take_pp(1)
                if kind == "ple" and (a, kt) == (1, 0):
                    act.wait_ge(bc_mm, 1)
                    nc.scalar.activation(rbc, PS[:, 4, :], ACT.Copy).then_inc(bc_done, 1)
                    for i in range(KT):
                        act.wait_ge(h2_f, i + 1)
                        nc.scalar.activation(h2h[:, i, :], hst[:, i % 2, :], ACT.Copy).then_inc(h2_hi, 1)
                if kind == "ple" and (a, kt) == (1, 1):
                    for k in range(2, 8):
                        take_pp(k)
                if kind == "up" and kt == KT - 1:
                    conv_bias(2 * a)
                    conv_bias(2 * a + 1)
                if (kind == "up" and kt == 0 and a > 0) or (kind == "dn" and a == 0 and kt == 0):
                    u = a - 1 if kind == "up" else NF // 2 - 1
                    gelu(2 * u)
                    gelu(2 * u + 1)
                if (kind == "up" and kt == 1 and a > 0) or (kind == "dn" and a == 0 and kt == 1):
                    u = a - 1 if kind == "up" else NF // 2 - 1
                    g_high(2 * u)
                    g_high(2 * u + 1)
                if kind == "dn" and kt == NF - 1:
                    for m in range(4):
                        i = 4 * a + m
                        act.wait_ge(x2_done, i + 1)
                        nc.scalar.activation(h2h[:, i, :], x1T[:, i, :], ACT.Copy).then_inc(x2_hi, 1)
                if kind == "pg" and kt == KT - 1:
                    for tt in range(NT):
                        k = 4 * a + tt
                        act.wait_ge(chunk_done, e + 1)
                        if k == 0:
                            act.wait_ge(x2_tr, 8)
                            act.wait_ge(x2_lo, 8)
                        if k >= 4:
                            act.wait_ge(o_done, k - 3)
                        nc.scalar.activation(thb[:, k % 4, :], PS[:, 4 * a + tt, :], ACT.Tanh, scale=0.5).then_inc(th_done, 1)
                if c < NC:
                    split_chunk(c)

        @block.vector
        def _(dve):
            nch = [0]

            def link(ins):
                nch[0] += 1
                ins.then_inc(chain, 1)
                dve.wait_ge(chain, nch[0])

            def rsqrt(dst, src, inv_n, wdt, parts=P, done=None):
                v = st[0:parts, 40:40 + wdt]
                y = dst
                a = st[0:parts, 60:60 + wdt]
                link(nc.vector.tensor_scalar(v, src, inv_n, EPS, ALU.mult, ALU.add))
                link(nc.vector.tensor_scalar(a.bitcast(I32), v.bitcast(I32), 1, None, ALU.logical_shift_right))
                link(nc.vector.tensor_scalar(y.bitcast(I32), a.bitcast(I32), -1.0, float(0x5F3759DF), ALU.mult, ALU.add))
                for it in range(3):
                    link(nc.vector.tensor_tensor(a, y, y, ALU.mult))
                    link(nc.vector.scalar_tensor_tensor(out=a, in0=a, scalar=-0.5, in1=v, op0=ALU.mult, op1=ALU.mult))
                    ins = nc.vector.scalar_tensor_tensor(out=y, in0=a, scalar=1.5, in1=y, op0=ALU.add, op1=ALU.mult)
                    if it == 2 and done is not None:
                        ins.then_inc(done, 1)
                    else:
                        link(ins)

            dve.wait_ge(x_sq, NT)
            rsqrt(st[:, 80:84], ssx, 1.0 / D, 4)
            for tt in range(NT):
                nc.vector.tensor_scalar(xnat[:, tt, :], xnat[:, tt, :], st[:, 80 + tt:81 + tt], None, ALU.mult).then_inc(h_nat, 1)
            dve.wait_ge(cst_done, 3)
            dve.wait_ge(pool_const, 4)
            for c in (GQ, GQ + 2):
                link(nc.vector.tensor_scalar(cst[:, c:c + 1], cst[:, c:c + 1], -(DH ** -0.5), None, ALU.mult))
            for kt in range(KT):
                r = use_index[("trh", None, kt)]
                dve.wait_ge(hT_hi, kt + 1)
                nc.vector.scalar_tensor_tensor(out=hTl[:, kt, :], in0=PS[:, r % 2, :], scalar=cst[:, kt:kt + 1],
                                               in1=hTh[:, kt, :].bitcast(F32), op0=ALU.mult, op1=ALU.subtract).then_inc(hT_lo, 1)
            dve.wait_ge(gsig_tanh, 1)
            nc.vector.tensor_scalar(gsig, gsig, 0.5, 0.5, ALU.mult, ALU.add).then_inc(gsig_done, 1)
            for x in range(4):
                r = use_index[("vec", 0, x)]
                dve.wait_ge(tcmp_a, x + 1)
                nc.vector.tensor_copy(tcmp[DH:P, x, 0:S - 1], PS[DH:P, r % 2, 1:S]).then_inc(tcmp_b, 1)
            r = use_index[("cmpo", None, 0)]
            dve.wait_ge(bank_filled, r + 1)
            kps = PS[0:NCMP, r % 2, 0:P]
            vps = PS[0:NCMP, r % 2, P:2 * P].rearrange("p (g c) -> p g c", g=2)
            link(nc.vector.tensor_copy(F[0:NCMP, 13600:13728], kps))
            ksb = F[0:NCMP, 13600:13728].rearrange("p (g c) -> p g c", g=2)
            link(nc.vector.tensor_tensor(kcn[0:NCMP, :, 0:DH], ksb, ksb, ALU.mult))
            link(nc.vector.reduce_sum(s_k[0:NCMP, :], kcn[0:NCMP, :, 0:DH], AX))
            rsqrt(st[0:NCMP, 84:86], s_k[0:NCMP, :], 1.0 / DH, 2, NCMP)
            for a in range(2):
                ins = nc.vector.tensor_tensor(kcn[0:NCMP, :, a * DH:(a + 1) * DH], ksb,
                                              st[0:NCMP, 84:86].unsqueeze(2).broadcast_to([NCMP, 2, DH]), ALU.mult)
                if a == 0:
                    link(ins)
            ins.then_inc(kcn_done, 1)
            dve.wait_ge(vc_hi, 1)
            for g in range(2):
                for a in (0, 2):
                    ins = nc.vector.tensor_tensor(VCl[0:NCMP, g, a * DH:(a + 1) * DH], vps[:, g, :],
                                                  VCh[0:NCMP, g, a * DH:(a + 1) * DH].bitcast(F32), ALU.subtract)
            ins.then_inc(vc_lo, 1)
            r = use_index[("cmpt", None, 0)]
            dve.wait_ge(kc_hi, 1)
            for g in range(2):
                ins = nc.vector.scalar_tensor_tensor(out=KCl[:, g, 0:NCMP], in0=PS[:, r % 2, 32 * g:32 * g + NCMP], scalar=cst[:, GQ + 3:GQ + 4],
                                                     in1=KCh[:, g, 0:NCMP].bitcast(F32), op0=ALU.mult, op1=ALU.subtract)
            ins.then_inc(kc_lo, 1)

            def rstd(w):
                k = nvec(w)
                dve.wait_ge(sq_done, w)
                if w > 1:
                    dve.wait_ge(norm_done, w)
                link(nc.vector.reduce_sum(ss[:, 0:4 * k].rearrange("p (t v) -> p t v", t=NT), sq[:, :, 0:k * DH].rearrange("p t (v c) -> p t v c", v=k), AX))
                if k == 4:
                    rsqrt(rq[:, 0:16], ss[:, 0:16], 1.0 / DH, 16, done=rstd_done)
                else:
                    rsqrt(rq[:, 20:28], ss[:, 0:8], 1.0 / DH, 8)
                    nc.vector.tensor_copy(rq[:, 0:16].rearrange("p (t v) -> p t v", t=NT)[:, :, 0:2],
                                          rq[:, 20:28].rearrange("p (t v) -> p t v", t=NT)).then_inc(rstd_done, 1)

            def vec_low(w, x):
                n = w - 1
                r = use_index[("vec", w, x)]
                dve.wait_ge(vec_hi, vec_base[w] + x + 1 - 4)
                kind, s, e = vec_dst(w, x)
                if kind == "q":
                    c = GQ + (0 if n < 4 else 2)
                    nc.vector.scalar_tensor_tensor(out=QQ[DH:P, s, e, :], in0=PS[DH:P, r % 2, :], scalar=cst[DH:P, c:c + 1],
                                                   in1=QQ[DH:P, s, e, :].bitcast(F32), op0=ALU.mult, op1=ALU.subtract).then_inc(vec_lo, 1)
                else:
                    c = GQ + 1 if n < 4 else GQ + 4 + e
                    nc.vector.scalar_tensor_tensor(out=Kl[:, s, e, :], in0=PS[:, r % 2, :], scalar=cst[:, c:c + 1],
                                                   in1=Kh[:, s, e, :].bitcast(F32), op0=ALU.mult, op1=ALU.subtract).then_inc(vec_lo, 1)

            def bias(t):
                s = STEPS[t]
                n, e, i = s["n"], s["e"], s["i"]
                dve.wait_ge(score, t + 1)
                if t >= 4:
                    dve.wait_ge(turned, t - 3)
                if s["k"] == 0:
                    dve.wait_ge(strip_in[n % 2], 32 * (n // 2 + 1))
                if s["br"] != "cmp":
                    nk = P * (i + 1)
                    nc.vector.tensor_tensor_reduce(out=prob[:, t % 4, 0:nk], in0=PS[:, 2 + t % 2, 0:nk], in1=strip[:, n % 2, e, S - nk:S],
                                                   scale=1.0, scalar=3e38, op0=ALU.add, op1=ALU.min,
                                                   accum_out=mneg[:, t % 4:t % 4 + 1]).then_inc(biased, 1)
                else:
                    link(nc.vector.memset(sc_c, BIG))
                    for q in range(NT):
                        c0 = P * (NT - 1 - q) + CMP_LEN - 1
                        m = 7 + 8 * q
                        ins = nc.vector.tensor_tensor_reduce(out=sc_c[:, q, 0:m], in0=PS[:, 2 + t % 2, 32 * q:32 * q + m],
                                                             in1=strip[:, n % 2, e, c0:c0 + 16 * (m - 1) + 1:16], scale=1.0, scalar=1e29,
                                                             op0=ALU.add, op1=ALU.min, accum_out=mneg_c[:, q:q + 1])
                    link(ins)
                    nc.vector.tensor_tensor(sc_c, sc_c, mneg_c.unsqueeze(2).broadcast_to([P, NT, 32]), ALU.subtract).then_inc(biased, 1)

            def scale(t):
                s = STEPS[t]
                dve.wait_ge(exped, t + 1)
                n, e, i = s["n"], s["e"], s["i"]
                if s["br"] == "own":
                    nk = P * (i + 1)
                    link(nc.vector.reciprocal(rsum[:, t % 4:t % 4 + 1], rsum[:, t % 4:t % 4 + 1]))
                    nc.vector.tensor_scalar(prob[:, t % 4, 0:nk], prob[:, t % 4, 0:nk], rsum[:, t % 4:t % 4 + 1], None, ALU.mult).then_inc(scaled, 1)
                elif s["br"] != "cmp":
                    nk = P * (i + 1)
                    h = cat(s["br"]) * HN + 2 * (n - 4) + e
                    link(nc.vector.reciprocal(rsum[:, t % 4:t % 4 + 1], rsum[:, t % 4:t % 4 + 1]))
                    nc.vector.tensor_scalar(prob[:, t % 4, 0:nk], prob[:, t % 4, 0:nk], rsum[:, t % 4:t % 4 + 1], gsig[:, i, h:h + 1],
                                            ALU.mult, ALU.mult).then_inc(scaled, 1)
                else:
                    h = 2 * (n - 4) + e
                    pc = prob[:, t % 4, 0:P].rearrange("p (a b) -> p a b", a=NT)
                    link(nc.vector.reduce_sum(rsum_c, pc, AX))
                    link(nc.vector.tensor_scalar(rsum_c, rsum_c, 1e-30, None, ALU.max))
                    link(nc.vector.reciprocal(rsum_c, rsum_c))
                    link(nc.vector.tensor_tensor(rsum_c, rsum_c, gsig[:, :, h], ALU.mult))
                    nc.vector.tensor_tensor(pc, pc, rsum_c.unsqueeze(2).broadcast_to([P, NT, 32]), ALU.mult).then_inc(scaled, 1)

            def pt_low(t):
                s = STEPS[t]
                dve.wait_ge(pt_hi, t + 1)
                if s["br"] == "cmp":
                    nc.vector.tensor_tensor(PTl[0:32, s["u"] % 2, 0, :], PS[0:32, 4 + t % 2, :], PTh[0:32, s["u"] % 2, 0, :].bitcast(F32),
                                            ALU.subtract).then_inc(pt_lo, 1)
                else:
                    i = s["i"]
                    nc.vector.tensor_tensor(PTl[:, s["u"] % 2, 0:i + 1, P * i:P * (i + 1)],
                                            PS[:, 4 + t % 2, 0:P * (i + 1)].rearrange("p (j q) -> p j q", j=i + 1),
                                            PTh[:, s["u"] % 2, 0:i + 1, P * i:P * (i + 1)].bitcast(F32), ALU.subtract).then_inc(pt_lo, 1)

            rstd(1)
            for x in range(4):
                vec_low(1, x)
            for t in range(T + 2):
                if t < T:
                    bias(t)
                if 1 <= t <= T:
                    scale(t - 1)
                if t >= 2:
                    pt_low(t - 2)
                if t < T:
                    n, k, w = STEPS[t]["n"], STEPS[t]["k"], STEPS[t]["n"] + 2
                    if n < 7 and k == 4:
                        rstd(w)
                    v0 = 6 if n < 4 else 9
                    if n < 7 and k == v0:
                        vec_low(w, 0)
                        vec_low(w, 1)
                    if n < 7 and k == v0 + 1 and nvec(w) == 4:
                        vec_low(w, 2)
                        vec_low(w, 3)
                    if n > 0 and k == 2:
                        dve.wait_ge(pv_done, STEPS[last_t[n - 1]]["u"] + 1)
                        if n > 1:
                            dve.wait_ge(y_out, 16 * (n - 1))
                        else:
                            dve.wait_ge(bank_filled, use_index[("cmph", None, 1)] + 1)
                        nc.vector.tensor_copy(ystage, PS[:, 6, :]).then_inc(y_evac, 1)
            dve.wait_ge(yt_hi, 8)
            nc.vector.tensor_tensor(yTl[:, 7, :], PS[:, 6, :], yTh[:, 7, :].bitcast(F32), ALU.subtract).then_inc(y_evac, 1)

            for mg in range(2):
                for m in range(4):
                    dve.wait_ge(chunk_done, cidx[("bra", mg, 3)] + 1)
                    dve.wait_ge(ga_in[m], 16 * (mg + 1))
                    nc.vector.scalar_tensor_tensor(out=ga[:, m, :], in0=ga[:, m, :], scalar=1.0, in1=PS[:, m, :],
                                                   op0=ALU.add, op1=ALU.mult).then_inc(brA_done, 1)
                for m in range(4):
                    i = 4 * mg + m
                    dve.wait_ge(chunk_done, cidx[("brb", mg, 3)] + 1)
                    dve.wait_ge(gb_in[i % 2], 16 * (i // 2 + 1))
                    dve.wait_ge(brA_done, i + 1)
                    nc.vector.scalar_tensor_tensor(out=gb[:, i % 2, :], in0=gb[:, i % 2, :], scalar=1.0, in1=PS[:, 4 + m, :],
                                                   op0=ALU.add, op1=ALU.mult).then_inc(brB_done, 1)
                    dve.wait_ge(brB_done, i + 1)
                    nc.vector.tensor_tensor(ga[:, m, :], ga[:, m, :], gb[:, i % 2, :], ALU.add).then_inc(br_sum, 1)
                for m in range(4):
                    i = 4 * mg + m
                    dve.wait_ge(mT_hi, i + 1)
                    nc.vector.scalar_tensor_tensor(out=mTl[:, i, :], in0=ga[:, m, :], scalar=0.5, in1=mTh[:, i, :].bitcast(F32),
                                                   op0=ALU.mult, op1=ALU.subtract).then_inc(mT_lo, 1)
            for k in range(2):
                dve.wait_ge(pT_hi, k + 1)
                nc.vector.tensor_tensor(pTl[:, k, :], PS[:, 4 + k, :], pTh[:, k, :].bitcast(F32), ALU.subtract).then_inc(pT_lo, 1)
            dve.wait_ge(xT_done, 8)
            for mg in range(2):
                for m in range(4):
                    i = 4 * mg + m
                    dve.wait_ge(chunk_done, cidx[("wo", mg, KT - 1)] + 1)
                    nc.vector.tensor_tensor(x1T[:, i, :], PS[:, i, :], x1T[:, i, :], ALU.add).then_inc(x1_done, 1)
            dve.wait_ge(tok_sum, 1)
            rsqrt(st[:, 80:84], PS[:, 4, 0:4], 1.0 / D, 4)
            for tt in range(NT):
                ins = nc.vector.tensor_scalar(rdiag[:, tt * P:(tt + 1) * P], ident, st[:, 80 + tt:81 + tt], None, ALU.mult)
            ins.then_inc(rdiag_done, 1)
            dve.wait_ge(bc_done, 1)
            for i in range(KT):
                if i >= 2:
                    dve.wait_ge(h2_lo, i - 1)
                nc.vector.scalar_tensor_tensor(out=hst[:, i % 2, :], in0=x1T[:, i, :], scalar=cst[:, 8 + i:9 + i], in1=rbc,
                                               op0=ALU.mult, op1=ALU.mult).then_inc(h2_f, 1)
            for u in range(NF // 2):
                for q in range(2):
                    f = 2 * u + q
                    for half, (dst, sb_, sm) in enumerate(((ya, ya_bias, ya_conv), (yl, yl_bias, yl_conv))):
                        b = up_bank(u) + 2 * half + q
                        col = half * NF + f
                        dve.wait_ge(sb_, f + 1)
                        link(nc.vector.scalar_tensor_tensor(out=dst[:, f % 2, 1:S], in0=PS[:, b, 0:S - 1], scalar=cst[:, CONVW + 44 + col:CONVW + 45 + col],
                                                            in1=dst[:, f % 2, 1:S], op0=ALU.mult, op1=ALU.add))
                        nc.vector.scalar_tensor_tensor(out=dst[:, f % 2, 2:S], in0=PS[:, b, 0:S - 2], scalar=cst[:, CONVW + col:CONVW + 1 + col],
                                                       in1=dst[:, f % 2, 2:S], op0=ALU.mult, op1=ALU.add).then_inc(sm, 1)
                for q in range(2):
                    f = 2 * u + q
                    dve.wait_ge(gelu_done, f + 1)
                    dve.wait_ge(yl_conv, f + 1)
                    nc.vector.tensor_tensor(ya[:, f % 2, :], ya[:, f % 2, :], yl[:, f % 2, :], ALU.mult).then_inc(glu_done, 1)
                for q in range(2):
                    f = 2 * u + q
                    dve.wait_ge(gT_hi, f + 1)
                    nc.vector.tensor_tensor(gTl[:, f, :], ya[:, f % 2, :], gTh[:, f, :].bitcast(F32), ALU.subtract).then_inc(gT_lo, 1)
            for mg in range(2):
                for m in range(4):
                    i = 4 * mg + m
                    dve.wait_ge(chunk_done, cidx[("dn", mg, NF - 1)] + 1)
                    nc.vector.tensor_tensor(x1T[:, i, :], PS[:, 4 * mg + m, :], x1T[:, i, :], ALU.add).then_inc(x2_done, 1)
                for tt in range(NT):
                    dve.wait_ge(x2_tr, 4 * mg + tt + 1)
                    nc.vector.tensor_copy(x2n[:, tt, mg * 512:(mg + 1) * 512], PS[:, 4 * mg + tt, :]).then_inc(x2n_done, 1)
            for k in range(8):
                ng, tt = k // 4, k % 4
                dve.wait_ge(th_done, k + 1)
                dve.wait_ge(pp_in, 16 * 4 if k < 4 else 16 * 8)
                nc.vector.scalar_tensor_tensor(out=thb[:, k % 4, :], in0=thb[:, k % 4, :], scalar=1.0, in1=ppb[:, k % 4, :],
                                               op0=ALU.add, op1=ALU.mult).then_inc(th_mul, 1)
                dve.wait_ge(th_mul, k + 1)
                dve.wait_ge(x2n_done, 8)
                o = x2n[:, tt, ng * 512:(ng + 1) * 512]
                nc.vector.tensor_tensor(o, o, thb[:, k % 4, :], ALU.add).then_inc(o_done, 1)

        @block.tensor
        def _(pe):
            def three(o, ah, al, bh, bl, first, last):
                nc.tensor.matmul(o, ah, bh, start=first, stop=False)
                nc.tensor.matmul(o, ah, bl, start=False, stop=False)
                return nc.tensor.matmul(o, al, bh, start=False, stop=last)

            def turn_consts(k):
                r = use_index[("cst", None, k)]
                nr = (98, P, 4)[k]
                wait_free(pe, r)
                pe.wait_ge(const_in, 16 * 18)
                pe.wait_ge(pool_const, 4)
                nc.tensor.transpose(PS[:, r % 2, 0:nr], rows[0:nr, k, :], ident[0:nr, 0:nr]).then_inc(bank_filled, 1)

            def turn_input(kt):
                r = use_index[("trh", None, kt)]
                wait_free(pe, r)
                for tt in range(NT):
                    pe.wait_ge(h_nat, tt + 1)
                    ins = nc.tensor.transpose(PS[:, r % 2, P * tt:P * (tt + 1)], xnat[:, tt, P * kt:P * (kt + 1)], ident)
                ins.then_inc(bank_filled, 1)

            def project(w, tt):
                r = use_index[("proj", w, tt)]
                c = ucols(w)
                wait_free(pe, r)
                for kt in range(KT):
                    pe.wait_ge(w_lo, KT * w + kt + 1)
                    pe.wait_ge(hT_lo, kt + 1)
                    t_ = slice(P * tt, P * (tt + 1))
                    ins = three(PS[:, r % 2, 0:c], hTh[:, kt, t_], hTl[:, kt, t_], Wh[:, kt, 0:c], Wl[:, kt, 0:c], kt == 0, kt == KT - 1)
                ins.then_inc(bank_filled, 1)

            def turn_vector(w, x):
                r = use_index[("vec", w, x)]
                wait_free(pe, r)
                pe.wait_ge(norm_done, w + 1)
                for tt in range(NT):
                    ins = nc.tensor.transpose(PS[:, r % 2, P * tt:P * (tt + 1)], qn[:, tt, x, :], ident)
                ins.then_inc(bank_filled, 1)

            def gate(j):
                r = use_index[("gate", None, j)]
                wait_free(pe, r)
                pe.wait_ge(g_lo, j + 1)
                for kt in range(KT):
                    ins = three(PS[:, r % 2, :], Gh[:, kt, :], Gl[:, kt, :], hTh[:, kt, :], hTl[:, kt, :], kt == 0, kt == KT - 1)
                ins.then_inc(bank_filled, 1)

            def compress(kv):
                r = use_index[("cmph", None, kv)]
                wait_free(pe, r)
                pe.wait_ge(w1_in, 32 * (kv + 1))
                pe.wait_ge(bp_done, kv + 1)
                o = bp[:, kv, 0:992].rearrange("p (g l n) -> p g l n", g=2, l=16)
                for c in range(16):
                    wt = graw[:, c, :] if c < 8 else w1b[:, c - 8, :]
                    ins = nc.tensor.matmul(PS[:, r % 2, 0:62].rearrange("p (g n) -> p g n", g=2), wt, o[:, :, c, :], start=(c == 0), stop=(c == 15))
                ins.then_inc(bank_filled, 1)

            def compress_out():
                r = use_index[("cmpo", None, 0)]
                wait_free(pe, r)
                pe.wait_ge(hid_done, 2)
                for kv in range(2):
                    for g in range(2):
                        o = (2 * kv + g) * DH
                        ins = nc.tensor.matmul(PS[0:NCMP, r % 2, o:o + DH], hid[:, 62 * kv + 31 * g:62 * kv + 31 * (g + 1)], w2c[:, kv, :],
                                               start=True, stop=True)
                ins.then_inc(bank_filled, 1)
                r = use_index[("cmpt", None, 0)]
                wait_free(pe, r)
                pe.wait_ge(kcn_done, 1)
                for g in range(2):
                    ins = nc.tensor.transpose(PS[:, r % 2, 32 * g:32 * g + NCMP], kcn[0:NCMP, g, :], ident[0:NCMP, 0:NCMP])
                ins.then_inc(bank_filled, 1)

            def scores(t):
                s = STEPS[t]
                n, e, i = s["n"], s["e"], s["i"]
                if t >= 2:
                    pe.wait_ge(biased, t - 1)
                if s["k"] == 0:
                    pe.wait_ge(vec_lo, vec_base[n + 1] + nvec(n + 1) - 4)
                o = PS[:, 2 + t % 2, :]
                if s["br"] == "cmp":
                    pe.wait_ge(kc_lo, 1)
                    g = (n - 4) // 2
                    for q in range(NT):
                        nc.tensor.matmul(o[:, 32 * q:32 * q + 32], QQ[:, n % 2, e, P * q:P * (q + 1)], KCh[:, g, :], start=True, stop=False)
                        ins = nc.tensor.matmul(o[:, 32 * q:32 * q + 32], QQ[:, n % 2, e, P * q:P * (q + 1)], KCl[:, g, :], start=False, stop=True)
                else:
                    ks, ke = kslot(n, e, s["br"])
                    nk = P * (i + 1)
                    nc.tensor.matmul(o[:, 0:nk], QQ[:, n % 2, e, P * i:P * (i + 1)], Kh[:, ks, ke, 0:nk], start=True, stop=False)
                    ins = nc.tensor.matmul(o[:, 0:nk], QQ[:, n % 2, e, P * i:P * (i + 1)], Kl[:, ks, ke, 0:nk], start=False, stop=True)
                ins.then_inc(score, 1)

            def turn_probs(t):
                s = STEPS[t]
                pe.wait_ge(scaled, t + 1)
                if t >= 2:
                    pe.wait_ge(pt_lo, t - 1)
                if s["br"] == "cmp":
                    for q in range(NT):
                        ins = nc.tensor.transpose(PS[0:32, 4 + t % 2, P * q:P * (q + 1)], prob[:, t % 4, 32 * q:32 * q + 32], ident)
                else:
                    for j in range(s["i"] + 1):
                        ins = nc.tensor.transpose(PS[:, 4 + t % 2, P * j:P * (j + 1)], prob[:, t % 4, P * j:P * (j + 1)], ident)
                ins.then_inc(turned, 1)

            def values(t):
                s = STEPS[t]
                n, e, u = s["n"], s["e"], s["u"]
                pe.wait_ge(pt_lo, t + 1)
                opening = u == STEPS[first_t[n]]["u"]
                closing = t == last_t[n]
                if opening:
                    pe.wait_ge(v_lo, min(n + 1, 5) if n < 6 else 6)
                    if n > 0:
                        pe.wait_ge(y_evac, n)
                c0 = 0 if e == 0 else DH
                if s["br"] == "cmp":
                    pe.wait_ge(vc_lo, 1)
                    g = (n - 4) // 2
                    ins = three(PS[:, 6, :], VCh[0:32, g, c0:c0 + P], VCl[0:32, g, c0:c0 + P], PTh[0:32, u % 2, 0, :], PTl[0:32, u % 2, 0, :],
                                False, closing)
                else:
                    vs = vslot(n, s["br"])
                    for j in (reversed(range(NT)) if closing else range(NT)):
                        q = slice(P * j, S)
                        ins = three(PS[:, 6, q], Vh[:, vs, j, c0:c0 + P], Vl[:, vs, j, c0:c0 + P], PTh[:, u % 2, j, q], PTl[:, u % 2, j, q],
                                    opening and j == 0, closing and j == 0)
                ins.then_inc(pv_done, 1)

            for k in range(3):
                turn_consts(k)
            for kt in range(KT):
                turn_input(kt)
            for tt in range(NT):
                project(0, tt)
            for x in range(4):
                turn_vector(0, x)
            for tt in range(NT):
                project(1, tt)
            compress(0)
            compress(1)
            compress_out()
            for x in range(4):
                turn_vector(1, x)
            for t in range(T + 2):
                if t < T:
                    scores(t)
                    n, k, w = STEPS[t]["n"], STEPS[t]["k"], STEPS[t]["n"] + 2
                    if n < 7 and k < NT:
                        project(w, k)
                    v0, g0, g1 = (5, 4, 7) if n < 4 else (8, 5, 12)
                    if k == g0:
                        gate(2 * n)
                    if n < 7 and k == v0:
                        turn_vector(w, 0)
                        turn_vector(w, 1)
                    if n < 7 and k == v0 + 1 and nvec(w) == 4:
                        turn_vector(w, 2)
                        turn_vector(w, 3)
                    if k == g1:
                        gate(2 * n + 1)
                if 1 <= t <= T:
                    turn_probs(t - 1)
                if t >= 2 and STEPS[t - 2]["last"]:
                    values(t - 2)

            def turn_x(tt):
                pe.wait_ge(xs_in, 16 * (tt + 1))
                b = 4 + 2 * (tt % 2)
                if tt == 0:
                    pe.wait_ge(pt_lo, T)
                if tt == 1:
                    pe.wait_ge(y_evac, 8)
                if tt >= 2:
                    pe.wait_ge(brB_done, 8)
                for kt in range(KT):
                    ins = nc.tensor.transpose(PS[:, b + kt // 4, P * (kt % 4):P * (kt % 4 + 1)], xs[:, P * kt:P * (kt + 1)], ident)
                ins.then_inc(xs_tr, 1)

            def turn_p():
                pe.wait_ge(xs_in, 16 * 8)
                pe.wait_ge(xT_done, 8)
                for k in range(2):
                    for tt in range(NT):
                        ins = nc.tensor.transpose(PS[:, 4 + k, P * tt:P * (tt + 1)], xs[:, tt * PLE + P * k:tt * PLE + P * (k + 1)], ident)
                    ins.then_inc(p_tr, 1)

            def token_sums():
                pe.wait_ge(ssq_done, KT)
                pe.wait_ge(x1_done, KT)
                for tt in range(NT):
                    ins = nc.tensor.matmul(PS[:, 4, tt:tt + 1], sumsq[:, P * tt:P * (tt + 1)], ones[:, 0:1], start=True, stop=True)
                ins.then_inc(tok_sum, 1)

            def spread():
                pe.wait_ge(rdiag_done, 1)
                for tt in range(NT):
                    ins = nc.tensor.matmul(PS[:, 4, P * tt:P * (tt + 1)], ones, rdiag[:, P * tt:P * (tt + 1)], start=True, stop=True)
                ins.then_inc(bc_mm, 1)

            def turn_x2(half):
                pe.wait_ge(x2_done, 4 * half + 4)
                for tt in range(NT):
                    for kt in range(4):
                        ins = nc.tensor.transpose(PS[:, 4 * half + tt, P * kt:P * (kt + 1)], x1T[:, 4 * half + kt, P * tt:P * (tt + 1)], ident)
                    ins.then_inc(x2_tr, 1)

            for c in range(NC):
                kind, a, kt = CHUNKS[c]
                if c == 1:
                    turn_x(0)
                if c == 3:
                    turn_x(1)
                if (kind, a, kt) == ("wo", 0, 3):
                    turn_x(2)
                if (kind, a, kt) == ("wo", 0, 5):
                    turn_x(3)
                if (kind, a, kt) == ("wo", 1, 0):
                    turn_p()
                if (kind, a, kt) == ("ple", 1, 0):
                    token_sums()
                if (kind, a, kt) == ("ple", 1, 1):
                    spread()
                if (kind, a, kt) == ("dn", 1, 8):
                    turn_x2(0)
                if (kind, a, kt) == ("pg", 0, 6):
                    turn_x2(1)
                if kind == "bra":
                    pe.wait_ge(yt_lo, kt + 1)
                    act_h, act_l = yTh[:, kt, :], yTl[:, kt, :]
                    b0 = 0
                    if a == 0 and kt == 0:
                        pe.wait_ge(gate_tanh, NGATE)
                        pe.wait_ge(biased, T)
                    if a == 1 and kt == 0:
                        pe.wait_ge(brA_done, 4)
                elif kind == "brb":
                    if kt < 3:
                        pe.wait_ge(yt_lo, 4 + kt + 1)
                    else:
                        pe.wait_ge(y_evac, 8)
                    act_h, act_l = yTh[:, 4 + kt, :], yTl[:, 4 + kt, :]
                    b0 = 4
                    if kt == 0:
                        pe.wait_ge(xT_done, 4)
                        if a:
                            pe.wait_ge(brB_done, 4)
                elif kind == "wo":
                    pe.wait_ge(mT_lo, kt + 1)
                    act_h, act_l = mTh[:, kt, :], mTl[:, kt, :]
                    b0 = 4 * a
                    if kt == 0:
                        pe.wait_ge(brA_done, 8)
                        if a:
                            pe.wait_ge(pT_lo, 2)
                elif kind == "ple":
                    b0 = None
                    if kt == 0:
                        pe.wait_ge(x1_done, 4 if a == 0 else 8)
                        if a:
                            pe.wait_ge(pp_ev, 1)
                elif kind == "up":
                    pe.wait_ge(h2_lo, kt + 1)
                    act_h, act_l = h2h[:, kt, :], h2l[:, kt, :]
                    b0 = up_bank(a)
                    if kt == 0:
                        if a <= 1:
                            pe.wait_ge(pp_ev, 7 + a)
                        else:
                            pe.wait_ge(ya_conv, 2 * a - 2)
                            pe.wait_ge(yl_conv, 2 * a - 2)
                elif kind == "dn":
                    pe.wait_ge(gT_lo, kt + 1)
                    act_h, act_l = gTh[:, kt, :], gTl[:, kt, :]
                    b0 = 4 * a
                    if kt == 0:
                        u = 9 + a
                        pe.wait_ge(ya_conv, 2 * u + 2)
                        pe.wait_ge(yl_conv, 2 * u + 2)
                else:
                    pe.wait_ge(x2_lo, kt + 1)
                    b0 = None
                    if kt == 0:
                        pe.wait_ge(x2n_done, 4 * (a + 1))
                pe.wait_ge(w2_lo, c + 1)
                last = kt == {"bra": 3, "brb": 3, "wo": KT - 1, "ple": 1, "up": KT - 1, "dn": NF - 1, "pg": KT - 1}[kind]
                wh, wl = W2h[:, c % RING, :], W2l[:, c % RING, :]
                for m in range(4):
                    cs = slice(P * m, P * (m + 1))
                    if kind in ("ple", "pg"):
                        ah, al = (pTh, pTl) if kind == "ple" else (h2h, h2l)
                        b = ple_bank(a, m) if kind == "ple" else 4 * a + m
                        ins = three(PS[:, b, :], ah[:, kt, cs], al[:, kt, cs], wh, wl, kt == 0, last)
                    else:
                        ins = three(PS[:, b0 + m, :], wh[:, cs], wl[:, cs], act_h, act_l, kt == 0, last)
                ins.then_inc(chunk_done, 1)


_INS = ['x', 'p', 'rel_bias', 'attn_norm', 'w_in', 'moba_q_gain', 'moba_k_gain', 'nsa_q_gain', 'nsa_k_gain',
        'cmp_pos_k', 'cmp_w1_k', 'cmp_w2_k', 'cmp_pos_v', 'cmp_w1_v', 'cmp_w2_v', 'w_br_moba', 'w_br_nsa', 'w_o',
        'ffn_norm', 'w_up', 'conv_w', 'conv_b', 'w_down', 'w_ple_gate', 'w_ple']


def kernel(**inputs):
    import numpy as _np
    import concourse.bacc as _bacc
    from concourse.bass_utils import run_bass_kernel_spmd as _run

    nc = _bacc.Bacc("TRN2", target_bir_lowering=False, num_devices=1)
    arrays, args = {}, {}
    for name in _INS:
        a = _np.ascontiguousarray(inputs[name])
        arrays[f"in_{name}_dram"] = a
        args[name] = nc.dram_tensor(f"in_{name}_dram", a.shape, mybir.dt.from_np(a.dtype), kind="ExternalInput").ap()
    out = nc.dram_tensor("out_0_dram", (1, S, D), F32, kind="ExternalOutput").ap()
    layer(nc, args, out)
    r = _run(nc, [arrays], core_ids=[0])
    return r.results[0]["out_0_dram"]
```

```python
from contextlib import ExitStack

import numpy as np

import concourse.bass as bass
from concourse import mybir

ALU = mybir.AluOpType
ACT = mybir.ActivationFunctionType
F32 = mybir.dt.float32
F32R = mybir.dt.float32r
I32 = mybir.dt.int32
AX = mybir.AxisListType.X

P = 128
S, D, DH = 512, 1024, 64
NT, KT = S // P, D // P
DFF, PLE = 2816, 256
NF = DFF // P
HM = HN = 8
GR = 2
CMP_LEN, CMP_STRIDE = 32, 16
NCMP = (S - CMP_LEN) // CMP_STRIDE + 1
CW = 384
C_MQ, C_MK, C_NQ, C_KC, C_KS, C_NG, C_MG = 0, 512, 1536, 2048, 2304, 2816, 2840
NPAIR = 8
NGATE = 2 * D // P
EPS = 1e-6
BIG = 1e30
PITCH = 640


def bucket_edges():
    n = np.arange(S)
    nf = np.maximum(n, 1).astype(np.float32)
    large = 16 + (np.log(nf / np.float32(16)) / np.float32(np.log(128 / 16)) * np.float32(16)).astype(np.int32)
    b = np.where(n < 16, n, np.minimum(large, 31))
    return [(int(np.min(n[b == k])), int(np.max(n[b == k])) + 1) for k in range(32)]


def attention_steps():
    steps, u = [], 0
    for n in range(NPAIR):
        for e in range(2):
            for br in (["own"] if n < 4 else ["slc", "win", "cmp"]):
                tiles = range(1) if br == "cmp" else range(NT)
                for i in tiles:
                    steps.append(dict(n=n, e=e, br=br, i=i, u=u, last=(i == tiles[-1]), first=False, k=0))
                u += 1
        steps[-1]["pair_last"] = True
    k = 0
    for t, s in enumerate(steps):
        new = t == 0 or steps[t - 1]["n"] != s["n"]
        k = 0 if new else k + 1
        s["k"], s["first"] = k, new
    return steps


def layer(nc, A, out):
    STEPS = attention_steps()
    T = len(STEPS)
    first_t = [next(t for t, s in enumerate(STEPS) if s["n"] == n) for n in range(NPAIR)]
    last_t = [max(t for t, s in enumerate(STEPS) if s["n"] == n) for n in range(NPAIR)]
    NSTEP = [last_t[n] - first_t[n] + 1 for n in range(NPAIR)]
    unit_last_t = {s["u"]: t for t, s in enumerate(STEPS) if s["last"]}

    def ucols(w):
        return 2 * P + 24 if w == 0 else (P if w in (6, 8) else CW)

    def udmas(w):
        return {0: 0, 5: 3, 7: 3}.get(w, 1)

    def nvec(w):
        return 2 if w in (6, 8) else 4

    W_UNITS = 9
    USES = []
    USES += [("proj", 0, tt) for tt in range(NT)]
    USES += [("vec", 0, x) for x in range(4)]
    USES += [("proj", 1, tt) for tt in range(NT)]
    USES += [("vec", 1, x) for x in range(4)]
    for w in range(2, W_UNITS):
        USES += [("proj", w, tt) for tt in range(NT)]
        USES += [("vec", w, x) for x in range(nvec(w))]
    use_index = {u: r for r, u in enumerate(USES)}
    GATE_STEPS = {}
    for n, tiles in enumerate([[2], [3], [4], [5], [6, 7, 8], [9, 10], [11, 12, 13], [14, 15]]):
        for a, j in enumerate(tiles):
            if n < 4:
                lots = {3: range(0, 3), 4: range(3, 6), 5: range(6, 8)}
            else:
                k0 = (0, 6, 12)[a] if len(tiles) == 3 else (3, 11)[a]
                lots = {k0 + b: range(2 * b, 2 * b + 2) for b in range(4)}
            for k, kts in lots.items():
                GATE_STEPS[(n, k)] = (j, kts)
    gate_end = {j: first_t[n] + k for (n, k), (j, kts) in GATE_STEPS.items() if kts[-1] == KT - 1}

    PROJ = {}
    for w in range(2, W_UNITS):
        t0 = first_t[w - 2]
        if w < 6:
            for tt in range(NT):
                PROJ[t0 + tt - 1] = (w, tt, range(KT))
        else:
            for a in range(2 * NT):
                PROJ[t0 + a] = (w, a // 2, range(4 * (a % 2), 4 * (a % 2) + 4))

    def proj_end(t):
        p = PROJ.get(t - 1)
        return p[:2] if p and t > 0 and p[2][-1] == KT - 1 else None

    def square_step(n):
        return 3 if n < 4 else 8

    def norm_step(n):
        return square_step(n) + 1

    def v_step(n):
        return square_step(n) + 2

    def vec_steps(n, k):
        k0 = 5 if n < 4 else 12
        if n == NPAIR - 1 or k not in (k0, k0 + 1) or (k == k0 + 1 and nvec(n + 2) == 2):
            return ()
        return (0, 1) if k == k0 else (2, 3)

    def split_steps(n, k):
        if n + 3 >= W_UNITS:
            return ()
        if n < 4:
            return (2 * (k - 3), 2 * (k - 3) + 1) if 3 <= k < 7 else ()
        return (k - 9,) if 9 <= k < 17 else ()

    LAG = 3
    VLAG = LAG + 2
    vec_base = {}
    acc = 0
    for w in range(W_UNITS):
        vec_base[w] = acc
        acc += nvec(w)

    CHUNKS = []
    for mg in range(2):
        CHUNKS += [("bra", mg, kt) for kt in range(4)] + [("brb", mg, kt) for kt in range(4)]
    for mg in range(2):
        CHUNKS += [("wo", mg, kt) for kt in range(KT)]
    for ng in range(2):
        CHUNKS += [("ple", ng, kt) for kt in range(2)]
    for u in range(NF // 2):
        CHUNKS += [("up", u, kt) for kt in range(KT)]
    for mg in range(2):
        CHUNKS += [("dn", mg, kt) for kt in range(NF)]
    for ng in range(2):
        CHUNKS += [("pg", ng, kt) for kt in range(KT)]
    NC = len(CHUNKS)
    cidx = {c: i for i, c in enumerate(CHUNKS)}
    RING = 8

    x_d = A["x"].rearrange("b (t p) d -> (b t) p d", p=P)
    o_d = out.rearrange("b (t p) d -> (b t) p d", p=P)
    p_d = A["p"].rearrange("l b (t p) d -> (l b t) p d", p=P)
    win = A["w_in"].rearrange("l (k p) n -> (l k) p n", p=P)
    brm = A["w_br_moba"].rearrange("l (k p) n -> (l k) p n", p=P)
    brn = A["w_br_nsa"].rearrange("l (k p) n -> (l k) p n", p=P)
    wo_d = A["w_o"].rearrange("l (k p) n -> (l k) p n", p=P)
    up_d = A["w_up"].rearrange("l (k p) (h n) -> (l k) p h n", p=P, h=2)
    dn_d = A["w_down"].rearrange("l (k p) n -> (l k) p n", p=P)
    pg_d = A["w_ple_gate"].rearrange("l (k p) n -> (l k) p n", p=P)
    pl_d = A["w_ple"].rearrange("l (k p) n -> (l k) p n", p=P)
    w1_d = [A["cmp_w1_k"].rearrange("l (c p) h -> p (l c) h", p=P), A["cmp_w1_v"].rearrange("l (c p) h -> p (l c) h", p=P)]

    skew_d = nc.dram_tensor("skew", [16, P * PITCH], F32, kind="Internal").ap()
    gate_d = nc.dram_tensor("gates", [NGATE, P, S], F32, kind="Internal").ap()
    y_d = nc.dram_tensor("ys", [NPAIR, P, S], F32, kind="Internal").ap()
    pp_d = nc.dram_tensor("pps", [2 * NT, P, S], F32, kind="Internal").ap()

    with ExitStack() as ctx:
        def sem(n):
            return ctx.enter_context(nc.semaphore(n))

        R = ctx.enter_context(nc.sbuf_tensor("split_arena", [P, 38912], F32R))
        F = ctx.enter_context(nc.sbuf_tensor("plain_arena", [P, 14280], F32))
        PS = ctx.enter_context(nc.psum_tensor("banks", [P, 8, 512], F32))

        def r3(o, a, b):
            return R[:, o:o + a * b].rearrange("p (a b) -> p a b", a=a)

        def f3(o, a, b):
            return F[:, o:o + a * b].rearrange("p (a b) -> p a b", a=a)

        hTh, hTl = r3(0, KT, S), r3(4096, KT, S)
        Wh, Wl = r3(8192, KT, CW), r3(8192 + KT * CW, KT, CW)
        Gh, Gl = r3(14336, KT, P), r3(15360, KT, P)
        PTh = R[:, 16384:20480].rearrange("p (u j q) -> p u j q", u=2, j=NT)
        PTl = R[:, 20480:24576].rearrange("p (u j q) -> p u j q", u=2, j=NT)
        QQ = R[:, 24576:26624].rearrange("p (s e q) -> p s e q", s=2, e=2)
        Kh = R[:, 26624:28672].rearrange("p (s e q) -> p s e q", s=2, e=2)
        Kl = R[:, 28672:30720].rearrange("p (s e q) -> p s e q", s=2, e=2)
        Vh = R[:, 30720:33792].rearrange("p (s t c) -> p s t c", s=4, t=NT)
        Vl = R[:, 33792:36864].rearrange("p (s t c) -> p s t c", s=4, t=NT)
        VCh, VCl = r3(36864, 2, 192), r3(37248, 2, 192)
        KCh, KCl = r3(37632, 2, 32), r3(37696, 2, 32)
        yTh, yTl = r3(0, KT, S), r3(4096, KT, S)
        h2h, h2l = r3(0, KT, S), r3(4096, KT, S)
        W2h, W2l = r3(8192, RING, 512), r3(12288, RING, 512)
        mTh, mTl = r3(16384, KT, S), r3(20480, KT, S)
        pTh, pTl = r3(36864, 2, S), r3(37888, 2, S)
        gTh, gTl = r3(16384, NF, S), r3(16384 + NF * S, NF, S)

        raw = f3(0, KT, CW)
        graw = f3(3072, KT, P)
        strip = F[:, 4096:6144].rearrange("p (s e c) -> p s e c", s=2, e=2)
        prob = f3(6144, 4, S)
        xnat = f3(4096, NT, D)
        tcmp = f3(6144, 4, S)
        qkv = f3(8192, NT, CW)
        sq = F[:, 9728:10752].rearrange("p (t c) -> p t c", t=NT)
        qn = F[:, 9728:11776].rearrange("p (t v c) -> p t v c", t=NT, v=4)
        bp = f3(9728, 2, 1024)
        ystage = F[:, 11776:12288]
        gstage = F[:, 12288:12800]
        w1k = f3(4096, 16, P)
        rtab = F[0:16, 11776:12288]
        masked = F[0:16, 13600:13728]
        rbt = F[0:16, 8900:8932]
        rows = f3(9216, 3, P)
        ytmp = f3(8192, 7, S)
        raw2 = f3(0, RING, 512)
        x1T = f3(4096, KT, S)
        xs = F[:, 8192:9216]
        gb = f3(9216, 2, S)
        ga = f3(10240, 4, S)
        spare = F[:, 12288:12800]
        sumsq = F[:, 12288:12800]
        sqt = f3(8192, 2, S)
        rdiag = F[:, 9216:9728]
        rbc = F[:, 9728:10240]
        hst = f3(10240, 2, S)
        ppst = [F[:, o:o + S] for o in (11264, 11776, 8192, 8704)]
        ya, yl = f3(8192, 2, S), f3(10240, 2, S)
        x2n = f3(8192, NT, D)
        thb = f3(4096, 4, S)
        ppb = f3(6144, 4, S)
        ident = F[:, 12800:12928]
        ones = F[:, 12928:13056]
        cst = F[:, 13056:13296]
        gsig = F[:, 13296:13392].rearrange("p (t c) -> p t c", t=NT)
        st = F[:, 13392:13520]
        rq = F[:, 13520:13600]
        sc_c = f3(13600, NT, 32)
        hid = F[:, 13728:13852]
        kcn = F[:, 13852:13852 + 256].rearrange("p (g c) -> p g c", g=2)
        w2c = F[:, 14108:14236].rearrange("p (v c) -> p v c", v=2)
        neg8 = st[:, 100:102]
        mneg, rsum = st[:, 0:4], st[:, 4:8]
        rsum_c, mneg_c = st[:, 8:12], st[:, 12:16]
        ssx = st[:, 16:20]
        ss = st[:, 20:36]
        s_k = st[:, 36:38]

        CONVB, POSK, POSV, GQ, CONVW = 16, 60, 76, 92, 98

        x_in = [sem(f"x_in{i}") for i in range(NT)]
        const_in, rbt_in, w2c_in = sem("const_in"), sem("rbt_in"), sem("w2c_in")
        raw0_in = [sem("raw0_in0"), sem("raw0_in1")]
        raw_in = [sem(f"raw_in{k}") for k in range(KT)]
        graw_in = sem("graw_in")
        strip_in = [sem("strip_in0"), sem("strip_in1")]
        skew_out = sem("skew_out")
        w1k_in = sem("w1k_in")
        y_out, g_out = sem("y_out"), sem("g_out")
        y_in = sem("y_in")
        pool_const = sem("pool_const")
        rtab_done = sem("rtab_done")
        x_sq = sem("x_sq")
        h_nat = sem("h_nat")
        bank_filled = sem("bank_filled")
        cst_turned, x_turned = sem("cst_turned"), sem("x_turned")
        cmp_hidden, cmp_out, cmp_turned = sem("cmp_hidden"), sem("cmp_out"), sem("cmp_turned")
        hT_hi, hT_lo = sem("hT_hi"), sem("hT_lo")
        cst_done = sem("cst_done")
        w_hi, w_lo = sem("w_hi"), sem("w_lo")
        g_hi, g_lo = sem("g_hi"), sem("g_lo")
        w_used, gate_filled = sem("w_used"), sem("gate_filled")
        norm_dve = sem("norm_dve")
        qkv_done = sem("qkv_done")
        sq_done = sem("sq_done")
        rstd_done = sem("rstd_done")
        norm_done = sem("norm_done")
        vec_hi, vec_lo = sem("vec_hi"), sem("vec_lo")
        v_hi, v_lo = sem("v_hi"), sem("v_lo")
        gate_tanh = sem("gate_tanh")
        gsig_tanh, gsig_done = sem("gsig_tanh"), sem("gsig_done")
        tcmp_a, tcmp_b = sem("tcmp_a"), sem("tcmp_b")
        bp_done = sem("bp_done")
        hid_done = sem("hid_done")
        cmp_sq = sem("cmp_sq")
        kcn_done = sem("kcn_done")
        vc_hi, vc_lo = sem("vc_hi"), sem("vc_lo")
        kc_hi, kc_lo = sem("kc_hi"), sem("kc_lo")
        score, biased, exped, scaled = sem("score"), sem("biased"), sem("exped"), sem("scaled")
        turned, pt_hi, pt_lo = sem("turned"), sem("pt_hi"), sem("pt_lo")
        pv_done = sem("pv_done")
        y_evac = sem("y_evac")
        chain = sem("dve_chain")
        yt_hi, yt_lo = sem("yt_hi"), sem("yt_lo")
        raw2_in = [sem(f"raw2_in{k}") for k in range(RING)]
        w2_hi, w2_lo, chunk_done = sem("w2_hi"), sem("w2_lo"), sem("chunk_done")
        xs_in, xs_tr, xT_done = sem("xs_in"), sem("xs_tr"), sem("xT_done")
        p_tr, pT_hi, pT_lo = sem("p_tr"), sem("pT_hi"), sem("pT_lo")
        ga_in, gb_in = [sem(f"ga_in{i}") for i in range(4)], [sem(f"gb_in{i}") for i in range(2)]
        brA_done, brB_done, br_sum = sem("brA_done"), sem("brB_done"), sem("br_sum")
        mT_hi, mT_lo = sem("mT_hi"), sem("mT_lo")
        x1_done, x1_sq, ssq_done = sem("x1_done"), sem("x1_sq"), sem("ssq_done")
        tok_sum, rdiag_done, bc_mm, bc_done = sem("tok_sum"), sem("rdiag_done"), sem("bc_mm"), sem("bc_done")
        h2_f, h2_hi, h2_lo = sem("h2_f"), sem("h2_hi"), sem("h2_lo")
        pp_ev, pp_out = sem("pp_ev"), [sem(f"pp_out{i}") for i in range(4)]
        ya_bias, yl_bias = sem("ya_bias"), sem("yl_bias")
        ya_conv, yl_conv = sem("ya_conv"), sem("yl_conv")
        gelu_done, glu_done, gT_hi, gT_lo = sem("gelu_done"), sem("glu_done"), sem("gT_hi"), sem("gT_lo")
        x2_done, x2_hi, x2_lo = sem("x2_done"), sem("x2_hi"), sem("x2_lo")
        x2_tr, x2n_done = sem("x2_tr"), sem("x2n_done")
        pp_in, th_done, th_mul, o_done, o_out = sem("pp_in"), sem("th_done"), sem("th_mul"), sem("o_done"), sem("o_out")

        def wait_free(eng, r):
            if r < 2:
                return
            kind, w, x = USES[r - 2]
            if kind == "proj":
                eng.wait_ge(qkv_done, 4 * w + x + 1)
            elif kind == "vec":
                if w == 0:
                    eng.wait_ge(tcmp_b, x + 1)
                else:
                    eng.wait_ge(vec_lo, vec_base[w] + x + 1 - 4)

        def turn_bank(kt):
            return 2 + kt % 6

        def kslot(n, e, br):
            if n < 4:
                return n % 2, e
            return (n - 4) // 2, (0 if br == "slc" else 1)

        def vslot(n, br):
            if n < 4:
                return n % 2
            return 2 * (1 - (n - 4) // 2) + (0 if br == "slc" else 1)

        def vec_dst(w, x):
            n = w - 1
            if x < 2:
                return "q", n % 2, x
            return ("k", n % 2, x - 2) if n < 4 else ("k", (n - 4) // 2, x - 2)

        def ple_bank(ng, tt):
            return tt if ng == 0 else (5, 6, 7, 0)[tt]

        def up_bank(u):
            return 4 * ((u + 1) % 2)

        cmp_bank = {"hidden": 2, "out": 4, "turned": 5}

        def cat(br):
            return {"cmp": 0, "slc": 1, "win": 2}[br]

        block = ctx.enter_context(nc.Block())

        @block.sync
        def _(sp):
            for tt in range(NT):
                sp.dma_start(xnat[:, tt, :], x_d[tt]).then_inc(x_in[tt], 16)
            def load_unit(w, kts):
                for kt in kts:
                    if w > 0:
                        sp.wait_ge(w_lo, KT * (w - 1) + kt + 1)
                    if w <= 4:
                        n = w - 1
                        src = win[kt][:, 0:1536].rearrange("p (a c) -> p a c", a=3)[:, :, n * P:(n + 1) * P]
                        sp.dma_start(raw[:, kt, :].rearrange("p (a c) -> p a c", a=3), src).then_inc(raw_in[kt], 16)
                    else:
                        n = w - 5
                        sp.dma_start(raw[:, kt, 0:P], win[kt][:, C_NQ + n * P:C_NQ + (n + 1) * P]).then_inc(raw_in[kt], 16)
                        if n % 2 == 0:
                            g = n // 2
                            src = win[kt][:, C_KS:C_KS + 512].rearrange("p (b v c) -> p v b c", b=2, v=2)
                            dst = raw[:, kt, P:P + 256].rearrange("p (v b c) -> p v b c", v=2, b=2)
                            for v in range(2):
                                sp.dma_start(dst[:, v], src[:, v, :, g * DH:(g + 1) * DH]).then_inc(raw_in[kt], 16)

            def load_strips(n):
                if n >= 2:
                    sp.wait_ge(biased, last_t[n - 2] + 1)
                for e in range(2):
                    h = 2 * n + e
                    src = bass.AP(tensor=skew_d.tensor, offset=h * P * PITCH + P - 1, ap=[[PITCH - 1, P], [1, S]])
                    sp.dma_start(strip[:, n % 2, e, :], src).then_inc(strip_in[n % 2], 16)

            def load_gate_weights(j):
                if j > 0:
                    sp.wait_ge(g_lo, j)
                sp.dma_start(graw[:, :, :], A["w_in"].rearrange("l (k p) n -> p (l k) n", p=P)[
                    :, :, C_MG + j * P:C_MG + (j + 1) * P]).then_inc(graw_in, 16)

            def spill_gate(j):
                sp.wait_ge(gate_tanh, j + 1)
                sp.dma_start(gate_d[j], gstage).then_inc(g_out, 16)

            def spill_y(n):
                sp.wait_ge(y_evac, n + 1)
                sp.dma_start(y_d[n], ystage).then_inc(y_out, 16)

            cw = A["conv_w"].rearrange("l w (r c) -> (l w r) c", c=P)
            blocks = [(rows[0:8, 0, :], A["attn_norm"].rearrange("l (r c) -> (l r) c", c=P)),
                      (rows[8:16, 0, :], A["ffn_norm"].rearrange("l (r c) -> (l r) c", c=P)),
                      (rows[CONVB:CONVB + 44, 0, :], A["conv_b"].rearrange("l (r c) -> (l r) c", c=P)),
                      (rows[POSK:POSK + 16, 0, :], A["cmp_pos_k"].rearrange("l (r a) c -> (l r) (a c)", a=2)),
                      (rows[POSV:POSV + 16, 0, :], A["cmp_pos_v"].rearrange("l (r a) c -> (l r) (a c)", a=2)),
                      (rows[:, 1, :], cw[0:P, :]), (rows[0:4, 2, :], cw[P:P + 4, :])]
            for dst, src in blocks:
                sp.dma_start(dst, src).then_inc(const_in, 16)
            wk = A["w_in"].rearrange("l (k p) n -> p (l k) n", p=P)
            for half in range(2):
                ks = slice(4 * half, 4 * half + 4)
                sp.dma_start(raw[:, ks, 0:256], wk[:, ks, C_KC:C_KC + 256]).then_inc(raw0_in[half], 16)
                sp.dma_start(raw[:, ks, 256:280], wk[:, ks, C_NG:C_NG + 24]).then_inc(raw0_in[half], 16)
            load_gate_weights(0)
            for v, nm in enumerate(("cmp_w2_k", "cmp_w2_v")):
                sp.dma_start(w2c[:, v, :], A[nm].rearrange("l k n -> (l k) n")).then_inc(w2c_in, 16)
            sp.wait_ge(x_turned, KT)
            sp.dma_start(w1k, w1_d[0]).then_inc(w1k_in, 16)
            load_unit(1, range(KT))
            sp.wait_ge(rtab_done, 1)
            for c0, part in ((0, rtab), (S, masked)):
                width = part.shape[1]
                dst = bass.AP(tensor=skew_d.tensor, offset=c0, ap=[[P * PITCH, 16], [PITCH, P], [1, width]])
                sp.dma_start(dst, part.unsqueeze(1).broadcast_to([16, P, width])).then_inc(skew_out, 16)
            load_gate_weights(1)
            spill_gate(0)
            load_unit(2, range(KT))
            sp.wait_ge(cmp_hidden, 1)
            sp.dma_start(w1k, w1_d[1]).then_inc(w1k_in, 16)
            load_gate_weights(2)
            sp.wait_ge(cmp_hidden, 2)
            sp.wait_ge(skew_out, 32)
            load_strips(0)
            spill_gate(1)
            load_unit(3, range(KT))
            load_gate_weights(3)
            for t in range(T):
                n, k = STEPS[t]["n"], STEPS[t]["k"]
                if k == 0 and n + 1 < NPAIR:
                    load_strips(n + 1)
                if k == 4 and n > 0:
                    spill_y(n - 1)
                if n + 4 < W_UNITS:
                    load_unit(n + 4, split_steps(n, k))
                for j, end in gate_end.items():
                    if t == end + 1:
                        spill_gate(j)
                        if j + 2 < NGATE:
                            load_gate_weights(j + 2)
            sp.wait_ge(y_out, 16 * 7)
            for n in range(7):
                sp.dma_start(ytmp[:, n, :], y_d[n]).then_inc(y_in, 16)

            def load_chunk(c):
                kind, a, kt = CHUNKS[c]
                if c >= RING:
                    sp.wait_ge(w2_lo, c - RING + 1)
                dst = raw2[:, c % RING, :]
                n0, n1 = a * 512, (a + 1) * 512
                src = {"bra": lambda: brm[kt][:, n0:n1], "brb": lambda: brn[kt][:, n0:n1], "wo": lambda: wo_d[kt][:, n0:n1],
                       "ple": lambda: pl_d[kt][:, n0:n1], "dn": lambda: dn_d[kt][:, n0:n1], "pg": lambda: pg_d[kt][:, n0:n1],
                       "up": lambda: up_d[kt][:, :, a * 256:(a + 1) * 256]}[kind]()
                if kind == "up":
                    dst = dst.rearrange("p (h c) -> p h c", h=2)
                sp.dma_start(dst, src).then_inc(raw2_in[c % RING], 16)

            def load_gates_a(mg):
                for m in range(4):
                    if mg:
                        sp.wait_ge(mT_lo, m + 1)
                    sp.dma_start(ga[:, m, :], gate_d[4 * mg + m]).then_inc(ga_in[m], 16)

            def load_gate_b(k):
                if k >= 2:
                    sp.wait_ge(br_sum, k - 1)
                sp.dma_start(gb[:, k % 2, :], gate_d[8 + k]).then_inc(gb_in[k % 2], 16)

            def load_x(tt):
                if tt:
                    sp.wait_ge(xs_tr, tt)
                sp.dma_start(xs, x_d[tt]).then_inc(xs_in, 16)

            sp.wait_ge(w_lo, KT * W_UNITS)
            for c in range(6):
                load_chunk(c)
            sp.wait_ge(g_lo, NGATE)
            for c in range(6, RING):
                load_chunk(c)
            sp.wait_ge(g_out, 16 * NGATE)
            sp.wait_ge(yt_lo, 7)
            load_x(0)
            for k in range(2):
                load_gate_b(k)
            load_gates_a(0)
            for c in range(RING, NC):
                load_chunk(c)
                if c == 15:
                    load_gate_b(2)
                    load_gate_b(3)
                if c == 18:
                    load_gates_a(1)
                    load_gate_b(4)
                    load_gate_b(5)
                if c == 19:
                    load_x(1)
                if c == 24:
                    load_gate_b(6)
                    load_gate_b(7)
                    load_x(2)
                if c == 26:
                    load_x(3)
                if c == 28:
                    sp.wait_ge(xs_tr, 4)
                    for tt in range(NT):
                        sp.dma_start(xs[:, tt * PLE:(tt + 1) * PLE], p_d[tt]).then_inc(xs_in, 16)
                if c in (47, 49):
                    for k in (range(0, 2) if c == 47 else range(2, 8)):
                        sp.wait_ge(pp_ev, k + 1)
                        sp.dma_start(pp_d[k], ppst[k % 4]).then_inc(pp_out[k % 4], 16)
            for k in range(4):
                sp.wait_ge(pp_out[k], 32)
            sp.wait_ge(x2_tr, 8)
            sp.wait_ge(x2_lo, 8)
            for k in range(4):
                sp.dma_start(ppb[:, k % 4, :], pp_d[k]).then_inc(pp_in, 16)
            for k in range(8):
                sp.wait_ge(o_done, k + 1)
                ng, tt = k // 4, k % 4
                sp.dma_start(o_d[tt][:, ng * 512:(ng + 1) * 512], x2n[:, tt, ng * 512:(ng + 1) * 512]).then_inc(o_out, 16)
                if k < 4:
                    sp.dma_start(ppb[:, k % 4, :], pp_d[k + 4]).then_inc(pp_in, 16)
            sp.wait_ge(o_out, 16 * 8)

        @block.gpsimd
        def _(pool):
            pool.memset(ident, 0.0).then_inc(pool_const, 1)
            pool.memset(ones, 1.0).then_inc(pool_const, 1)
            pool.memset(neg8[:, 0:1], -(DH ** -0.5)).then_inc(pool_const, 1)
            pool.wait_ge(pool_const, 1)
            pool.affine_select(out=ident, in_=ident, compare_op=ALU.not_equal, fill=1.0, base=0,
                               pattern=[[-1, P]], channel_multiplier=1).then_inc(pool_const, 1)
            for t_ in (Vh, Vl):
                pool.memset(t_[:, :, :, DH:2 * DH].bitcast(F32), 0.0).then_inc(pool_const, 1)
            for t_ in (VCh, VCl, KCh, KCl):
                pool.memset(t_.bitcast(F32), 0.0).then_inc(pool_const, 1)
            pool.memset(rtab, BIG).then_inc(pool_const, 1)
            pool.memset(masked, BIG).then_inc(pool_const, 1)
            pool.wait_ge(rbt_in, 16)
            pool.wait_ge(pool_const, 12)
            for b, (lo, hi) in enumerate(bucket_edges()):
                ins = pool.tensor_scalar(rtab[:, S - hi:S - lo], rbt[:, b:b + 1].broadcast_to([16, hi - lo]), -1.0, None, ALU.mult)
            ins.then_inc(rtab_done, 1)

            def split_unit(w, kts):
                c = ucols(w)
                for kt in kts:
                    pool.wait_ge(w_hi, KT * w + kt + 1)
                    pool.tensor_tensor(Wl[:, kt, 0:c], raw[:, kt, 0:c], Wh[:, kt, 0:c].bitcast(F32), ALU.subtract).then_inc(w_lo, 1)

            def split_gate(j):
                pool.wait_ge(g_hi, j + 1)
                pool.tensor_tensor(Gl, graw, Gh.bitcast(F32), ALU.subtract).then_inc(g_lo, 1)

            def v_low(w):
                n = w - 1
                pool.wait_ge(v_hi, w if n <= 4 else 6)
                if n < 4:
                    o = Vl[:, n % 2].rearrange("p t (a c) -> p t a c", a=3)[:, :, 0:3:2, :]
                    hi = Vh[:, n % 2].rearrange("p t (a c) -> p t a c", a=3)[:, :, 0:3:2, :]
                    i = qkv[:, :, 256:384].rearrange("p t (a c) -> p t a c", a=2)
                    pool.tensor_tensor(o, i, hi.bitcast(F32), ALU.subtract).then_inc(v_lo, 1)
                else:
                    for b in range(2):
                        s = vslot(n, ("slc", "win")[b])
                        for a in (0, 2):
                            ins = pool.tensor_tensor(Vl[:, s, :, a * DH:(a + 1) * DH], qkv[:, :, 256 + b * DH:256 + (b + 1) * DH],
                                                     Vh[:, s, :, a * DH:(a + 1) * DH].bitcast(F32), ALU.subtract)
                    ins.then_inc(v_lo, 1)

            def normalise(w):
                k = nvec(w)
                pool.wait_ge(rstd_done, w)
                for tt in range(2):
                    i = qkv[:, tt, 0:k * DH].rearrange("p (v c) -> p v c", v=k)
                    for a in range(2):
                        ins = pool.tensor_tensor(qn[:, tt, 0:k, a * DH:(a + 1) * DH], i,
                                                 rq[:, 4 * tt:4 * tt + k].unsqueeze(2).broadcast_to([P, k, DH]), ALU.mult)
                ins.then_inc(norm_done, 1)

            split_unit(0, range(KT))
            split_gate(0)
            pool.wait_ge(cst_done, 1)
            for tt in range(2):
                pool.wait_ge(qkv_done, tt + 1)
                for a in range(2):
                    ins = pool.tensor_copy(qn[:, tt, :, a * DH:(a + 1) * DH], qkv[:, tt, 0:256].rearrange("p (v c) -> p v c", v=4))
            ins.then_inc(norm_done, 1)
            split_unit(1, range(KT))
            split_gate(1)
            for kv in range(2):
                for g in range(2):
                    pool.wait_ge(tcmp_b, 2 * kv + g + 1)
                pool.wait_ge(tcmp_a, 2 * kv + 2)
                pool.wait_ge(bank_filled, use_index[("vec", 0, 3)] + 1)
                for half in range(2):
                    o = bp[:, kv, 0:992].rearrange("p (g l n) -> p g l n", g=2, l=16)
                    pos = cst[:, (POSV if kv else POSK) + 8 * half:(POSV if kv else POSK) + 8 * half + 8]
                    for g in range(2):
                        tk = tcmp[:, 2 * kv + g, 16 * half:16 * half + 496].rearrange("p (n l) -> p l n", l=16)[:, 0:16:2, :]
                        ins = pool.tensor_tensor(o[:, g, 8 * half:8 * half + 8, :], tk,
                                                 pos.unsqueeze(2).broadcast_to([P, 8, NCMP]), ALU.add)
                ins.then_inc(bp_done, 1)
            normalise(1)
            v_low(1)
            split_unit(2, range(KT))
            split_gate(2)
            for t in range(T):
                n, k, w = STEPS[t]["n"], STEPS[t]["k"], STEPS[t]["n"] + 2
                if n < NPAIR - 1 and k == norm_step(n):
                    normalise(w)
                if n < NPAIR - 1 and k == v_step(n) and w not in (6, 8):
                    v_low(w)
                split_unit(n + 3, split_steps(n, k))
                for j, end in gate_end.items():
                    if t == end + 1 and j + 1 < NGATE:
                        split_gate(j + 1)

            def y_low(n):
                pool.wait_ge(yt_hi, n + 1)
                pool.tensor_tensor(yTl[:, n, :], ytmp[:, n, :], yTh[:, n, :].bitcast(F32), ALU.subtract).then_inc(yt_lo, 1)

            def split_chunk(c):
                pool.wait_ge(w2_hi, c + 1)
                pool.tensor_tensor(W2l[:, c % RING, :], raw2[:, c % RING, :], W2h[:, c % RING, :].bitcast(F32),
                                   ALU.subtract).then_inc(w2_lo, 1)

            for c in range(NC):
                if c % 2 == 0 and c < RING:
                    for m in range(c, min(c + 2, 7)):
                        y_low(m)
                split_chunk(c)
                for mg in range(2):
                    for m in range(4):
                        if c == cidx[("wo", mg, KT - 1)] + 7:
                            kt = 4 * mg + m
                            pool.wait_ge(x1_sq, kt + 1)
                            if kt == 0:
                                pool.tensor_copy(sumsq, sqt[:, 0, :]).then_inc(ssq_done, 1)
                            else:
                                pool.wait_ge(ssq_done, kt)
                                pool.tensor_tensor(sumsq, sumsq, sqt[:, kt % 2, :], ALU.add).then_inc(ssq_done, 1)
                if c == cidx[("ple", 1, 0)] + 7:
                    for kt in range(KT):
                        pool.wait_ge(h2_hi, kt + 1)
                        pool.tensor_tensor(h2l[:, kt, :], hst[:, kt % 2, :], h2h[:, kt, :].bitcast(F32), ALU.subtract).then_inc(h2_lo, 1)
                for mg in range(2):
                    if c == cidx[("dn", mg, NF - 1)] + 7:
                        for m in range(4):
                            kt = 4 * mg + m
                            pool.wait_ge(x2_hi, kt + 1)
                            pool.tensor_tensor(h2l[:, kt, :], x1T[:, kt, :], h2h[:, kt, :].bitcast(F32), ALU.subtract).then_inc(x2_lo, 1)

        @block.scalar
        def _(act):
            for r0, n, src in ((GQ, 1, A["moba_q_gain"]), (GQ + 1, 1, A["moba_k_gain"]), (GQ + 2, 1, A["nsa_q_gain"]),
                               (GQ + 3, 3, A["nsa_k_gain"].rearrange("l b c -> (l b) c"))):
                act.dma_start(rows[r0:r0 + n, 0, :].rearrange("r (a c) -> r a c", a=2),
                              src.unsqueeze(1).broadcast_to([n, 2, DH])).then_inc(const_in, 16)
            act.dma_start(rbt, A["rel_bias"]).then_inc(rbt_in, 16)
            for tt in range(NT):
                act.wait_ge(x_in[tt], 16)
                nc.scalar.activation(R[:, 8192 + tt * D:8192 + (tt + 1) * D], xnat[:, tt, :], ACT.Square, accum_out=ssx[:, tt:tt + 1]).then_inc(x_sq, 1)

            def take_proj(w, tt):
                r = use_index[("proj", w, tt)]
                act.wait_ge(bank_filled, r + 1)
                if w == 1:
                    act.wait_ge(norm_done, 1)
                    act.wait_ge(norm_dve, 1)
                    act.wait_ge(gsig_tanh, 1)
                if w > 1 and tt == 0:
                    act.wait_ge(norm_dve, w)
                    act.wait_ge(norm_done, w)
                    if w - 1 not in (6, 8):
                        act.wait_ge(v_lo, min(w - 1, 5) if w - 1 < 7 else 6)
                nc.scalar.activation(qkv[:, tt, 0:ucols(w)], PS[:, r % 2, 0:ucols(w)], ACT.Copy).then_inc(qkv_done, 1)

            def squares(w):
                k = nvec(w)
                act.wait_ge(qkv_done, 4 * w + 4)
                if w == 1:
                    act.wait_ge(cmp_hidden, 1)
                else:
                    act.wait_ge(bank_filled, use_index[("vec", w - 1, nvec(w - 1) - 1)] + 1)
                nc.scalar.activation(sq[:, :, 0:k * DH], qkv[:, :, 0:k * DH], ACT.Square).then_inc(sq_done, 1)

            def v_high(w):
                n = w - 1
                act.wait_ge(qkv_done, 4 * w + 4)
                if n < 4:
                    if n >= 2:
                        act.wait_ge(pv_done, 2 * n - 2)
                    o = Vh[:, n % 2].rearrange("p t (a c) -> p t a c", a=3)[:, :, 0:3:2, :]
                    nc.scalar.activation(o, qkv[:, :, 256:384].rearrange("p t (a c) -> p t a c", a=2), ACT.Copy).then_inc(v_hi, 1)
                else:
                    if n == 6:
                        act.wait_ge(pv_done, 8)
                    for b in range(2):
                        s = vslot(n, ("slc", "win")[b])
                        for a in (0, 2):
                            ins = nc.scalar.activation(Vh[:, s, :, a * DH:(a + 1) * DH], qkv[:, :, 256 + b * DH:256 + (b + 1) * DH], ACT.Copy)
                    ins.then_inc(v_hi, 1)

            def vec_high(w, x):
                n = w - 1
                r = use_index[("vec", w, x)]
                act.wait_ge(bank_filled, r + 1)
                kind, s, e = vec_dst(w, x)
                if kind == "q":
                    if n >= 2:
                        act.wait_ge(score, last_t[n - 2] + 1)
                    g = cst[:, GQ + (0 if n < 4 else 2):GQ + (0 if n < 4 else 2) + 1]
                    dst = QQ[:, s, e, :]
                else:
                    if n >= 2:
                        act.wait_ge(score, last_t[min(n - 2, 3)] + 1)
                    g = cst[:, GQ + 1:GQ + 2] if n < 4 else cst[:, GQ + 4 + e:GQ + 5 + e]
                    dst = Kh[:, s, e, :]
                nc.scalar.activation(dst, PS[:, r % 2, :], ACT.Copy, scale=g).then_inc(vec_hi, 1)

            def exp(t):
                s = STEPS[t]
                act.wait_ge(biased, t + 1)
                if s["br"] == "cmp":
                    nc.scalar.activation(prob[:, t % 4, 0:P], sc_c.rearrange("p a b -> p (a b)"), ACT.Exp, scale=-1.0).then_inc(exped, 1)
                else:
                    nk = P * (s["i"] + 1)
                    nc.scalar.activation(prob[:, t % 4, 0:nk], prob[:, t % 4, 0:nk], ACT.Exp, bias=mneg[:, t % 4:t % 4 + 1],
                                         scale=-1.0, accum_out=rsum[:, t % 4:t % 4 + 1]).then_inc(exped, 1)

            def pt_high(t):
                s = STEPS[t]
                act.wait_ge(turned, t + 1)
                if s["u"] >= 2:
                    act.wait_ge(pv_done, s["u"] - 1)
                if s["br"] == "cmp":
                    nc.scalar.activation(PTh[0:32, s["u"] % 2, 0, :], PS[0:32, 4 + t % 2, :], ACT.Copy).then_inc(pt_hi, 1)
                else:
                    i = s["i"]
                    nc.scalar.activation(PTh[:, s["u"] % 2, 0:i + 1, P * i:P * (i + 1)],
                                         PS[:, 4 + t % 2, 0:P * (i + 1)].rearrange("p (j q) -> p j q", j=i + 1), ACT.Copy).then_inc(pt_hi, 1)

            def take_gate(j):
                act.wait_ge(gate_filled, j + 1)
                if j > 0:
                    act.wait_ge(g_out, 16 * j)
                nc.scalar.activation(gstage, PS[:, 7, :], ACT.Tanh, scale=0.5).then_inc(gate_tanh, 1)

            def split_chunk(c):
                act.wait_ge(raw2_in[c % RING], 16 * (c // RING + 1))
                if c >= RING:
                    act.wait_ge(chunk_done, c - RING + 1)
                if c == 0:
                    act.wait_ge(gate_filled, NGATE)
                    act.wait_ge(bank_filled, len(USES))
                nc.scalar.activation(W2h[:, c % RING, :], raw2[:, c % RING, :], ACT.Copy).then_inc(w2_hi, 1)

            act.wait_ge(cst_turned, 3)
            nc.scalar.activation(cst[:, 0:CONVW + P + 4], PS[:, 0, 0:CONVW + P + 4], ACT.Copy).then_inc(cst_done, 1)
            act.wait_ge(cst_done, 1)
            for kt in range(KT):
                act.wait_ge(x_turned, kt + 1)
                nc.scalar.activation(hTh[:, kt, :], PS[:, turn_bank(kt), :], ACT.Copy, scale=cst[:, kt:kt + 1]).then_inc(hT_hi, 1)
            for tt in range(NT):
                take_proj(0, tt)
            act.wait_ge(qkv_done, 4)
            nc.scalar.activation(gsig, qkv[:, :, 256:280], ACT.Tanh, scale=0.5).then_inc(gsig_tanh, 1)
            for x in range(4):
                r = use_index[("vec", 0, x)]
                act.wait_ge(bank_filled, r + 1)
                nc.scalar.activation(tcmp[0:DH, x, :], PS[0:DH, r % 2, :], ACT.Copy).then_inc(tcmp_a, 1)
            take_gate(0)
            for tt in range(NT):
                take_proj(1, tt)
            v_high(1)
            for kv in range(2):
                act.wait_ge(cmp_hidden, kv + 1)
                nc.scalar.activation(hid[:, kv * 62:kv * 62 + 62], PS[:, cmp_bank["hidden"] + kv, 0:62], ACT.Gelu_apprx_tanh).then_inc(hid_done, 1)
                if kv == 0:
                    squares(1)
                    take_gate(1)
            for x in range(4):
                vec_high(1, x)
            act.wait_ge(cmp_out, 1)
            vps = PS[0:NCMP, cmp_bank["out"], P:2 * P].rearrange("p (g c) -> p g c", g=2)
            act.wait_ge(pool_const, 12)
            act.wait_ge(kcn_done, 1)
            for g in range(2):
                for a in (0, 2):
                    ins = nc.scalar.activation(VCh[0:NCMP, g, a * DH:(a + 1) * DH], vps[:, g, :], ACT.Copy)
            ins.then_inc(vc_hi, 1)
            take_proj(2, 0)
            act.wait_ge(cmp_turned, 1)
            for g in range(2):
                ins = nc.scalar.activation(KCh[:, g, 0:NCMP], PS[:, cmp_bank["turned"], 32 * g:32 * g + NCMP], ACT.Copy, scale=cst[:, GQ + 3:GQ + 4])
            ins.then_inc(kc_hi, 1)
            for t in range(T + LAG):
                n, k, w = (STEPS[t]["n"], STEPS[t]["k"], STEPS[t]["n"] + 2) if t < T else (NPAIR, 0, 0)
                if proj_end(t):
                    take_proj(*proj_end(t))
                for j, end in gate_end.items():
                    if t == end + 1:
                        take_gate(j)
                if t < T:
                    exp(t)
                if n < NPAIR - 1:
                    if k == square_step(n):
                        squares(w)
                    if k == v_step(n) and w not in (6, 8):
                        v_high(w)
                    for x in vec_steps(n, k):
                        vec_high(w, x)
                if LAG <= t:
                    pt_high(t - LAG)
                if t == T - 3:
                    act.wait_ge(gate_filled, NGATE)
                    act.wait_ge(y_in, 16 * 7)
                if T - 3 <= t < T + 1:
                    for m in range(2 * (t - T + 3), min(2 * (t - T + 3) + 2, 7)):
                        nc.scalar.activation(yTh[:, m, :], ytmp[:, m, :], ACT.Copy).then_inc(yt_hi, 1)
                    for c in range(2 * (t - T + 3), 2 * (t - T + 3) + 2):
                        split_chunk(c)

            act.wait_ge(pv_done, STEPS[-1]["u"] + 1)
            nc.scalar.activation(yTh[:, 7, :], PS[:, 6, :], ACT.Copy).then_inc(yt_hi, 1)

            def take_x(tt):
                for half in range(2):
                    b = (4 + 2 * (tt % 2)) + half
                    act.wait_ge(xs_tr, tt + 1)
                    nc.scalar.activation(x1T[:, 4 * half:4 * half + 4, P * tt:P * (tt + 1)],
                                         PS[:, b, :].rearrange("p (k q) -> p k q", k=4), ACT.Copy).then_inc(xT_done, 1)

            def conv_bias(f):
                u, q = f // 2, f % 2
                act.wait_ge(chunk_done, cidx[("up", u, KT - 1)] + 1)
                for half, (dst, sm) in enumerate(((ya, ya_bias), (yl, yl_bias))):
                    b = up_bank(u) + 2 * half + q
                    if f == 0 and half == 0:
                        act.wait_ge(h2_lo, KT)
                        act.wait_ge(h2_f, KT)
                        for k in range(4):
                            act.wait_ge(pp_out[k], 32)
                    if f >= 2:
                        act.wait_ge(gT_lo, f - 1)
                    col = half * NF + f
                    nc.scalar.activation(dst[:, f % 2, :], PS[:, b, :], ACT.Identity, scale=cst[:, CONVW + 88 + col:CONVW + 89 + col],
                                         bias=cst[:, CONVB + col:CONVB + col + 1]).then_inc(sm, 1)

            def gelu(f):
                act.wait_ge(ya_conv, f + 1)
                nc.scalar.activation(ya[:, f % 2, :], ya[:, f % 2, :], ACT.Gelu_apprx_tanh).then_inc(gelu_done, 1)

            def g_high(f):
                act.wait_ge(glu_done, f + 1)
                if f == 0:
                    act.wait_ge(chunk_done, cidx[("ple", 1, 1)] + 1)
                nc.scalar.activation(gTh[:, f, :], ya[:, f % 2, :], ACT.Copy).then_inc(gT_hi, 1)

            def take_pp(k):
                act.wait_ge(chunk_done, cidx[("ple", k // 4, 1)] + 1)
                if k == 2:
                    act.wait_ge(ssq_done, KT)
                if k >= 4:
                    act.wait_ge(pp_out[k % 4], 16)
                nc.scalar.activation(ppst[k % 4], PS[:, ple_bank(k // 4, k % 4), :], ACT.Copy, scale=0.5).then_inc(pp_ev, 1)

            for c in range(RING, NC + 10):
                if c == 11 + RING:
                    take_x(0)
                e = c - RING
                kind, a, kt = CHUNKS[e] if e < NC else (None, 0, 0)
                if kind == "brb" and kt == 3:
                    for m in range(4):
                        i = 4 * a + m
                        act.wait_ge(br_sum, i + 1)
                        nc.scalar.activation(mTh[:, i, :], ga[:, m, :], ACT.Copy, scale=0.5).then_inc(mT_hi, 1)
                if kind == "wo" and a == 0 and kt in (2, 4, 5):
                    take_x({2: 1, 4: 2, 5: 3}[kt])
                if kind == "wo" and a == 0 and kt == 7:
                    for k in range(2):
                        act.wait_ge(p_tr, k + 1)
                        nc.scalar.activation(pTh[:, k, :], PS[:, 4 + k, :], ACT.Copy).then_inc(pT_hi, 1)
                if kind == "wo" and kt == KT - 1:
                    for m in range(4):
                        i = 4 * a + m
                        act.wait_ge(x1_done, i + 1)
                        if i >= 2:
                            act.wait_ge(ssq_done, i - 1)
                        nc.scalar.activation(sqt[:, i % 2, :], x1T[:, i, :], ACT.Square).then_inc(x1_sq, 1)
                if kind == "ple" and (a, kt) == (0, 1):
                    take_pp(0)
                    take_pp(1)
                if kind == "ple" and (a, kt) == (1, 0):
                    act.wait_ge(bc_mm, 1)
                    nc.scalar.activation(rbc, PS[:, 4, :], ACT.Copy).then_inc(bc_done, 1)
                    for i in range(KT):
                        act.wait_ge(h2_f, i + 1)
                        nc.scalar.activation(h2h[:, i, :], hst[:, i % 2, :], ACT.Copy).then_inc(h2_hi, 1)
                if kind == "ple" and (a, kt) == (1, 1):
                    for k in range(2, 8):
                        take_pp(k)
                if kind == "up" and kt == KT - 1:
                    conv_bias(2 * a)
                    conv_bias(2 * a + 1)
                if (kind == "up" and kt == 0 and a > 0) or (kind == "dn" and a == 0 and kt == 0):
                    u = a - 1 if kind == "up" else NF // 2 - 1
                    gelu(2 * u)
                    gelu(2 * u + 1)
                if (kind == "up" and kt == 1 and a > 0) or (kind == "dn" and a == 0 and kt == 1):
                    u = a - 1 if kind == "up" else NF // 2 - 1
                    g_high(2 * u)
                    g_high(2 * u + 1)
                if kind == "dn" and kt == NF - 1:
                    for m in range(4):
                        i = 4 * a + m
                        act.wait_ge(x2_done, i + 1)
                        nc.scalar.activation(h2h[:, i, :], x1T[:, i, :], ACT.Copy).then_inc(x2_hi, 1)
                if kind == "pg" and kt == KT - 1:
                    for tt in range(NT):
                        k = 4 * a + tt
                        act.wait_ge(chunk_done, e + 1)
                        if k == 0:
                            act.wait_ge(x2_tr, 8)
                            act.wait_ge(x2_lo, 8)
                        if k >= 4:
                            act.wait_ge(o_done, k - 3)
                        nc.scalar.activation(thb[:, k % 4, :], PS[:, 4 * a + tt, :], ACT.Tanh, scale=0.5).then_inc(th_done, 1)
                if c < NC:
                    split_chunk(c)

        @block.vector
        def _(dve):
            nch = [0]

            def link(ins):
                nch[0] += 1
                ins.then_inc(chain, 1)
                dve.wait_ge(chain, nch[0])

            def rsqrt(dst, src, inv_n, wdt, parts=P, done=None):
                v = st[0:parts, 40:40 + wdt]
                y = dst
                a = st[0:parts, 60:60 + wdt]
                link(nc.vector.tensor_scalar(v, src, inv_n, EPS, ALU.mult, ALU.add))
                link(nc.vector.tensor_scalar(a.bitcast(I32), v.bitcast(I32), 1, None, ALU.logical_shift_right))
                link(nc.vector.tensor_scalar(y.bitcast(I32), a.bitcast(I32), -1.0, float(0x5F3759DF), ALU.mult, ALU.add))
                for it in range(3):
                    link(nc.vector.tensor_tensor(a, y, y, ALU.mult))
                    link(nc.vector.scalar_tensor_tensor(out=a, in0=a, scalar=-0.5, in1=v, op0=ALU.mult, op1=ALU.mult))
                    ins = nc.vector.scalar_tensor_tensor(out=y, in0=a, scalar=1.5, in1=y, op0=ALU.add, op1=ALU.mult)
                    if it == 2 and done is not None:
                        ins.then_inc(done, 1)
                    else:
                        link(ins)

            def split_unit(w, kts):
                c = ucols(w)
                for kt in kts:
                    if w == 0:
                        dve.wait_ge(raw0_in[kt // 4], 32)
                    else:
                        dve.wait_ge(raw_in[kt], 16 * sum(udmas(v) for v in range(w + 1)))
                    if w > 0:
                        if kt < KT - 1:
                            dve.wait_ge(w_used, (KT - 1) * (w - 1) + kt + 1)
                        else:
                            dve.wait_ge(bank_filled, use_index[("proj", w - 1, NT - 1)] + 1)
                    else:
                        dve.wait_ge(x_sq, NT)
                    nc.vector.tensor_copy(Wh[:, kt, 0:c], raw[:, kt, 0:c]).then_inc(w_hi, 1)

            def split_gate(j):
                dve.wait_ge(graw_in, 16 * (j + 1))
                if j > 0:
                    dve.wait_ge(gate_filled, j)
                nc.vector.tensor_copy(Gh, graw).then_inc(g_hi, 1)

            dve.wait_ge(x_sq, NT)
            rsqrt(st[:, 80:84], ssx, 1.0 / D, 4)
            for tt in range(NT):
                nc.vector.tensor_scalar(xnat[:, tt, :], xnat[:, tt, :], st[:, 80 + tt:81 + tt], None, ALU.mult).then_inc(h_nat, 1)
            split_unit(0, range(KT))
            dve.wait_ge(cst_done, 1)
            dve.wait_ge(pool_const, 4)
            for c in (GQ, GQ + 2):
                link(nc.vector.tensor_scalar(cst[:, c:c + 1], cst[:, c:c + 1], -(DH ** -0.5), None, ALU.mult))
            for kt in range(KT):
                dve.wait_ge(hT_hi, kt + 1)
                nc.vector.scalar_tensor_tensor(out=hTl[:, kt, :], in0=PS[:, turn_bank(kt), :], scalar=cst[:, kt:kt + 1],
                                               in1=hTh[:, kt, :].bitcast(F32), op0=ALU.mult, op1=ALU.subtract).then_inc(hT_lo, 1)
            split_gate(0)
            split_unit(1, range(4))
            for tt in range(2, NT):
                dve.wait_ge(qkv_done, tt + 1)
                for a in range(2):
                    ins = nc.vector.tensor_copy(qn[:, tt, :, a * DH:(a + 1) * DH], qkv[:, tt, 0:256].rearrange("p (v c) -> p v c", v=4))
            ins.then_inc(norm_dve, 1)
            split_unit(1, range(4, KT))
            dve.wait_ge(gsig_tanh, 1)
            nc.vector.tensor_scalar(gsig, gsig, 0.5, 0.5, ALU.mult, ALU.add).then_inc(gsig_done, 1)
            for x in range(4):
                r = use_index[("vec", 0, x)]
                dve.wait_ge(tcmp_a, x + 1)
                nc.vector.tensor_copy(tcmp[DH:P, x, 0:S - 1], PS[DH:P, r % 2, 1:S]).then_inc(tcmp_b, 1)
            split_gate(1)
            def rstd(w):
                k = nvec(w)
                dve.wait_ge(sq_done, w)
                if w > 1:
                    dve.wait_ge(norm_done, w)
                    dve.wait_ge(norm_dve, w)
                link(nc.vector.reduce_sum(ss[:, 0:4 * k].rearrange("p (t v) -> p t v", t=NT), sq[:, :, 0:k * DH].rearrange("p t (v c) -> p t v c", v=k), AX))
                if k == 4:
                    rsqrt(rq[:, 0:16], ss[:, 0:16], 1.0 / DH, 16, done=rstd_done)
                else:
                    rsqrt(rq[:, 20:28], ss[:, 0:8], 1.0 / DH, 8)
                    nc.vector.tensor_copy(rq[:, 0:16].rearrange("p (t v) -> p t v", t=NT)[:, :, 0:2],
                                          rq[:, 20:28].rearrange("p (t v) -> p t v", t=NT)).then_inc(rstd_done, 1)

            def normalise(w):
                k = nvec(w)
                dve.wait_ge(rstd_done, w)
                if w == 1:
                    dve.wait_ge(cmp_hidden, 2)
                for tt in range(2, NT):
                    i = qkv[:, tt, 0:k * DH].rearrange("p (v c) -> p v c", v=k)
                    for a in range(2):
                        ins = nc.vector.tensor_tensor(qn[:, tt, 0:k, a * DH:(a + 1) * DH], i,
                                                      rq[:, 4 * tt:4 * tt + k].unsqueeze(2).broadcast_to([P, k, DH]), ALU.mult)
                ins.then_inc(norm_dve, 1)

            def vec_low(w, x):
                n = w - 1
                r = use_index[("vec", w, x)]
                dve.wait_ge(vec_hi, vec_base[w] + x + 1 - 4)
                kind, s, e = vec_dst(w, x)
                if kind == "q":
                    c = GQ + (0 if n < 4 else 2)
                    nc.vector.scalar_tensor_tensor(out=QQ[DH:P, s, e, :], in0=PS[DH:P, r % 2, :], scalar=cst[DH:P, c:c + 1],
                                                   in1=QQ[DH:P, s, e, :].bitcast(F32), op0=ALU.mult, op1=ALU.subtract).then_inc(vec_lo, 1)
                else:
                    c = GQ + 1 if n < 4 else GQ + 4 + e
                    nc.vector.scalar_tensor_tensor(out=Kl[:, s, e, :], in0=PS[:, r % 2, :], scalar=cst[:, c:c + 1],
                                                   in1=Kh[:, s, e, :].bitcast(F32), op0=ALU.mult, op1=ALU.subtract).then_inc(vec_lo, 1)

            def bias(t):
                s = STEPS[t]
                n, e, i = s["n"], s["e"], s["i"]
                dve.wait_ge(score, t + 1)
                if t >= 4:
                    dve.wait_ge(turned, t - 3)
                if s["k"] == 0:
                    dve.wait_ge(strip_in[n % 2], 32 * (n // 2 + 1))
                if s["br"] != "cmp":
                    nk = P * (i + 1)
                    nc.vector.tensor_tensor_reduce(out=prob[:, t % 4, 0:nk], in0=PS[:, 2 + t % 2, 0:nk], in1=strip[:, n % 2, e, S - nk:S],
                                                   scale=1.0, scalar=3e38, op0=ALU.add, op1=ALU.min,
                                                   accum_out=mneg[:, t % 4:t % 4 + 1]).then_inc(biased, 1)
                else:
                    link(nc.vector.memset(sc_c, BIG))
                    for q in range(NT):
                        c0 = P * (NT - 1 - q) + CMP_LEN - 1
                        m = 7 + 8 * q
                        ins = nc.vector.tensor_tensor_reduce(out=sc_c[:, q, 0:m], in0=PS[:, 2 + t % 2, 32 * q:32 * q + m],
                                                             in1=strip[:, n % 2, e, c0:c0 + 16 * (m - 1) + 1:16], scale=1.0, scalar=1e29,
                                                             op0=ALU.add, op1=ALU.min, accum_out=mneg_c[:, q:q + 1])
                    link(ins)
                    nc.vector.tensor_tensor(sc_c, sc_c, mneg_c.unsqueeze(2).broadcast_to([P, NT, 32]), ALU.subtract).then_inc(biased, 1)

            def scale(t):
                s = STEPS[t]
                dve.wait_ge(exped, t + 1)
                n, e, i = s["n"], s["e"], s["i"]
                if s["br"] == "own":
                    nk = P * (i + 1)
                    link(nc.vector.reciprocal(rsum[:, t % 4:t % 4 + 1], rsum[:, t % 4:t % 4 + 1]))
                    nc.vector.tensor_scalar(prob[:, t % 4, 0:nk], prob[:, t % 4, 0:nk], rsum[:, t % 4:t % 4 + 1], None, ALU.mult).then_inc(scaled, 1)
                elif s["br"] != "cmp":
                    nk = P * (i + 1)
                    h = cat(s["br"]) * HN + 2 * (n - 4) + e
                    link(nc.vector.reciprocal(rsum[:, t % 4:t % 4 + 1], rsum[:, t % 4:t % 4 + 1]))
                    nc.vector.tensor_scalar(prob[:, t % 4, 0:nk], prob[:, t % 4, 0:nk], rsum[:, t % 4:t % 4 + 1], gsig[:, i, h:h + 1],
                                            ALU.mult, ALU.mult).then_inc(scaled, 1)
                else:
                    h = 2 * (n - 4) + e
                    pc = prob[:, t % 4, 0:P].rearrange("p (a b) -> p a b", a=NT)
                    link(nc.vector.reduce_sum(rsum_c, pc, AX))
                    link(nc.vector.tensor_scalar(rsum_c, rsum_c, 1e-30, None, ALU.max))
                    link(nc.vector.reciprocal(rsum_c, rsum_c))
                    link(nc.vector.tensor_tensor(rsum_c, rsum_c, gsig[:, :, h], ALU.mult))
                    nc.vector.tensor_tensor(pc, pc, rsum_c.unsqueeze(2).broadcast_to([P, NT, 32]), ALU.mult).then_inc(scaled, 1)

            def pt_low(t):
                s = STEPS[t]
                dve.wait_ge(pt_hi, t + 1)
                if s["br"] == "cmp":
                    nc.vector.tensor_tensor(PTl[0:32, s["u"] % 2, 0, :], PS[0:32, 4 + t % 2, :], PTh[0:32, s["u"] % 2, 0, :].bitcast(F32),
                                            ALU.subtract).then_inc(pt_lo, 1)
                else:
                    i = s["i"]
                    nc.vector.tensor_tensor(PTl[:, s["u"] % 2, 0:i + 1, P * i:P * (i + 1)],
                                            PS[:, 4 + t % 2, 0:P * (i + 1)].rearrange("p (j q) -> p j q", j=i + 1),
                                            PTh[:, s["u"] % 2, 0:i + 1, P * i:P * (i + 1)].bitcast(F32), ALU.subtract).then_inc(pt_lo, 1)

            rstd(1)
            normalise(1)
            split_unit(2, range(KT))
            split_gate(2)
            for x in range(4):
                vec_low(1, x)
            dve.wait_ge(cmp_out, 1)
            kps = PS[0:NCMP, cmp_bank["out"], 0:P]
            vps = PS[0:NCMP, cmp_bank["out"], P:2 * P].rearrange("p (g c) -> p g c", g=2)
            dve.wait_ge(skew_out, 32)
            link(nc.vector.tensor_copy(F[0:NCMP, 13600:13728], kps))
            ksb = F[0:NCMP, 13600:13728].rearrange("p (g c) -> p g c", g=2)
            link(nc.vector.tensor_tensor(kcn[0:NCMP, :, 0:DH], ksb, ksb, ALU.mult))
            link(nc.vector.reduce_sum(s_k[0:NCMP, :], kcn[0:NCMP, :, 0:DH], AX))
            rsqrt(st[0:NCMP, 84:86], s_k[0:NCMP, :], 1.0 / DH, 2, NCMP)
            for a in range(2):
                ins = nc.vector.tensor_tensor(kcn[0:NCMP, :, a * DH:(a + 1) * DH], ksb,
                                              st[0:NCMP, 84:86].unsqueeze(2).broadcast_to([NCMP, 2, DH]), ALU.mult)
                if a == 0:
                    link(ins)
            ins.then_inc(kcn_done, 1)
            dve.wait_ge(vc_hi, 1)
            for g in range(2):
                for a in (0, 2):
                    ins = nc.vector.tensor_tensor(VCl[0:NCMP, g, a * DH:(a + 1) * DH], vps[:, g, :],
                                                  VCh[0:NCMP, g, a * DH:(a + 1) * DH].bitcast(F32), ALU.subtract)
            ins.then_inc(vc_lo, 1)
            dve.wait_ge(kc_hi, 1)
            for g in range(2):
                ins = nc.vector.scalar_tensor_tensor(out=KCl[:, g, 0:NCMP], in0=PS[:, cmp_bank["turned"], 32 * g:32 * g + NCMP], scalar=cst[:, GQ + 3:GQ + 4],
                                                     in1=KCh[:, g, 0:NCMP].bitcast(F32), op0=ALU.mult, op1=ALU.subtract)
            ins.then_inc(kc_lo, 1)

            for t in range(T + LAG + 1):
                n, k, w = (STEPS[t]["n"], STEPS[t]["k"], STEPS[t]["n"] + 2) if t < T else (NPAIR, 0, 0)
                for x in vec_steps(n, k - 1) if t < T else ():
                    vec_low(w, x)
                if t < T:
                    bias(t)
                if 1 <= t <= T:
                    scale(t - 1)
                if t >= LAG + 1:
                    pt_low(t - LAG - 1)
                if t < T:
                    if n < NPAIR - 1 and k == norm_step(n):
                        rstd(w)
                        normalise(w)
                    split_unit(n + 3, split_steps(n, k))
                    for j, end in gate_end.items():
                        if t == end + 1 and j + 1 < NGATE:
                            split_gate(j + 1)
                    if n > 0 and k == VLAG - 1:
                        dve.wait_ge(pv_done, STEPS[last_t[n - 1]]["u"] + 1)
                        if n > 1:
                            dve.wait_ge(y_out, 16 * (n - 1))
                        else:
                            dve.wait_ge(cmp_hidden, 2)
                        nc.vector.tensor_copy(ystage, PS[:, 6, :]).then_inc(y_evac, 1)
            dve.wait_ge(yt_hi, 8)
            nc.vector.tensor_tensor(yTl[:, 7, :], PS[:, 6, :], yTh[:, 7, :].bitcast(F32), ALU.subtract).then_inc(y_evac, 1)

            for mg in range(2):
                for m in range(4):
                    dve.wait_ge(chunk_done, cidx[("bra", mg, 3)] + 1)
                    dve.wait_ge(ga_in[m], 16 * (mg + 1))
                    nc.vector.scalar_tensor_tensor(out=ga[:, m, :], in0=ga[:, m, :], scalar=1.0, in1=PS[:, m, :],
                                                   op0=ALU.add, op1=ALU.mult).then_inc(brA_done, 1)
                for m in range(4):
                    i = 4 * mg + m
                    dve.wait_ge(chunk_done, cidx[("brb", mg, 3)] + 1)
                    dve.wait_ge(gb_in[i % 2], 16 * (i // 2 + 1))
                    dve.wait_ge(brA_done, i + 1)
                    nc.vector.scalar_tensor_tensor(out=gb[:, i % 2, :], in0=gb[:, i % 2, :], scalar=1.0, in1=PS[:, 4 + m, :],
                                                   op0=ALU.add, op1=ALU.mult).then_inc(brB_done, 1)
                    dve.wait_ge(brB_done, i + 1)
                    nc.vector.tensor_tensor(ga[:, m, :], ga[:, m, :], gb[:, i % 2, :], ALU.add).then_inc(br_sum, 1)
                for m in range(4):
                    i = 4 * mg + m
                    dve.wait_ge(mT_hi, i + 1)
                    nc.vector.scalar_tensor_tensor(out=mTl[:, i, :], in0=ga[:, m, :], scalar=0.5, in1=mTh[:, i, :].bitcast(F32),
                                                   op0=ALU.mult, op1=ALU.subtract).then_inc(mT_lo, 1)
            for k in range(2):
                dve.wait_ge(pT_hi, k + 1)
                nc.vector.tensor_tensor(pTl[:, k, :], PS[:, 4 + k, :], pTh[:, k, :].bitcast(F32), ALU.subtract).then_inc(pT_lo, 1)
            dve.wait_ge(xT_done, 8)
            for mg in range(2):
                for m in range(4):
                    i = 4 * mg + m
                    dve.wait_ge(chunk_done, cidx[("wo", mg, KT - 1)] + 1)
                    nc.vector.tensor_tensor(x1T[:, i, :], PS[:, i, :], x1T[:, i, :], ALU.add).then_inc(x1_done, 1)
            dve.wait_ge(tok_sum, 1)
            rsqrt(st[:, 80:84], PS[:, 4, 0:4], 1.0 / D, 4)
            for tt in range(NT):
                ins = nc.vector.tensor_scalar(rdiag[:, tt * P:(tt + 1) * P], ident, st[:, 80 + tt:81 + tt], None, ALU.mult)
            ins.then_inc(rdiag_done, 1)
            dve.wait_ge(bc_done, 1)
            for i in range(KT):
                if i >= 2:
                    dve.wait_ge(h2_lo, i - 1)
                nc.vector.scalar_tensor_tensor(out=hst[:, i % 2, :], in0=x1T[:, i, :], scalar=cst[:, 8 + i:9 + i], in1=rbc,
                                               op0=ALU.mult, op1=ALU.mult).then_inc(h2_f, 1)
            for u in range(NF // 2):
                for q in range(2):
                    f = 2 * u + q
                    for half, (dst, sb_, sm) in enumerate(((ya, ya_bias, ya_conv), (yl, yl_bias, yl_conv))):
                        b = up_bank(u) + 2 * half + q
                        col = half * NF + f
                        dve.wait_ge(sb_, f + 1)
                        link(nc.vector.scalar_tensor_tensor(out=dst[:, f % 2, 1:S], in0=PS[:, b, 0:S - 1], scalar=cst[:, CONVW + 44 + col:CONVW + 45 + col],
                                                            in1=dst[:, f % 2, 1:S], op0=ALU.mult, op1=ALU.add))
                        nc.vector.scalar_tensor_tensor(out=dst[:, f % 2, 2:S], in0=PS[:, b, 0:S - 2], scalar=cst[:, CONVW + col:CONVW + 1 + col],
                                                       in1=dst[:, f % 2, 2:S], op0=ALU.mult, op1=ALU.add).then_inc(sm, 1)
                for q in range(2):
                    f = 2 * u + q
                    dve.wait_ge(gelu_done, f + 1)
                    dve.wait_ge(yl_conv, f + 1)
                    nc.vector.tensor_tensor(ya[:, f % 2, :], ya[:, f % 2, :], yl[:, f % 2, :], ALU.mult).then_inc(glu_done, 1)
                for q in range(2):
                    f = 2 * u + q
                    dve.wait_ge(gT_hi, f + 1)
                    nc.vector.tensor_tensor(gTl[:, f, :], ya[:, f % 2, :], gTh[:, f, :].bitcast(F32), ALU.subtract).then_inc(gT_lo, 1)
            for mg in range(2):
                for m in range(4):
                    i = 4 * mg + m
                    dve.wait_ge(chunk_done, cidx[("dn", mg, NF - 1)] + 1)
                    nc.vector.tensor_tensor(x1T[:, i, :], PS[:, 4 * mg + m, :], x1T[:, i, :], ALU.add).then_inc(x2_done, 1)
                for tt in range(NT):
                    dve.wait_ge(x2_tr, 4 * mg + tt + 1)
                    nc.vector.tensor_copy(x2n[:, tt, mg * 512:(mg + 1) * 512], PS[:, 4 * mg + tt, :]).then_inc(x2n_done, 1)
            for k in range(8):
                ng, tt = k // 4, k % 4
                dve.wait_ge(th_done, k + 1)
                dve.wait_ge(pp_in, 16 * 4 if k < 4 else 16 * 8)
                nc.vector.scalar_tensor_tensor(out=thb[:, k % 4, :], in0=thb[:, k % 4, :], scalar=1.0, in1=ppb[:, k % 4, :],
                                               op0=ALU.add, op1=ALU.mult).then_inc(th_mul, 1)
                dve.wait_ge(th_mul, k + 1)
                dve.wait_ge(x2n_done, 8)
                o = x2n[:, tt, ng * 512:(ng + 1) * 512]
                nc.vector.tensor_tensor(o, o, thb[:, k % 4, :], ALU.add).then_inc(o_done, 1)

        @block.tensor
        def _(pe):
            def three(o, ah, al, bh, bl, first, last):
                nc.tensor.matmul(o, ah, bh, start=first, stop=False)
                nc.tensor.matmul(o, ah, bl, start=False, stop=False)
                return nc.tensor.matmul(o, al, bh, start=False, stop=last)

            def turn_consts():
                pe.wait_ge(const_in, 16 * 11)
                pe.wait_ge(pool_const, 4)
                for k, (o0, nr) in enumerate(((0, CONVW), (CONVW, P), (CONVW + P, 4))):
                    nc.tensor.transpose(PS[:, 0, o0:o0 + nr], rows[0:nr, k, :], ident[0:nr, 0:nr]).then_inc(cst_turned, 1)

            def turn_input(kt):
                if kt == 0:
                    pe.wait_ge(pool_const, 4)
                if kt >= 6:
                    pe.wait_ge(hT_lo, kt - 5)
                for tt in range(NT):
                    pe.wait_ge(h_nat, tt + 1)
                    ins = nc.tensor.transpose(PS[:, turn_bank(kt), P * tt:P * (tt + 1)], xnat[:, tt, P * kt:P * (kt + 1)], ident)
                ins.then_inc(x_turned, 1)

            def project(w, tt, kts=range(KT)):
                r = use_index[("proj", w, tt)]
                c = ucols(w)
                if kts[0] == 0:
                    wait_free(pe, r)
                for kt in kts:
                    pe.wait_ge(w_lo, KT * w + kt + 1)
                    pe.wait_ge(hT_lo, kt + 1)
                    t_ = slice(P * tt, P * (tt + 1))
                    ins = three(PS[:, r % 2, 0:c], hTh[:, kt, t_], hTl[:, kt, t_], Wh[:, kt, 0:c], Wl[:, kt, 0:c], kt == 0, kt == KT - 1)
                    if tt == NT - 1 and kt < KT - 1:
                        ins.then_inc(w_used, 1)
                if kts[-1] == KT - 1:
                    ins.then_inc(bank_filled, 1)

            def turn_vector(w, x):
                r = use_index[("vec", w, x)]
                wait_free(pe, r)
                pe.wait_ge(norm_done, w + 1)
                pe.wait_ge(norm_dve, w + 1)
                for tt in range(NT):
                    ins = nc.tensor.transpose(PS[:, r % 2, P * tt:P * (tt + 1)], qn[:, tt, x, :], ident)
                ins.then_inc(bank_filled, 1)

            def gate(j, kts=range(KT)):
                if kts[0] == 0:
                    pe.wait_ge(g_lo, j + 1)
                    if j:
                        pe.wait_ge(gate_tanh, j)
                for kt in kts:
                    ins = three(PS[:, 7, :], Gh[:, kt, :], Gl[:, kt, :], hTh[:, kt, :], hTl[:, kt, :], kt == 0, kt == KT - 1)
                if kts[-1] == KT - 1:
                    ins.then_inc(gate_filled, 1)

            def compress(kv):
                pe.wait_ge(w1k_in, 16 * (kv + 1))
                pe.wait_ge(bp_done, kv + 1)
                pe.wait_ge(hT_lo, KT)
                o = bp[:, kv, 0:992].rearrange("p (g l n) -> p g l n", g=2, l=16)
                for c in range(16):
                    wt = w1k[:, c, :]
                    ins = nc.tensor.matmul(PS[:, cmp_bank["hidden"] + kv, 0:62].rearrange("p (g n) -> p g n", g=2), wt, o[:, :, c, :],
                                           start=(c == 0), stop=(c == 15))
                ins.then_inc(cmp_hidden, 1)

            def compress_out():
                pe.wait_ge(hid_done, 2)
                pe.wait_ge(w2c_in, 32)
                for kv in range(2):
                    for g in range(2):
                        o = (2 * kv + g) * DH
                        ins = nc.tensor.matmul(PS[0:NCMP, cmp_bank["out"], o:o + DH], hid[:, 62 * kv + 31 * g:62 * kv + 31 * (g + 1)], w2c[:, kv, :],
                                               start=True, stop=True)
                ins.then_inc(cmp_out, 1)

            def turn_compressed_keys():
                pe.wait_ge(kcn_done, 1)
                for g in range(2):
                    ins = nc.tensor.transpose(PS[:, cmp_bank["turned"], 32 * g:32 * g + NCMP], kcn[0:NCMP, g, :], ident[0:NCMP, 0:NCMP])
                ins.then_inc(cmp_turned, 1)

            def scores(t):
                s = STEPS[t]
                n, e, i = s["n"], s["e"], s["i"]
                if t < 2:
                    pe.wait_ge(hid_done, t + 1)
                if t >= 2:
                    pe.wait_ge(biased, t - 1)
                if s["k"] == 0:
                    pe.wait_ge(vec_lo, vec_base[n + 1] + nvec(n + 1) - 4)
                o = PS[:, 2 + t % 2, :]
                if s["br"] == "cmp":
                    pe.wait_ge(kc_lo, 1)
                    g = (n - 4) // 2
                    for q in range(NT):
                        nc.tensor.matmul(o[:, 32 * q:32 * q + 32], QQ[:, n % 2, e, P * q:P * (q + 1)], KCh[:, g, :], start=True, stop=False)
                        ins = nc.tensor.matmul(o[:, 32 * q:32 * q + 32], QQ[:, n % 2, e, P * q:P * (q + 1)], KCl[:, g, :], start=False, stop=True)
                else:
                    ks, ke = kslot(n, e, s["br"])
                    nk = P * (i + 1)
                    nc.tensor.matmul(o[:, 0:nk], QQ[:, n % 2, e, P * i:P * (i + 1)], Kh[:, ks, ke, 0:nk], start=True, stop=False)
                    ins = nc.tensor.matmul(o[:, 0:nk], QQ[:, n % 2, e, P * i:P * (i + 1)], Kl[:, ks, ke, 0:nk], start=False, stop=True)
                ins.then_inc(score, 1)

            def turn_probs(t):
                s = STEPS[t]
                pe.wait_ge(scaled, t + 1)
                if t == 0:
                    pe.wait_ge(vc_lo, 1)
                if t == 1:
                    pe.wait_ge(kc_lo, 1)
                if t >= 2:
                    pe.wait_ge(pt_lo, t - 1)
                if s["br"] == "cmp":
                    for q in range(NT):
                        ins = nc.tensor.transpose(PS[0:32, 4 + t % 2, P * q:P * (q + 1)], prob[:, t % 4, 32 * q:32 * q + 32], ident)
                else:
                    for j in range(s["i"] + 1):
                        ins = nc.tensor.transpose(PS[:, 4 + t % 2, P * j:P * (j + 1)], prob[:, t % 4, P * j:P * (j + 1)], ident)
                ins.then_inc(turned, 1)

            def values(t):
                s = STEPS[t]
                n, e, u = s["n"], s["e"], s["u"]
                pe.wait_ge(pt_lo, t + 1)
                opening = u == STEPS[first_t[n]]["u"]
                closing = t == last_t[n]
                if opening:
                    pe.wait_ge(v_lo, min(n + 1, 5) if n < 6 else 6)
                    if n > 0:
                        pe.wait_ge(y_evac, n)
                c0 = 0 if e == 0 else DH
                if s["br"] == "cmp":
                    pe.wait_ge(vc_lo, 1)
                    g = (n - 4) // 2
                    ins = three(PS[:, 6, :], VCh[0:32, g, c0:c0 + P], VCl[0:32, g, c0:c0 + P], PTh[0:32, u % 2, 0, :], PTl[0:32, u % 2, 0, :],
                                False, closing)
                else:
                    vs = vslot(n, s["br"])
                    for j in (reversed(range(NT)) if closing else range(NT)):
                        q = slice(P * j, S)
                        ins = three(PS[:, 6, q], Vh[:, vs, j, c0:c0 + P], Vl[:, vs, j, c0:c0 + P], PTh[:, u % 2, j, q], PTl[:, u % 2, j, q],
                                    opening and j == 0, closing and j == 0)
                ins.then_inc(pv_done, 1)

            for kt in range(4):
                turn_input(kt)
            turn_consts()
            for kt in range(4, KT):
                turn_input(kt)
            for tt in range(NT):
                project(0, tt)
            gate(0)
            for x in range(4):
                turn_vector(0, x)
            for tt in range(NT):
                project(1, tt)
            compress(0)
            gate(1)
            compress(1)
            for x in range(4):
                turn_vector(1, x)
            compress_out()
            project(2, 0)
            turn_compressed_keys()
            for t in range(T):
                if t >= VLAG and STEPS[t - VLAG]["last"]:
                    values(t - VLAG)
                scores(t)
                n, k, w = STEPS[t]["n"], STEPS[t]["k"], STEPS[t]["n"] + 2
                if t in PROJ:
                    project(*PROJ[t])
                if (n, k) in GATE_STEPS:
                    gate(*GATE_STEPS[(n, k)])
                for x in vec_steps(n, k):
                    turn_vector(w, x)
                if t >= LAG:
                    turn_probs(t - LAG)

            def turn_x(tt):
                pe.wait_ge(xs_in, 16 * (tt + 1))
                b = 4 + 2 * (tt % 2)
                if tt == 0:
                    pe.wait_ge(brB_done, 4)
                if tt >= 1:
                    pe.wait_ge(brB_done, 8)
                if tt >= 2:
                    pe.wait_ge(xT_done, 2 * tt - 2)
                for kt in range(KT):
                    ins = nc.tensor.transpose(PS[:, b + kt // 4, P * (kt % 4):P * (kt % 4 + 1)], xs[:, P * kt:P * (kt + 1)], ident)
                ins.then_inc(xs_tr, 1)

            def turn_p():
                pe.wait_ge(xs_in, 16 * 8)
                pe.wait_ge(xT_done, 8)
                for k in range(2):
                    for tt in range(NT):
                        ins = nc.tensor.transpose(PS[:, 4 + k, P * tt:P * (tt + 1)], xs[:, tt * PLE + P * k:tt * PLE + P * (k + 1)], ident)
                    ins.then_inc(p_tr, 1)

            def token_sums():
                pe.wait_ge(ssq_done, KT)
                pe.wait_ge(x1_done, KT)
                for tt in range(NT):
                    ins = nc.tensor.matmul(PS[:, 4, tt:tt + 1], sumsq[:, P * tt:P * (tt + 1)], ones[:, 0:1], start=True, stop=True)
                ins.then_inc(tok_sum, 1)

            def spread():
                pe.wait_ge(rdiag_done, 1)
                for tt in range(NT):
                    ins = nc.tensor.matmul(PS[:, 4, P * tt:P * (tt + 1)], ones, rdiag[:, P * tt:P * (tt + 1)], start=True, stop=True)
                ins.then_inc(bc_mm, 1)

            def turn_x2(half):
                pe.wait_ge(x2_done, 4 * half + 4)
                for tt in range(NT):
                    for kt in range(4):
                        ins = nc.tensor.transpose(PS[:, 4 * half + tt, P * kt:P * (kt + 1)], x1T[:, 4 * half + kt, P * tt:P * (tt + 1)], ident)
                    ins.then_inc(x2_tr, 1)

            for c in range(NC):
                kind, a, kt = CHUNKS[c]
                if T + c < T + VLAG:
                    if STEPS[T + c - VLAG]["last"]:
                        values(T + c - VLAG)
                    if c < LAG:
                        turn_probs(T + c - LAG)
                if c == 10:
                    turn_x(0)
                if (kind, a, kt) == ("wo", 0, 1):
                    turn_x(1)
                if (kind, a, kt) == ("wo", 0, 3):
                    turn_x(2)
                if (kind, a, kt) == ("wo", 0, 5):
                    turn_x(3)
                if (kind, a, kt) == ("wo", 1, 0):
                    turn_p()
                if (kind, a, kt) == ("ple", 1, 0):
                    token_sums()
                if (kind, a, kt) == ("ple", 1, 1):
                    spread()
                if (kind, a, kt) == ("dn", 1, 8):
                    turn_x2(0)
                if (kind, a, kt) == ("pg", 0, 6):
                    turn_x2(1)
                if kind == "bra":
                    pe.wait_ge(yt_lo, kt + 1)
                    act_h, act_l = yTh[:, kt, :], yTl[:, kt, :]
                    b0 = 0
                    if a == 0 and kt == 0:
                        pe.wait_ge(gate_tanh, NGATE)
                        pe.wait_ge(biased, T)
                    if a == 1 and kt == 0:
                        pe.wait_ge(brA_done, 4)
                elif kind == "brb":
                    if kt < 3:
                        pe.wait_ge(yt_lo, 4 + kt + 1)
                    else:
                        pe.wait_ge(y_evac, 8)
                        pe.wait_ge(yt_hi, 8)
                    act_h, act_l = yTh[:, 4 + kt, :], yTl[:, 4 + kt, :]
                    b0 = 4
                    if kt == 0:
                        if a:
                            pe.wait_ge(xT_done, 2)
                        else:
                            pe.wait_ge(pt_lo, T)
                elif kind == "wo":
                    pe.wait_ge(mT_lo, kt + 1)
                    act_h, act_l = mTh[:, kt, :], mTl[:, kt, :]
                    b0 = 4 * a
                    if kt == 0:
                        pe.wait_ge(brA_done, 8)
                        if a:
                            pe.wait_ge(pT_lo, 2)
                elif kind == "ple":
                    b0 = None
                    if kt == 0:
                        pe.wait_ge(x1_done, 4 if a == 0 else 8)
                        if a:
                            pe.wait_ge(pp_ev, 1)
                elif kind == "up":
                    pe.wait_ge(h2_lo, kt + 1)
                    act_h, act_l = h2h[:, kt, :], h2l[:, kt, :]
                    b0 = up_bank(a)
                    if kt == 0:
                        if a <= 1:
                            pe.wait_ge(pp_ev, 7 + a)
                        else:
                            pe.wait_ge(ya_conv, 2 * a - 2)
                            pe.wait_ge(yl_conv, 2 * a - 2)
                elif kind == "dn":
                    pe.wait_ge(gT_lo, kt + 1)
                    act_h, act_l = gTh[:, kt, :], gTl[:, kt, :]
                    b0 = 4 * a
                    if kt == 0:
                        u = 9 + a
                        pe.wait_ge(ya_conv, 2 * u + 2)
                        pe.wait_ge(yl_conv, 2 * u + 2)
                else:
                    pe.wait_ge(x2_lo, kt + 1)
                    b0 = None
                    if kt == 0:
                        pe.wait_ge(x2n_done, 4 * (a + 1))
                pe.wait_ge(w2_lo, c + 1)
                last = kt == {"bra": 3, "brb": 3, "wo": KT - 1, "ple": 1, "up": KT - 1, "dn": NF - 1, "pg": KT - 1}[kind]
                wh, wl = W2h[:, c % RING, :], W2l[:, c % RING, :]
                for m in (0, 1, 3, 2):
                    cs = slice(P * m, P * (m + 1))
                    if kind == "brb" and a == 0 and kt == 0 and m == 2:
                        pe.wait_ge(y_evac, 8)
                    if kind in ("ple", "pg"):
                        ah, al = (pTh, pTl) if kind == "ple" else (h2h, h2l)
                        b = ple_bank(a, m) if kind == "ple" else 4 * a + m
                        ins = three(PS[:, b, :], ah[:, kt, cs], al[:, kt, cs], wh, wl, kt == 0, last)
                    else:
                        ins = three(PS[:, b0 + m, :], wh[:, cs], wl[:, cs], act_h, act_l, kt == 0, last)
                ins.then_inc(chunk_done, 1)


_INS = ['x', 'p', 'rel_bias', 'attn_norm', 'w_in', 'moba_q_gain', 'moba_k_gain', 'nsa_q_gain', 'nsa_k_gain',
        'cmp_pos_k', 'cmp_w1_k', 'cmp_w2_k', 'cmp_pos_v', 'cmp_w1_v', 'cmp_w2_v', 'w_br_moba', 'w_br_nsa', 'w_o',
        'ffn_norm', 'w_up', 'conv_w', 'conv_b', 'w_down', 'w_ple_gate', 'w_ple']


def kernel(**inputs):
    import numpy as _np
    import concourse.bacc as _bacc
    from concourse.bass_utils import run_bass_kernel_spmd as _run

    nc = _bacc.Bacc("TRN2", target_bir_lowering=False, num_devices=1)
    arrays, args = {}, {}
    for name in _INS:
        a = _np.ascontiguousarray(inputs[name])
        arrays[f"in_{name}_dram"] = a
        args[name] = nc.dram_tensor(f"in_{name}_dram", a.shape, mybir.dt.from_np(a.dtype), kind="ExternalInput").ap()
    out = nc.dram_tensor("out_0_dram", (1, S, D), F32, kind="ExternalOutput").ap()
    layer(nc, args, out)
    r = _run(nc, [arrays], core_ids=[0])
    return r.results[0]["out_0_dram"]
```

```python
from contextlib import ExitStack

import numpy as np

import concourse.bass as bass
from concourse import mybir

ALU = mybir.AluOpType
ACT = mybir.ActivationFunctionType
F32 = mybir.dt.float32
F32R = mybir.dt.float32r
I32 = mybir.dt.int32
AX = mybir.AxisListType.X

P = 128
S, D, DH = 512, 1024, 64
NT, KT = S // P, D // P
DFF, PLE = 2816, 256
NF = DFF // P
HM = HN = 8
GR = 2
CMP_LEN, CMP_STRIDE = 32, 16
NCMP = (S - CMP_LEN) // CMP_STRIDE + 1
CW = 384
C_MQ, C_MK, C_NQ, C_KC, C_KS, C_NG, C_MG = 0, 512, 1536, 2048, 2304, 2816, 2840
NPAIR = 8
NGATE = 2 * D // P
EPS = 1e-6
BIG = 1e30
PITCH = 640


def bucket_edges():
    n = np.arange(S)
    nf = np.maximum(n, 1).astype(np.float32)
    large = 16 + (np.log(nf / np.float32(16)) / np.float32(np.log(128 / 16)) * np.float32(16)).astype(np.int32)
    b = np.where(n < 16, n, np.minimum(large, 31))
    return [(int(np.min(n[b == k])), int(np.max(n[b == k])) + 1) for k in range(32)]


def attention_steps():
    steps, u = [], 0
    for n in range(NPAIR):
        for e in range(2):
            for br in (["own"] if n < 4 else ["slc", "win", "cmp"]):
                tiles = range(1) if br == "cmp" else range(NT)
                for i in tiles:
                    steps.append(dict(n=n, e=e, br=br, i=i, u=u, last=(i == tiles[-1]), first=False, k=0))
                u += 1
        steps[-1]["pair_last"] = True
    k = 0
    for t, s in enumerate(steps):
        new = t == 0 or steps[t - 1]["n"] != s["n"]
        k = 0 if new else k + 1
        s["k"], s["first"] = k, new
    return steps


def layer(nc, A, out):
    STEPS = attention_steps()
    T = len(STEPS)
    first_t = [next(t for t, s in enumerate(STEPS) if s["n"] == n) for n in range(NPAIR)]
    last_t = [max(t for t, s in enumerate(STEPS) if s["n"] == n) for n in range(NPAIR)]
    NSTEP = [last_t[n] - first_t[n] + 1 for n in range(NPAIR)]
    unit_last_t = {s["u"]: t for t, s in enumerate(STEPS) if s["last"]}

    def ucols(w):
        return 2 * P + 24 if w == 0 else (P if w in (6, 8) else CW)

    def udmas(w):
        return {0: 0, 5: 3, 7: 3}.get(w, 1)

    def nvec(w):
        return 2 if w in (6, 8) else 4

    W_UNITS = 9
    GATE, j = {}, 2
    for n in range(NPAIR):
        if n in (1, 3):
            for k in range(KT):
                if k:
                    GATE[first_t[n] + k - 1] = (j, range(k, k + 1) if k > 1 else range(0, 2))
            j += 1
        elif n >= 4:
            for a in range(3):
                for b, rows in enumerate((range(0, 2), range(2, 4), range(4, 6), range(6, 8))):
                    GATE[first_t[n] + 6 * a + b] = (j, rows)
                j += 1
    gate_end = {j: t for t, (j, kts) in GATE.items() if kts[-1] == KT - 1}
    PROJ, SPLIT, NORM, VALUES, VEC = {}, {}, {}, {}, {}
    for w in range(2, W_UNITS):
        b0 = first_t[w - 2]
        if w < 6:
            start, rows_per_step, split0, split_rows = b0 - 6, 4, b0 - 7, 4
        elif w == 7:
            start, rows_per_step, split0, split_rows = b0 - 6, 2, b0 - 8, 2
        else:
            start, rows_per_step, split0, split_rows = b0, 4, (b0 - 6 if w == 6 else b0 - 8), 2
        for a in range(NT * KT // rows_per_step):
            k0 = a * rows_per_step % KT
            PROJ[start + a] = (w, a * rows_per_step // KT, range(k0, k0 + rows_per_step))
        for a in range(KT // split_rows):
            SPLIT[split0 + a] = (w, range(a * split_rows, (a + 1) * split_rows))
        end = start + NT * KT // rows_per_step
        NORM[end], VALUES[end] = w, w
        for x in range(nvec(w)):
            VEC[end + 2 + (w >= 6) + x] = (w, x)

    def proj_end(t):
        p = PROJ.get(t - 1)
        return p[:2] if p and t > 0 and p[2][-1] == KT - 1 else None

    EARLY = {T - 10 + 2 * c: c for c in range(4)}
    LAG = 3
    VLAG = LAG + 2
    vec_base = {}
    acc = 0
    for w in range(W_UNITS):
        vec_base[w] = acc
        acc += nvec(w)

    CHUNKS = []
    for mg in range(2):
        CHUNKS += [("bra", mg, kt) for kt in range(4)] + [("brb", mg, kt) for kt in range(4)]
    for mg in range(2):
        CHUNKS += [("wo", mg, kt) for kt in range(KT)]
    for ng in range(2):
        CHUNKS += [("ple", ng, kt) for kt in range(2)]
    for u in range(NF // 2):
        CHUNKS += [("up", u, kt) for kt in range(KT)]
    for mg in range(2):
        CHUNKS += [("dn", mg, kt) for kt in range(NF)]
    for ng in range(2):
        CHUNKS += [("pg", ng, kt) for kt in range(KT)]
    NC = len(CHUNKS)
    cidx = {c: i for i, c in enumerate(CHUNKS)}
    RING = 8

    x_d = A["x"].rearrange("b (t p) d -> (b t) p d", p=P)
    o_d = out.rearrange("b (t p) d -> (b t) p d", p=P)
    p_d = A["p"].rearrange("l b (t p) d -> (l b t) p d", p=P)
    win = A["w_in"].rearrange("l (k p) n -> (l k) p n", p=P)
    brm = A["w_br_moba"].rearrange("l (k p) n -> (l k) p n", p=P)
    brn = A["w_br_nsa"].rearrange("l (k p) n -> (l k) p n", p=P)
    wo_d = A["w_o"].rearrange("l (k p) n -> (l k) p n", p=P)
    up_d = A["w_up"].rearrange("l (k p) (h n) -> (l k) p h n", p=P, h=2)
    dn_d = A["w_down"].rearrange("l (k p) n -> (l k) p n", p=P)
    pg_d = A["w_ple_gate"].rearrange("l (k p) n -> (l k) p n", p=P)
    pl_d = A["w_ple"].rearrange("l (k p) n -> (l k) p n", p=P)
    w1_d = [A["cmp_w1_k"].rearrange("l (c p) h -> p (l c) h", p=P), A["cmp_w1_v"].rearrange("l (c p) h -> p (l c) h", p=P)]

    skew_d = nc.dram_tensor("skew", [16, P * PITCH], F32, kind="Internal").ap()
    gate_d = nc.dram_tensor("gates", [NGATE, P, S], F32, kind="Internal").ap()
    y_d = nc.dram_tensor("ys", [NPAIR, P, S], F32, kind="Internal").ap()
    pp_d = nc.dram_tensor("pps", [2 * NT, P, S], F32, kind="Internal").ap()

    with ExitStack() as ctx:
        def sem(n):
            return ctx.enter_context(nc.semaphore(n))

        R = ctx.enter_context(nc.sbuf_tensor("split_arena", [P, 38912], F32R))
        F = ctx.enter_context(nc.sbuf_tensor("plain_arena", [P, 14280], F32))
        PS = ctx.enter_context(nc.psum_tensor("banks", [P, 8, 512], F32))

        def r3(o, a, b):
            return R[:, o:o + a * b].rearrange("p (a b) -> p a b", a=a)

        def f3(o, a, b):
            return F[:, o:o + a * b].rearrange("p (a b) -> p a b", a=a)

        hTh, hTl = r3(0, KT, S), r3(4096, KT, S)
        Wh, Wl = r3(8192, KT, CW), r3(8192 + KT * CW, KT, CW)
        Gh, Gl = r3(14336, KT, P), r3(15360, KT, P)
        PTh = R[:, 16384:20480].rearrange("p (u j q) -> p u j q", u=2, j=NT)
        PTl = R[:, 20480:24576].rearrange("p (u j q) -> p u j q", u=2, j=NT)
        QQ = R[:, 24576:26624].rearrange("p (s e q) -> p s e q", s=2, e=2)
        Kh = R[:, 26624:28672].rearrange("p (s e q) -> p s e q", s=2, e=2)
        Kl = R[:, 28672:30720].rearrange("p (s e q) -> p s e q", s=2, e=2)
        Vh = R[:, 30720:33792].rearrange("p (s t c) -> p s t c", s=4, t=NT)
        Vl = R[:, 33792:36864].rearrange("p (s t c) -> p s t c", s=4, t=NT)
        VCh, VCl = r3(36864, 2, 192), r3(37248, 2, 192)
        KCh, KCl = r3(37632, 2, 32), r3(37696, 2, 32)
        yTh, yTl = r3(0, KT, S), r3(4096, KT, S)
        h2h, h2l = r3(0, KT, S), r3(4096, KT, S)
        W2h, W2l = r3(8192, RING, 512), r3(12288, RING, 512)
        mTh, mTl = r3(16384, KT, S), r3(20480, KT, S)
        pTh, pTl = r3(36864, 2, S), r3(37888, 2, S)
        gTh, gTl = r3(16384, NF, S), r3(16384 + NF * S, NF, S)

        raw = f3(0, KT, CW)
        graw = f3(3072, KT, P)
        strip = F[:, 4096:6144].rearrange("p (s e c) -> p s e c", s=2, e=2)
        prob = f3(6144, 4, S)
        xnat = f3(4096, NT, D)
        tcmp = f3(6144, 4, S)
        qkv = f3(8192, NT, CW)
        sq = F[:, 9728:10752].rearrange("p (t c) -> p t c", t=NT)
        qn = F[:, 9728:11776].rearrange("p (t v c) -> p t v c", t=NT, v=4)
        bp = f3(9728, 2, 1024)
        ystage = F[:, 11776:12288]
        gstage = F[:, 12288:12800]
        w1k = f3(4096, 16, P)
        rtab = F[0:16, 11776:12288]
        masked = F[0:16, 13600:13728]
        rbt = F[0:16, 8900:8932]
        rows = f3(9216, 3, P)
        ytmp = f3(8192, 7, S)
        raw2 = f3(0, RING, 512)
        x1T = f3(4096, KT, S)
        xs = F[:, 8192:9216]
        gb = f3(9216, 2, S)
        ga = f3(10240, 4, S)
        spare = F[:, 12288:12800]
        sumsq = F[:, 12288:12800]
        xg = F[:, 9216:10240]
        sqt = f3(8192, 4, S)
        rdiag = F[:, 9216:9728]
        rbc = F[:, 9728:10240]
        hst = f3(10240, 2, S)
        ppst = [F[:, o:o + S] for o in (11264, 11776, 8192, 8704)]
        ya, yl = f3(8192, 2, S), f3(10240, 2, S)
        x2n = f3(8192, NT, D)
        thb = f3(4096, 4, S)
        ppb = f3(6144, 4, S)
        ident = F[:, 12800:12928]
        ones = F[:, 12928:13056]
        cst = F[:, 13056:13296]
        gsig = F[:, 13296:13392].rearrange("p (t c) -> p t c", t=NT)
        st = F[:, 13392:13520]
        rq = F[:, 13520:13600]
        sc_c = f3(13600, NT, 32)
        hid = F[:, 13728:13852]
        sqt2 = f3(13728, 2, 256)
        kcn = F[:, 13852:13852 + 256].rearrange("p (g c) -> p g c", g=2)
        w2c = F[:, 14108:14236].rearrange("p (v c) -> p v c", v=2)
        neg8 = st[:, 100:102]
        mneg, rsum = st[:, 0:4], st[:, 4:8]
        rsum_c, mneg_c = st[:, 8:12], st[:, 12:16]
        ssx = st[:, 16:20]
        ss = st[:, 20:36]
        s_k = st[:, 36:38]

        CONVB, POSK, POSV, GQ, CONVW = 16, 60, 76, 92, 98

        x_in = [sem(f"x_in{i}") for i in range(NT)]
        const_in, rbt_in, w2c_in = sem("const_in"), sem("rbt_in"), sem("w2c_in")
        raw0_in = [sem("raw0_in0"), sem("raw0_in1")]
        raw_in = [sem(f"raw_in{k}") for k in range(KT)]
        graw_in = sem("graw_in")
        strip_in = [sem("strip_in0"), sem("strip_in1")]
        skew_out = sem("skew_out")
        w1k_in = sem("w1k_in")
        y_out, g_out = sem("y_out"), sem("g_out")
        y_in = sem("y_in")
        pool_const = sem("pool_const")
        rtab_done = sem("rtab_done")
        x_sq = sem("x_sq")
        h_nat = sem("h_nat")
        proj_filled, vec_filled = sem("proj_filled"), sem("vec_filled")
        cst_turned, x_turned = sem("cst_turned"), sem("x_turned")
        cmp_hidden, cmp_out, cmp_turned = sem("cmp_hidden"), sem("cmp_out"), sem("cmp_turned")
        hT_hi, hT_lo = sem("hT_hi"), sem("hT_lo")
        cst_done = sem("cst_done")
        w_hi, w_lo = sem("w_hi"), [sem("w_lo_even"), sem("w_lo_odd")]
        g_hi, g_lo = sem("g_hi"), [sem("g_lo_first"), sem("g_lo_second")]
        w_used, gate_filled = sem("w_used"), sem("gate_filled")
        norm_dve = sem("norm_dve")
        qkv_done = sem("qkv_done")
        sq_done, ss_done = sem("sq_done"), sem("ss_done")
        rstd_done = sem("rstd_done")
        norm_done = sem("norm_done")
        vec_hi, vec_lo = sem("vec_hi"), sem("vec_lo")
        v_hi, v_lo = sem("v_hi"), sem("v_lo")
        gate_tanh = sem("gate_tanh")
        gsig_tanh, gsig_done = sem("gsig_tanh"), sem("gsig_done")
        tcmp_a, tcmp_b = sem("tcmp_a"), sem("tcmp_b")
        bp_done = sem("bp_done")
        hid_done = sem("hid_done")
        cmp_sq = sem("cmp_sq")
        kcn_done = sem("kcn_done")
        vc_hi, vc_lo = sem("vc_hi"), sem("vc_lo")
        kc_hi, kc_lo = sem("kc_hi"), sem("kc_lo")
        score, biased, exped, scaled = sem("score"), sem("biased"), sem("exped"), sem("scaled")
        turned, pt_hi, pt_lo = sem("turned"), sem("pt_hi"), sem("pt_lo")
        pv_done = sem("pv_done")
        y_evac = sem("y_evac")
        chain = sem("dve_chain")
        yt_hi, yt_lo = sem("yt_hi"), [sem("yt_lo_even"), sem("yt_lo_odd")]
        raw2_in = [sem(f"raw2_in{k}") for k in range(RING)]
        w2_hi, w2_lo, chunk_done = sem("w2_hi"), sem("w2_lo"), sem("chunk_done")
        xg_in = sem("xg_in")
        sq_summed = sem("sq_summed")
        tail_done = sem("tail_done")
        xs_in, xs_tr, xT_done = sem("xs_in"), sem("xs_tr"), sem("xT_done")
        p_tr, pT_hi, pT_lo = sem("p_tr"), sem("pT_hi"), sem("pT_lo")
        ga_in, gb_in = [sem(f"ga_in{i}") for i in range(4)], [sem(f"gb_in{i}") for i in range(2)]
        brA_done, brB_done, br_sum = sem("brA_done"), sem("brB_done"), sem("br_sum")
        mT_hi, mT_lo = sem("mT_hi"), sem("mT_lo")
        x1_done, x1_sq, ssq_done = sem("x1_done"), sem("x1_sq"), sem("ssq_done")
        tok_sum, rdiag_done, bc_mm, bc_done = sem("tok_sum"), sem("rdiag_done"), sem("bc_mm"), sem("bc_done")
        h2_f, h2_hi, h2_lo = sem("h2_f"), sem("h2_hi"), sem("h2_lo")
        pp_ev, pp_out = sem("pp_ev"), [sem(f"pp_out{i}") for i in range(4)]
        ya_bias, yl_bias = sem("ya_bias"), sem("yl_bias")
        ya_conv, yl_conv = sem("ya_conv"), sem("yl_conv")
        gelu_done, glu_done, gT_hi, gT_lo = sem("gelu_done"), sem("glu_done"), sem("gT_hi"), sem("gT_lo")
        x2_done, x2_hi, x2_lo = sem("x2_done"), sem("x2_hi"), sem("x2_lo")
        x2_tr, x2n_done = sem("x2_tr"), sem("x2n_done")
        pp_in, th_done, th_mul, o_done, o_out = sem("pp_in"), sem("th_done"), sem("th_mul"), sem("o_done"), sem("o_out")

        def wait_weights(eng, w, kt):
            eng.wait_ge(w_lo[kt % 2], KT // 2 * w + kt // 2 + 1)

        def wait_unit(eng, w, kt):
            if w == 0:
                eng.wait_ge(raw0_in[kt // 4], 32)
                eng.wait_ge(x_sq, NT)
            else:
                eng.wait_ge(raw_in[kt], 16 * sum(udmas(v) for v in range(w + 1)))
                if kt < KT - 1:
                    eng.wait_ge(w_used, (KT - 1) * (w - 1) + kt + 1)
                else:
                    eng.wait_ge(proj_filled, 4 * w)

        def proj_bank(w, tt):
            return 6 if w <= 2 and tt % 2 and (w, tt) != (2, 3) else 0

        def vec_bank(w, x):
            return 4 if w <= 1 and x % 2 else 1

        def vec_number(w, x):
            return vec_base[w] + x + 1

        def turn_bank(kt):
            return 2 + kt % 6

        def kslot(n, e, br):
            if n < 4:
                return n % 2, e
            return (n - 4) // 2, (0 if br == "slc" else 1)

        def vslot(n, br):
            if n < 4:
                return n % 3
            return ((3, 1), (0, 2))[(n - 4) // 2][0 if br == "slc" else 1]

        def vec_dst(w, x):
            n = w - 1
            if x < 2:
                return "q", n % 2, x
            return ("k", n % 2, x - 2) if n < 4 else ("k", (n - 4) // 2, x - 2)

        def up_bank(u):
            return 4 * ((u + 1) % 2)

        cmp_bank = {"hidden": 2, "out": 4, "turned": 5}

        def cat(br):
            return {"cmp": 0, "slc": 1, "win": 2}[br]

        block = ctx.enter_context(nc.Block())

        @block.sync
        def _(sp):
            for tt in range(NT):
                sp.dma_start(xnat[:, tt, :], x_d[tt]).then_inc(x_in[tt], 16)
            def load_unit(w, kts):
                for kt in kts:
                    if w > 0:
                        wait_weights(sp, w - 1, kt)
                    if w <= 4:
                        n = w - 1
                        src = win[kt][:, 0:1536].rearrange("p (a c) -> p a c", a=3)[:, :, n * P:(n + 1) * P]
                        sp.dma_start(raw[:, kt, :].rearrange("p (a c) -> p a c", a=3), src).then_inc(raw_in[kt], 16)
                    else:
                        n = w - 5
                        sp.dma_start(raw[:, kt, 0:P], win[kt][:, C_NQ + n * P:C_NQ + (n + 1) * P]).then_inc(raw_in[kt], 16)
                        if n % 2 == 0:
                            g = n // 2
                            src = win[kt][:, C_KS:C_KS + 512].rearrange("p (b v c) -> p v b c", b=2, v=2)
                            dst = raw[:, kt, P:P + 256].rearrange("p (v b c) -> p v b c", v=2, b=2)
                            for v in range(2):
                                sp.dma_start(dst[:, v], src[:, v, :, g * DH:(g + 1) * DH]).then_inc(raw_in[kt], 16)

            def load_strips(n):
                if n >= 2:
                    sp.wait_ge(biased, last_t[n - 2] + 1)
                for e in range(2):
                    h = 2 * n + e
                    src = bass.AP(tensor=skew_d.tensor, offset=h * P * PITCH + P - 1, ap=[[PITCH - 1, P], [1, S]])
                    sp.dma_start(strip[:, n % 2, e, :], src).then_inc(strip_in[n % 2], 16)

            def load_gate_weights(j):
                if j > 0:
                    sp.wait_ge(g_lo[0], j)
                    sp.wait_ge(g_lo[1], j)
                sp.dma_start(graw[:, :, :], A["w_in"].rearrange("l (k p) n -> p (l k) n", p=P)[
                    :, :, C_MG + j * P:C_MG + (j + 1) * P]).then_inc(graw_in, 16)

            def spill_gate(j):
                sp.wait_ge(gate_tanh, j + 1)
                sp.dma_start(gate_d[j], gstage).then_inc(g_out, 16)

            def spill_y(n):
                sp.wait_ge(y_evac, n + 1)
                sp.dma_start(y_d[n], ystage).then_inc(y_out, 16)

            cw = A["conv_w"].rearrange("l w (r c) -> (l w r) c", c=P)
            blocks = [(rows[0:8, 0, :], A["attn_norm"].rearrange("l (r c) -> (l r) c", c=P)),
                      (rows[8:16, 0, :], A["ffn_norm"].rearrange("l (r c) -> (l r) c", c=P)),
                      (rows[CONVB:CONVB + 44, 0, :], A["conv_b"].rearrange("l (r c) -> (l r) c", c=P)),
                      (rows[POSK:POSK + 16, 0, :], A["cmp_pos_k"].rearrange("l (r a) c -> (l r) (a c)", a=2)),
                      (rows[POSV:POSV + 16, 0, :], A["cmp_pos_v"].rearrange("l (r a) c -> (l r) (a c)", a=2)),
                      (rows[:, 1, :], cw[0:P, :]), (rows[0:4, 2, :], cw[P:P + 4, :])]
            for dst, src in blocks:
                sp.dma_start(dst, src).then_inc(const_in, 16)
            def load_chunk(c):
                kind, a, kt = CHUNKS[c]
                if c >= RING:
                    sp.wait_ge(w2_lo, c - RING + 1)
                dst = raw2[:, c % RING, :]
                n0, n1 = a * 512, (a + 1) * 512
                src = {"bra": lambda: brm[kt][:, n0:n1], "brb": lambda: brn[kt][:, n0:n1], "wo": lambda: wo_d[kt][:, n0:n1],
                       "ple": lambda: pl_d[kt][:, n0:n1], "dn": lambda: dn_d[kt][:, n0:n1], "pg": lambda: pg_d[kt][:, n0:n1],
                       "up": lambda: up_d[kt][:, :, a * 256:(a + 1) * 256]}[kind]()
                if kind == "up":
                    dst = dst.rearrange("p (h c) -> p h c", h=2)
                sp.dma_start(dst, src).then_inc(raw2_in[c % RING], 16)

            wk = A["w_in"].rearrange("l (k p) n -> p (l k) n", p=P)
            for half in range(2):
                ks = slice(4 * half, 4 * half + 4)
                sp.dma_start(raw[:, ks, 0:256], wk[:, ks, C_KC:C_KC + 256]).then_inc(raw0_in[half], 16)
                sp.dma_start(raw[:, ks, 256:280], wk[:, ks, C_NG:C_NG + 24]).then_inc(raw0_in[half], 16)
            load_gate_weights(0)
            for v, nm in enumerate(("cmp_w2_k", "cmp_w2_v")):
                sp.dma_start(w2c[:, v, :], A[nm].rearrange("l k n -> (l k) n")).then_inc(w2c_in, 16)
            sp.wait_ge(x_turned, KT)
            sp.dma_start(w1k, w1_d[0]).then_inc(w1k_in, 16)
            load_unit(1, range(KT))
            sp.wait_ge(rtab_done, 1)
            for c0, part in ((0, rtab), (S, masked)):
                width = part.shape[1]
                dst = bass.AP(tensor=skew_d.tensor, offset=c0, ap=[[P * PITCH, 16], [PITCH, P], [1, width]])
                sp.dma_start(dst, part.unsqueeze(1).broadcast_to([16, P, width])).then_inc(skew_out, 16)
            load_gate_weights(1)
            spill_gate(0)
            load_unit(2, range(KT))
            sp.wait_ge(cmp_hidden, 1)
            sp.dma_start(w1k, w1_d[1]).then_inc(w1k_in, 16)
            load_gate_weights(2)
            sp.wait_ge(cmp_hidden, 2)
            sp.wait_ge(skew_out, 32)
            load_strips(0)
            spill_gate(1)
            load_unit(3, range(KT))
            load_gate_weights(3)
            for t in range(T):
                n, k = STEPS[t]["n"], STEPS[t]["k"]
                if k == 0 and n + 1 < NPAIR:
                    load_strips(n + 1)
                if n == NPAIR - 1 and k == 1:
                    wait_weights(sp, W_UNITS - 1, KT - 2)
                    wait_weights(sp, W_UNITS - 1, KT - 1)
                    for c in range(6):
                        load_chunk(c)
                if k == 4 and n > 0:
                    spill_y(n - 1)
                if n == NPAIR - 1 and k == 5:
                    sp.wait_ge(y_out, 16 * 7)
                    for m in range(7):
                        sp.dma_start(ytmp[:, m, :], y_d[m]).then_inc(y_in, 16)
                if t in SPLIT and SPLIT[t][0] + 1 < W_UNITS:
                    load_unit(SPLIT[t][0] + 1, SPLIT[t][1])
                for j, end in gate_end.items():
                    if t == end + 1:
                        spill_gate(j)
                        if j + 2 < NGATE:
                            load_gate_weights(j + 2)
            def load_gates_a(mg):
                for m in range(4):
                    if mg:
                        sp.wait_ge(mT_lo, m + 1)
                    sp.dma_start(ga[:, m, :], gate_d[4 * mg + m]).then_inc(ga_in[m], 16)

            def load_gate_b(k):
                if k >= 2:
                    sp.wait_ge(br_sum, k - 1)
                sp.dma_start(gb[:, k % 2, :], gate_d[8 + k]).then_inc(gb_in[k % 2], 16)

            def load_x(tt):
                if tt in (1, 3):
                    sp.wait_ge(xs_tr, tt if tt == 1 else 2)
                if tt == 2:
                    sp.wait_ge(br_sum, 8)
                    sp.dma_start(xg, x_d[tt]).then_inc(xg_in, 16)
                else:
                    sp.dma_start(xs, x_d[tt]).then_inc(xs_in, 16)

            for part in range(2):
                sp.wait_ge(g_lo[part], NGATE)
            for c in range(6, RING):
                load_chunk(c)
            sp.wait_ge(g_out, 16 * NGATE)
            sp.wait_ge(yt_lo[0], 4)
            sp.wait_ge(yt_lo[1], 3)
            load_x(0)
            for k in range(2):
                load_gate_b(k)
            load_gates_a(0)
            for c in range(RING, NC):
                load_chunk(c)
                if c == 15:
                    load_gate_b(2)
                    load_gate_b(3)
                if c == 18:
                    load_gates_a(1)
                    load_gate_b(4)
                    load_gate_b(5)
                if c == 19:
                    load_x(1)
                if c == 24:
                    load_gate_b(6)
                    load_gate_b(7)
                if c == 25:
                    load_x(2)
                    load_x(3)
                if c == 28:
                    sp.wait_ge(xs_tr, 3)
                    for tt in range(NT):
                        sp.dma_start(xg[:, tt * PLE:(tt + 1) * PLE], p_d[tt]).then_inc(xg_in, 16)
                if c in (47, 49):
                    for k in (range(0, 2) if c == 47 else range(2, 8)):
                        sp.wait_ge(pp_ev, k + 1)
                        sp.dma_start(pp_d[k], ppst[k % 4]).then_inc(pp_out[k % 4], 16)
            for k in range(4):
                sp.wait_ge(pp_out[k], 32)
            sp.wait_ge(x2_tr, 8)
            sp.wait_ge(x2_lo, 8)
            for k in range(4):
                sp.dma_start(ppb[:, k % 4, :], pp_d[k]).then_inc(pp_in, 16)
            for k in range(8):
                sp.wait_ge(o_done, k + 1)
                ng, tt = k // 4, k % 4
                sp.dma_start(o_d[tt][:, ng * 512:(ng + 1) * 512], x2n[:, tt, ng * 512:(ng + 1) * 512]).then_inc(o_out, 16)
                if k < 4:
                    sp.dma_start(ppb[:, k % 4, :], pp_d[k + 4]).then_inc(pp_in, 16)
            sp.wait_ge(o_out, 16 * 8)

        @block.gpsimd
        def _(pool):
            pool.memset(ident, 0.0).then_inc(pool_const, 1)
            pool.memset(ones, 1.0).then_inc(pool_const, 1)
            pool.memset(neg8[:, 0:1], -(DH ** -0.5)).then_inc(pool_const, 1)
            pool.wait_ge(pool_const, 1)
            pool.affine_select(out=ident, in_=ident, compare_op=ALU.not_equal, fill=1.0, base=0,
                               pattern=[[-1, P]], channel_multiplier=1).then_inc(pool_const, 1)
            for t_ in (Vh, Vl):
                pool.memset(t_[:, :, :, DH:2 * DH].bitcast(F32), 0.0).then_inc(pool_const, 1)
            for t_ in (VCh, VCl, KCh, KCl):
                pool.memset(t_.bitcast(F32), 0.0).then_inc(pool_const, 1)
            pool.memset(rtab, BIG).then_inc(pool_const, 1)
            pool.memset(masked, BIG).then_inc(pool_const, 1)
            pool.wait_ge(rbt_in, 16)
            pool.wait_ge(pool_const, 12)
            for b, (lo, hi) in enumerate(bucket_edges()):
                ins = pool.tensor_scalar(rtab[:, S - hi:S - lo], rbt[:, b:b + 1].broadcast_to([16, hi - lo]), -1.0, None, ALU.mult)
            ins.then_inc(rtab_done, 1)

            def split_unit(w, kts):
                c = ucols(w)
                for kt in kts:
                    if kt % 2:
                        pool.wait_ge(w_hi, KT * w + kt + 1)
                        pool.tensor_tensor(Wl[:, kt, 0:c], raw[:, kt, 0:c], Wh[:, kt, 0:c].bitcast(F32), ALU.subtract).then_inc(w_lo[1], 1)

            def split_gate(j):
                pool.wait_ge(g_hi, j + 1)
                pool.tensor_tensor(Gl[:, 4:8, :], graw[:, 4:8, :], Gh[:, 4:8, :].bitcast(F32), ALU.subtract).then_inc(g_lo[1], 1)

            def v_low(w):
                n = w - 1
                pool.wait_ge(v_hi, w if n <= 4 else 6)
                if n < 4:
                    o = Vl[:, vslot(n, "own")].rearrange("p t (a c) -> p t a c", a=3)[:, :, 0:3:2, :]
                    hi = Vh[:, vslot(n, "own")].rearrange("p t (a c) -> p t a c", a=3)[:, :, 0:3:2, :]
                    i = qkv[:, :, 256:384].rearrange("p t (a c) -> p t a c", a=2)
                    pool.tensor_tensor(o, i, hi.bitcast(F32), ALU.subtract).then_inc(v_lo, 1)
                else:
                    for b in range(2):
                        s = vslot(n, ("slc", "win")[b])
                        for a in (0, 2):
                            ins = pool.tensor_tensor(Vl[:, s, :, a * DH:(a + 1) * DH], qkv[:, :, 256 + b * DH:256 + (b + 1) * DH],
                                                     Vh[:, s, :, a * DH:(a + 1) * DH].bitcast(F32), ALU.subtract)
                    ins.then_inc(v_lo, 1)

            def normalise(w):
                k = nvec(w)
                pool.wait_ge(rstd_done, w)
                if w > 1:
                    pool.wait_ge(vec_filled, vec_number(w - 1, nvec(w - 1) - 1))
                for tt in range(2):
                    i = qkv[:, tt, 0:k * DH].rearrange("p (v c) -> p v c", v=k)
                    for a in range(2):
                        ins = pool.tensor_tensor(qn[:, tt, 0:k, a * DH:(a + 1) * DH], i,
                                                 rq[:, 4 * tt:4 * tt + k].unsqueeze(2).broadcast_to([P, k, DH]), ALU.mult)
                ins.then_inc(norm_done, 1)

            def split_chunk(c):
                pool.wait_ge(w2_hi, c + 1)
                pool.tensor_tensor(W2l[:, c % RING, :], raw2[:, c % RING, :], W2h[:, c % RING, :].bitcast(F32),
                                   ALU.subtract).then_inc(w2_lo, 1)

            split_unit(0, range(KT))
            split_gate(0)
            pool.wait_ge(cst_done, 1)
            for tt in range(2):
                pool.wait_ge(qkv_done, tt + 1)
                for a in range(2):
                    ins = pool.tensor_copy(qn[:, tt, :, a * DH:(a + 1) * DH], qkv[:, tt, 0:256].rearrange("p (v c) -> p v c", v=4))
            ins.then_inc(norm_done, 1)
            split_unit(1, range(KT))
            split_gate(1)
            for kv in range(2):
                for g in range(2):
                    pool.wait_ge(tcmp_b, 2 * kv + g + 1)
                pool.wait_ge(tcmp_a, 2 * kv + 2)
                pool.wait_ge(vec_filled, 4)
                for half in range(2):
                    o = bp[:, kv, 0:992].rearrange("p (g l n) -> p g l n", g=2, l=16)
                    pos = cst[:, (POSV if kv else POSK) + 8 * half:(POSV if kv else POSK) + 8 * half + 8]
                    for g in range(2):
                        tk = tcmp[:, 2 * kv + g, 16 * half:16 * half + 496].rearrange("p (n l) -> p l n", l=16)[:, 0:16:2, :]
                        ins = pool.tensor_tensor(o[:, g, 8 * half:8 * half + 8, :], tk,
                                                 pos.unsqueeze(2).broadcast_to([P, 8, NCMP]), ALU.add)
                ins.then_inc(bp_done, 1)
            normalise(1)
            v_low(1)
            split_unit(2, range(KT))
            split_gate(2)
            for t in range(T):
                n, k, w = STEPS[t]["n"], STEPS[t]["k"], STEPS[t]["n"] + 2
                for j, end in gate_end.items():
                    if t == end + 1 and j + 1 < NGATE:
                        split_gate(j + 1)
                if t in SPLIT:
                    split_unit(*SPLIT[t])
                if t in NORM:
                    normalise(NORM[t])
                if t in VALUES and VALUES[t] not in (6, 8):
                    v_low(VALUES[t])
                if t in EARLY:
                    split_chunk(EARLY[t])

            for c in range(NC):
                if c >= 4:
                    if c == 4:
                        pool.wait_ge(gate_filled, NGATE)
                    if c < RING:
                        pool.wait_ge(yt_hi, 2 * (c - 4) + 1)
                        pool.tensor_tensor(yTl[:, 2 * (c - 4), :], ytmp[:, 2 * (c - 4), :], yTh[:, 2 * (c - 4), :].bitcast(F32),
                                           ALU.subtract).then_inc(yt_lo[0], 1)
                    split_chunk(c)
                for mg in range(1):
                    for m in range(4):
                        if mg == 0 and c == cidx[("wo", mg, KT - 1)] + 7:
                            kt = m
                            pool.wait_ge(x1_sq, kt + 1)
                            if kt == 0:
                                pool.tensor_copy(sumsq, sqt[:, 0, :]).then_inc(ssq_done, 1)
                            else:
                                pool.wait_ge(ssq_done, kt)
                                pool.tensor_tensor(sumsq, sumsq, sqt[:, kt % 2, :], ALU.add).then_inc(ssq_done, 1)
                if c == cidx[("ple", 1, 0)] + 7:
                    for kt in range(KT):
                        pool.wait_ge(h2_hi, kt + 1)
                        pool.tensor_tensor(h2l[:, kt, :], hst[:, kt % 2, :], h2h[:, kt, :].bitcast(F32), ALU.subtract).then_inc(h2_lo, 1)
                for mg in range(2):
                    if c == cidx[("dn", mg, NF - 1)] + 7:
                        for m in range(4):
                            kt = 4 * mg + m
                            pool.wait_ge(x2_hi, kt + 1)
                            pool.tensor_tensor(h2l[:, kt, :], x1T[:, kt, :], h2h[:, kt, :].bitcast(F32), ALU.subtract).then_inc(x2_lo, 1)

        @block.scalar
        def _(act):
            for r0, n, src in ((GQ, 1, A["moba_q_gain"]), (GQ + 1, 1, A["moba_k_gain"]), (GQ + 2, 1, A["nsa_q_gain"]),
                               (GQ + 3, 3, A["nsa_k_gain"].rearrange("l b c -> (l b) c"))):
                act.dma_start(rows[r0:r0 + n, 0, :].rearrange("r (a c) -> r a c", a=2),
                              src.unsqueeze(1).broadcast_to([n, 2, DH])).then_inc(const_in, 16)
            act.dma_start(rbt, A["rel_bias"]).then_inc(rbt_in, 16)
            for tt in (0, 1, 3):
                act.wait_ge(x_in[tt], 16)
                nc.scalar.activation(R[:, 8192 + tt * D:8192 + (tt + 1) * D], xnat[:, tt, :], ACT.Square, accum_out=ssx[:, tt:tt + 1]).then_inc(x_sq, 1)

            def take_proj(w, tt):
                act.wait_ge(proj_filled, 4 * w + tt + 1)
                if w == 1:
                    act.wait_ge(norm_done, 1)
                    act.wait_ge(norm_dve, 1)
                    act.wait_ge(gsig_tanh, 1)
                if w > 1 and tt == 0:
                    act.wait_ge(norm_dve, w)
                    act.wait_ge(norm_done, w)
                    if w - 1 not in (6, 8):
                        act.wait_ge(v_lo, min(w - 1, 5) if w - 1 < 7 else 6)
                nc.scalar.activation(qkv[:, tt, 0:ucols(w)], PS[:, proj_bank(w, tt), 0:ucols(w)], ACT.Copy).then_inc(qkv_done, 1)

            def w_high(w, kts):
                for kt in kts:
                    wait_unit(act, w, kt)
                    nc.scalar.activation(Wh[:, kt, 0:ucols(w)], raw[:, kt, 0:ucols(w)], ACT.Copy).then_inc(w_hi, 1)

            def squares_tile(w, tt):
                q = (w - 2) * NT + tt
                act.wait_ge(qkv_done, 4 * w + tt + 1)
                if q >= 2:
                    act.wait_ge(ss_done, q - 1)
                if q == 0:
                    act.wait_ge(cmp_turned, 1)
                nc.scalar.activation(sqt2[:, q % 2, 0:nvec(w) * DH], qkv[:, tt, 0:nvec(w) * DH], ACT.Square).then_inc(sq_done, 1)

            def squares(w):
                k = nvec(w)
                act.wait_ge(qkv_done, 4 * w + 4)
                act.wait_ge(cmp_hidden, 1)
                nc.scalar.activation(sq[:, :, 0:k * DH], qkv[:, :, 0:k * DH], ACT.Square).then_inc(sq_done, 1)

            def v_high(w):
                n = w - 1
                act.wait_ge(qkv_done, 4 * w + 4)
                if n < 4:
                    if n == 3:
                        act.wait_ge(pv_done, 2)
                    o = Vh[:, vslot(n, "own")].rearrange("p t (a c) -> p t a c", a=3)[:, :, 0:3:2, :]
                    nc.scalar.activation(o, qkv[:, :, 256:384].rearrange("p t (a c) -> p t a c", a=2), ACT.Copy).then_inc(v_hi, 1)
                else:
                    act.wait_ge(pv_done, 4 if n == 4 else 8)
                    for b in range(2):
                        s = vslot(n, ("slc", "win")[b])
                        for a in (0, 2):
                            ins = nc.scalar.activation(Vh[:, s, :, a * DH:(a + 1) * DH], qkv[:, :, 256 + b * DH:256 + (b + 1) * DH], ACT.Copy)
                    ins.then_inc(v_hi, 1)

            def vec_high(w, x):
                n = w - 1
                act.wait_ge(vec_filled, vec_number(w, x))
                kind, s, e = vec_dst(w, x)
                if kind == "q":
                    if n >= 2:
                        act.wait_ge(score, last_t[n - 2] + 1)
                    g = cst[:, GQ + (0 if n < 4 else 2):GQ + (0 if n < 4 else 2) + 1]
                    dst = QQ[:, s, e, :]
                else:
                    if n >= 2:
                        act.wait_ge(score, last_t[min(n - 2, 3)] + 1)
                    g = cst[:, GQ + 1:GQ + 2] if n < 4 else cst[:, GQ + 4 + e:GQ + 5 + e]
                    dst = Kh[:, s, e, :]
                nc.scalar.activation(dst, PS[:, vec_bank(w, x), :], ACT.Copy, scale=g).then_inc(vec_hi, 1)

            def exp(t):
                s = STEPS[t]
                act.wait_ge(biased, t + 1)
                if s["br"] == "cmp":
                    nc.scalar.activation(prob[:, t % 4, 0:P], sc_c.rearrange("p a b -> p (a b)"), ACT.Exp, scale=-1.0).then_inc(exped, 1)
                else:
                    nk = P * (s["i"] + 1)
                    nc.scalar.activation(prob[:, t % 4, 0:nk], prob[:, t % 4, 0:nk], ACT.Exp, bias=mneg[:, t % 4:t % 4 + 1],
                                         scale=-1.0, accum_out=rsum[:, t % 4:t % 4 + 1]).then_inc(exped, 1)

            def pt_high(t):
                s = STEPS[t]
                act.wait_ge(turned, t + 1)
                if s["u"] >= 2:
                    act.wait_ge(pv_done, s["u"] - 1)
                if s["br"] == "cmp":
                    nc.scalar.activation(PTh[0:32, s["u"] % 2, 0, :], PS[0:32, 4 + t % 2, :], ACT.Copy).then_inc(pt_hi, 1)
                else:
                    i = s["i"]
                    nc.scalar.activation(PTh[:, s["u"] % 2, 0:i + 1, P * i:P * (i + 1)],
                                         PS[:, 4 + t % 2, 0:P * (i + 1)].rearrange("p (j q) -> p j q", j=i + 1), ACT.Copy).then_inc(pt_hi, 1)

            def take_gate(j):
                act.wait_ge(gate_filled, j + 1)
                if j > 0:
                    act.wait_ge(g_out, 16 * j)
                nc.scalar.activation(gstage, PS[:, 7, :], ACT.Tanh, scale=0.5).then_inc(gate_tanh, 1)

            def split_chunk(c):
                act.wait_ge(raw2_in[c % RING], 16 * (c // RING + 1))
                if c >= RING:
                    act.wait_ge(chunk_done, c - RING + 1)
                if c == 0:
                    act.wait_ge(proj_filled, 4 * W_UNITS)
                    act.wait_ge(vec_filled, vec_number(8, 1))
                nc.scalar.activation(W2h[:, c % RING, :], raw2[:, c % RING, :], ACT.Copy).then_inc(w2_hi, 1)

            act.wait_ge(cst_turned, 3)
            nc.scalar.activation(cst[:, 0:CONVW + P + 4], PS[:, 0, 0:CONVW + P + 4], ACT.Copy).then_inc(cst_done, 1)
            act.wait_ge(cst_done, 1)
            for kt in range(KT):
                act.wait_ge(x_turned, kt + 1)
                nc.scalar.activation(hTh[:, kt, :], PS[:, turn_bank(kt), :], ACT.Copy, scale=cst[:, kt:kt + 1]).then_inc(hT_hi, 1)
            for tt in range(NT):
                take_proj(0, tt)
            act.wait_ge(qkv_done, 4)
            nc.scalar.activation(gsig, qkv[:, :, 256:280], ACT.Tanh, scale=0.5).then_inc(gsig_tanh, 1)
            for x in range(4):
                act.wait_ge(vec_filled, x + 1)
                nc.scalar.activation(tcmp[0:DH, x, :], PS[0:DH, vec_bank(0, x), :], ACT.Copy).then_inc(tcmp_a, 1)
            take_gate(0)
            for tt in range(3):
                take_proj(1, tt)
            for kv in range(2):
                act.wait_ge(cmp_hidden, kv + 1)
                nc.scalar.activation(hid[:, kv * 62:kv * 62 + 62], PS[:, cmp_bank["hidden"] + kv, 0:62], ACT.Gelu_apprx_tanh).then_inc(hid_done, 1)
                if kv == 0:
                    take_proj(1, 3)
                    squares(1)
                    v_high(1)
                    take_gate(1)
            for x in range(4):
                vec_high(1, x)
            take_proj(2, 0)
            act.wait_ge(cmp_out, 1)
            vps = PS[0:NCMP, cmp_bank["out"], P:2 * P].rearrange("p (g c) -> p g c", g=2)
            act.wait_ge(pool_const, 12)
            act.wait_ge(kcn_done, 1)
            for g in range(2):
                for a in (0, 2):
                    ins = nc.scalar.activation(VCh[0:NCMP, g, a * DH:(a + 1) * DH], vps[:, g, :], ACT.Copy)
            ins.then_inc(vc_hi, 1)
            take_proj(2, 1)
            act.wait_ge(cmp_turned, 1)
            for g in range(2):
                ins = nc.scalar.activation(KCh[:, g, 0:NCMP], PS[:, cmp_bank["turned"], 32 * g:32 * g + NCMP], ACT.Copy, scale=cst[:, GQ + 3:GQ + 4])
            ins.then_inc(kc_hi, 1)
            take_proj(2, 2)
            for tt in range(3):
                squares_tile(2, tt)
            for t in range(T + LAG):
                n, k, w = (STEPS[t]["n"], STEPS[t]["k"], STEPS[t]["n"] + 2) if t < T else (NPAIR, 0, 0)
                if proj_end(t):
                    take_proj(*proj_end(t))
                    squares_tile(*proj_end(t))
                for j, end in gate_end.items():
                    if t == end + 1:
                        take_gate(j)
                        if j + 1 < NGATE:
                            act.wait_ge(graw_in, 16 * (j + 2))
                            nc.scalar.activation(Gh, graw, ACT.Copy).then_inc(g_hi, 1)
                if t < T:
                    exp(t)
                if LAG <= t:
                    pt_high(t - LAG)
                if t in VEC:
                    vec_high(*VEC[t])
                if t in SPLIT:
                    w_high(*SPLIT[t])
                if t in VALUES and VALUES[t] not in (6, 8):
                    v_high(VALUES[t])
                if t in EARLY:
                    split_chunk(EARLY[t])
                if t == T - 2:
                    act.wait_ge(gate_filled, NGATE)
                    act.wait_ge(y_in, 16 * 7)
                if T - 2 <= t < T + 2:
                    for m in range(2 * (t - T + 2), min(2 * (t - T + 2) + 2, 7)):
                        nc.scalar.activation(yTh[:, m, :], ytmp[:, m, :], ACT.Copy).then_inc(yt_hi, 1)
                    split_chunk(4 + t - T + 2)

            act.wait_ge(pv_done, STEPS[-1]["u"] + 1)
            nc.scalar.activation(yTh[:, 7, :], PS[:, 6, :], ACT.Copy).then_inc(yt_hi, 1)

            def take_x(tt):
                for half in range(2):
                    b = (4 + 2 * (tt % 2)) + half
                    act.wait_ge(xs_tr, tt + 1)
                    nc.scalar.activation(x1T[:, 4 * half:4 * half + 4, P * tt:P * (tt + 1)],
                                         PS[:, b, :].rearrange("p (k q) -> p k q", k=4), ACT.Copy).then_inc(xT_done, 1)

            def conv_bias(f):
                u, q = f // 2, f % 2
                act.wait_ge(chunk_done, cidx[("up", u, KT - 1)] + 1)
                for half, (dst, sm) in enumerate(((ya, ya_bias), (yl, yl_bias))):
                    b = up_bank(u) + 2 * half + q
                    if f == 0 and half == 0:
                        act.wait_ge(h2_lo, KT)
                        act.wait_ge(h2_f, KT)
                        for k in range(4):
                            act.wait_ge(pp_out[k], 32)
                    if f >= 2:
                        act.wait_ge(gT_lo, f - 1)
                    col = half * NF + f
                    nc.scalar.activation(dst[:, f % 2, :], PS[:, b, :], ACT.Identity, scale=cst[:, CONVW + 88 + col:CONVW + 89 + col],
                                         bias=cst[:, CONVB + col:CONVB + col + 1]).then_inc(sm, 1)

            def gelu(f):
                act.wait_ge(ya_conv, f + 1)
                nc.scalar.activation(ya[:, f % 2, :], ya[:, f % 2, :], ACT.Gelu_apprx_tanh).then_inc(gelu_done, 1)

            def g_high(f):
                act.wait_ge(glu_done, f + 1)
                if f == 0:
                    act.wait_ge(chunk_done, cidx[("ple", 1, 1)] + 1)
                nc.scalar.activation(gTh[:, f, :], ya[:, f % 2, :], ACT.Copy).then_inc(gT_hi, 1)

            def take_pp(k):
                act.wait_ge(chunk_done, cidx[("ple", k // 4, 1)] + 1)
                if k == 2:
                    act.wait_ge(tok_sum, 1)
                if k >= 4:
                    act.wait_ge(pp_out[k % 4], 16)
                nc.scalar.activation(ppst[k % 4], PS[:, k % 4, :], ACT.Copy, scale=0.5).then_inc(pp_ev, 1)

            for c in range(RING, NC + 10):
                if c == 11 + RING:
                    take_x(0)
                e = c - RING
                kind, a, kt = CHUNKS[e] if e < NC else (None, 0, 0)
                if kind == "brb" and kt == 3:
                    for m in range(4):
                        i = 4 * a + m
                        act.wait_ge(br_sum, i + 1)
                        nc.scalar.activation(mTh[:, i, :], ga[:, m, :], ACT.Copy, scale=0.5).then_inc(mT_hi, 1)
                if kind == "wo" and a == 0 and kt in (2, 4, 5):
                    take_x({2: 1, 4: 2, 5: 3}[kt])
                if kind == "wo" and a == 0 and kt == 7:
                    for k in range(2):
                        act.wait_ge(p_tr, k + 1)
                        nc.scalar.activation(pTh[:, k, :], PS[:, 4 + k, :], ACT.Copy).then_inc(pT_hi, 1)
                if kind == "wo" and kt == KT - 1:
                    for m in range(4):
                        i = 4 * a + m
                        act.wait_ge(x1_done, i + 1)
                        if 2 <= i < 6:
                            act.wait_ge(ssq_done, i - 1)
                        nc.scalar.activation(sqt[:, i % 2 if i < 4 else i % 4, :], x1T[:, i, :], ACT.Square).then_inc(x1_sq, 1)
                if kind == "ple" and (a, kt) == (0, 1):
                    for k in range(4):
                        take_pp(k)
                if kind == "ple" and (a, kt) == (1, 0):
                    act.wait_ge(bc_mm, 1)
                    nc.scalar.activation(rbc, PS[:, 4, :], ACT.Copy).then_inc(bc_done, 1)
                    for i in range(KT):
                        act.wait_ge(h2_f, i + 1)
                        nc.scalar.activation(h2h[:, i, :], hst[:, i % 2, :], ACT.Copy).then_inc(h2_hi, 1)
                if kind == "ple" and (a, kt) == (1, 1):
                    for k in range(4, 8):
                        take_pp(k)
                if kind == "up" and kt == KT - 1:
                    conv_bias(2 * a)
                    conv_bias(2 * a + 1)
                if (kind == "up" and kt == 0 and a > 0) or (kind == "dn" and a == 0 and kt == 0):
                    u = a - 1 if kind == "up" else NF // 2 - 1
                    gelu(2 * u)
                    gelu(2 * u + 1)
                if (kind == "up" and kt == 1 and a > 0) or (kind == "dn" and a == 0 and kt == 1):
                    u = a - 1 if kind == "up" else NF // 2 - 1
                    g_high(2 * u)
                    g_high(2 * u + 1)
                if kind == "dn" and kt == NF - 1:
                    for m in range(4):
                        i = 4 * a + m
                        act.wait_ge(x2_done, i + 1)
                        nc.scalar.activation(h2h[:, i, :], x1T[:, i, :], ACT.Copy).then_inc(x2_hi, 1)
                if kind == "pg" and kt == KT - 1:
                    for tt in range(NT):
                        k = 4 * a + tt
                        if a == 0:
                            act.wait_ge(chunk_done, e + 1)
                        else:
                            act.wait_ge(tail_done, tt + 1)
                        if k == 0:
                            act.wait_ge(x2_tr, 8)
                            act.wait_ge(x2_lo, 8)
                        if k >= 4:
                            act.wait_ge(o_done, k - 3)
                        nc.scalar.activation(thb[:, k % 4, :], PS[:, 4 * a + tt, :], ACT.Tanh, scale=0.5).then_inc(th_done, 1)
                if c < NC:
                    split_chunk(c)

        @block.vector
        def _(dve):
            nch = [0]

            def link(ins):
                nch[0] += 1
                ins.then_inc(chain, 1)
                dve.wait_ge(chain, nch[0])

            def rsqrt(dst, src, inv_n, wdt, parts=P, done=None):
                v = st[0:parts, 40:40 + wdt]
                y = dst
                a = st[0:parts, 60:60 + wdt]
                link(nc.vector.tensor_scalar(v, src, inv_n, EPS, ALU.mult, ALU.add))
                link(nc.vector.tensor_scalar(a.bitcast(I32), v.bitcast(I32), 1, None, ALU.logical_shift_right))
                link(nc.vector.tensor_scalar(y.bitcast(I32), a.bitcast(I32), -1.0, float(0x5F3759DF), ALU.mult, ALU.add))
                for it in range(3):
                    link(nc.vector.tensor_tensor(a, y, y, ALU.mult))
                    link(nc.vector.scalar_tensor_tensor(out=a, in0=a, scalar=-0.5, in1=v, op0=ALU.mult, op1=ALU.mult))
                    ins = nc.vector.scalar_tensor_tensor(out=y, in0=a, scalar=1.5, in1=y, op0=ALU.add, op1=ALU.mult)
                    if it == 2 and done is not None:
                        ins.then_inc(done, 1)
                    else:
                        link(ins)

            def w_high(w, kts):
                for kt in kts:
                    wait_unit(dve, w, kt)
                    nc.vector.tensor_copy(Wh[:, kt, 0:ucols(w)], raw[:, kt, 0:ucols(w)]).then_inc(w_hi, 1)

            def w_low(w, kts):
                c = ucols(w)
                for kt in kts:
                    if kt % 2 == 0:
                        dve.wait_ge(w_hi, KT * w + kt + 1)
                        nc.vector.tensor_tensor(Wl[:, kt, 0:c], raw[:, kt, 0:c], Wh[:, kt, 0:c].bitcast(F32), ALU.subtract).then_inc(w_lo[0], 1)

            def split_unit(w, kts):
                for k0 in kts[::2]:
                    w_high(w, range(k0, k0 + 2))
                    w_low(w, range(k0, k0 + 2))

            def gate_high(j):
                dve.wait_ge(graw_in, 16 * (j + 1))
                if j > 0:
                    dve.wait_ge(gate_filled, j)
                nc.vector.tensor_copy(Gh, graw).then_inc(g_hi, 1)

            def gate_low(j):
                dve.wait_ge(g_hi, j + 1)
                nc.vector.tensor_tensor(Gl[:, 0:4, :], graw[:, 0:4, :], Gh[:, 0:4, :].bitcast(F32), ALU.subtract).then_inc(g_lo[0], 1)

            dve.wait_ge(x_in[2], 16)
            nc.vector.tensor_tensor_reduce(out=R[:, 8192 + 2 * D:8192 + 3 * D], in0=xnat[:, 2, :], in1=xnat[:, 2, :], scale=1.0, scalar=0.0,
                                           op0=ALU.mult, op1=ALU.add, accum_out=ssx[:, 2:3]).then_inc(x_sq, 1)
            dve.wait_ge(x_sq, NT)
            rsqrt(st[:, 80:84], ssx, 1.0 / D, 4)
            for tt in range(NT):
                nc.vector.tensor_scalar(xnat[:, tt, :], xnat[:, tt, :], st[:, 80 + tt:81 + tt], None, ALU.mult).then_inc(h_nat, 1)
            split_unit(0, range(KT))
            dve.wait_ge(cst_done, 1)
            dve.wait_ge(pool_const, 4)
            for c in (GQ, GQ + 2):
                link(nc.vector.tensor_scalar(cst[:, c:c + 1], cst[:, c:c + 1], -(DH ** -0.5), None, ALU.mult))
            for kt in range(KT):
                dve.wait_ge(hT_hi, kt + 1)
                nc.vector.scalar_tensor_tensor(out=hTl[:, kt, :], in0=PS[:, turn_bank(kt), :], scalar=cst[:, kt:kt + 1],
                                               in1=hTh[:, kt, :].bitcast(F32), op0=ALU.mult, op1=ALU.subtract).then_inc(hT_lo, 1)
            gate_high(0)
            gate_low(0)
            split_unit(1, range(4))
            for tt in range(2, NT):
                dve.wait_ge(qkv_done, tt + 1)
                for a in range(2):
                    ins = nc.vector.tensor_copy(qn[:, tt, :, a * DH:(a + 1) * DH], qkv[:, tt, 0:256].rearrange("p (v c) -> p v c", v=4))
            ins.then_inc(norm_dve, 1)
            split_unit(1, range(4, KT))
            dve.wait_ge(gsig_tanh, 1)
            nc.vector.tensor_scalar(gsig, gsig, 0.5, 0.5, ALU.mult, ALU.add).then_inc(gsig_done, 1)
            for x in range(4):
                dve.wait_ge(tcmp_a, x + 1)
                nc.vector.tensor_copy(tcmp[DH:P, x, 0:S - 1], PS[DH:P, vec_bank(0, x), 1:S]).then_inc(tcmp_b, 1)
            gate_high(1)
            gate_low(1)
            def sums(w, tt):
                k, q = nvec(w), (w - 2) * NT + tt
                dve.wait_ge(sq_done, q + 2)
                nc.vector.reduce_sum(ss[:, k * tt:k * (tt + 1)], sqt2[:, q % 2, 0:k * DH].rearrange("p (v c) -> p v c", v=k), AX).then_inc(ss_done, 1)

            def rstd(w):
                k = nvec(w)
                if w == 1:
                    dve.wait_ge(sq_done, 1)
                    link(nc.vector.reduce_sum(ss[:, 0:4 * k].rearrange("p (t v) -> p t v", t=NT), sq[:, :, 0:k * DH].rearrange("p t (v c) -> p t v c", v=k), AX))
                else:
                    dve.wait_ge(ss_done, NT * (w - 1))
                    dve.wait_ge(norm_done, w)
                    dve.wait_ge(norm_dve, w)
                if k == 4:
                    rsqrt(rq[:, 0:16], ss[:, 0:16], 1.0 / DH, 16, done=rstd_done)
                else:
                    rsqrt(rq[:, 20:28], ss[:, 0:8], 1.0 / DH, 8)
                    nc.vector.tensor_copy(rq[:, 0:16].rearrange("p (t v) -> p t v", t=NT)[:, :, 0:2],
                                          rq[:, 20:28].rearrange("p (t v) -> p t v", t=NT)).then_inc(rstd_done, 1)

            def normalise(w):
                k = nvec(w)
                dve.wait_ge(rstd_done, w)
                if w == 1:
                    dve.wait_ge(cmp_hidden, 2)
                else:
                    dve.wait_ge(vec_filled, vec_number(w - 1, nvec(w - 1) - 1))
                for tt in range(2, NT):
                    i = qkv[:, tt, 0:k * DH].rearrange("p (v c) -> p v c", v=k)
                    for a in range(2):
                        ins = nc.vector.tensor_tensor(qn[:, tt, 0:k, a * DH:(a + 1) * DH], i,
                                                      rq[:, 4 * tt:4 * tt + k].unsqueeze(2).broadcast_to([P, k, DH]), ALU.mult)
                ins.then_inc(norm_dve, 1)

            def vec_low(w, x):
                n = w - 1
                dve.wait_ge(vec_hi, vec_base[w] + x + 1 - 4)
                kind, s, e = vec_dst(w, x)
                if kind == "q":
                    c = GQ + (0 if n < 4 else 2)
                    nc.vector.scalar_tensor_tensor(out=QQ[DH:P, s, e, :], in0=PS[DH:P, vec_bank(w, x), :], scalar=cst[DH:P, c:c + 1],
                                                   in1=QQ[DH:P, s, e, :].bitcast(F32), op0=ALU.mult, op1=ALU.subtract).then_inc(vec_lo, 1)
                else:
                    c = GQ + 1 if n < 4 else GQ + 4 + e
                    nc.vector.scalar_tensor_tensor(out=Kl[:, s, e, :], in0=PS[:, vec_bank(w, x), :], scalar=cst[:, c:c + 1],
                                                   in1=Kh[:, s, e, :].bitcast(F32), op0=ALU.mult, op1=ALU.subtract).then_inc(vec_lo, 1)

            def bias(t):
                s = STEPS[t]
                n, e, i = s["n"], s["e"], s["i"]
                dve.wait_ge(score, t + 1)
                if t >= 4:
                    dve.wait_ge(turned, t - 3)
                if s["k"] == 0:
                    dve.wait_ge(strip_in[n % 2], 32 * (n // 2 + 1))
                if s["br"] != "cmp":
                    nk = P * (i + 1)
                    nc.vector.tensor_tensor_reduce(out=prob[:, t % 4, 0:nk], in0=PS[:, 2 + t % 2, 0:nk], in1=strip[:, n % 2, e, S - nk:S],
                                                   scale=1.0, scalar=3e38, op0=ALU.add, op1=ALU.min,
                                                   accum_out=mneg[:, t % 4:t % 4 + 1]).then_inc(biased, 1)
                else:
                    link(nc.vector.memset(sc_c, BIG))
                    for q in range(NT):
                        c0 = P * (NT - 1 - q) + CMP_LEN - 1
                        m = 7 + 8 * q
                        ins = nc.vector.tensor_tensor_reduce(out=sc_c[:, q, 0:m], in0=PS[:, 2 + t % 2, 32 * q:32 * q + m],
                                                             in1=strip[:, n % 2, e, c0:c0 + 16 * (m - 1) + 1:16], scale=1.0, scalar=1e29,
                                                             op0=ALU.add, op1=ALU.min, accum_out=mneg_c[:, q:q + 1])
                    link(ins)
                    nc.vector.tensor_tensor(sc_c, sc_c, mneg_c.unsqueeze(2).broadcast_to([P, NT, 32]), ALU.subtract).then_inc(biased, 1)

            def scale(t):
                s = STEPS[t]
                dve.wait_ge(exped, t + 1)
                n, e, i = s["n"], s["e"], s["i"]
                if s["br"] == "own":
                    nk = P * (i + 1)
                    link(nc.vector.reciprocal(rsum[:, t % 4:t % 4 + 1], rsum[:, t % 4:t % 4 + 1]))
                    nc.vector.tensor_scalar(prob[:, t % 4, 0:nk], prob[:, t % 4, 0:nk], rsum[:, t % 4:t % 4 + 1], None, ALU.mult).then_inc(scaled, 1)
                elif s["br"] != "cmp":
                    nk = P * (i + 1)
                    h = cat(s["br"]) * HN + 2 * (n - 4) + e
                    link(nc.vector.reciprocal(rsum[:, t % 4:t % 4 + 1], rsum[:, t % 4:t % 4 + 1]))
                    nc.vector.tensor_scalar(prob[:, t % 4, 0:nk], prob[:, t % 4, 0:nk], rsum[:, t % 4:t % 4 + 1], gsig[:, i, h:h + 1],
                                            ALU.mult, ALU.mult).then_inc(scaled, 1)
                else:
                    h = 2 * (n - 4) + e
                    pc = prob[:, t % 4, 0:P].rearrange("p (a b) -> p a b", a=NT)
                    link(nc.vector.reduce_sum(rsum_c, pc, AX))
                    link(nc.vector.tensor_scalar(rsum_c, rsum_c, 1e-30, None, ALU.max))
                    link(nc.vector.reciprocal(rsum_c, rsum_c))
                    link(nc.vector.tensor_tensor(rsum_c, rsum_c, gsig[:, :, h], ALU.mult))
                    nc.vector.tensor_tensor(pc, pc, rsum_c.unsqueeze(2).broadcast_to([P, NT, 32]), ALU.mult).then_inc(scaled, 1)

            def pt_low(t):
                s = STEPS[t]
                dve.wait_ge(pt_hi, t + 1)
                if s["br"] == "cmp":
                    nc.vector.tensor_tensor(PTl[0:32, s["u"] % 2, 0, :], PS[0:32, 4 + t % 2, :], PTh[0:32, s["u"] % 2, 0, :].bitcast(F32),
                                            ALU.subtract).then_inc(pt_lo, 1)
                else:
                    i = s["i"]
                    nc.vector.tensor_tensor(PTl[:, s["u"] % 2, 0:i + 1, P * i:P * (i + 1)],
                                            PS[:, 4 + t % 2, 0:P * (i + 1)].rearrange("p (j q) -> p j q", j=i + 1),
                                            PTh[:, s["u"] % 2, 0:i + 1, P * i:P * (i + 1)].bitcast(F32), ALU.subtract).then_inc(pt_lo, 1)

            rstd(1)
            normalise(1)
            vec_low(1, 0)
            vec_low(1, 1)
            split_unit(2, range(4))
            vec_low(1, 2)
            vec_low(1, 3)
            split_unit(2, range(4, KT))
            gate_high(2)
            gate_low(2)
            dve.wait_ge(cmp_out, 1)
            kps = PS[0:NCMP, cmp_bank["out"], 0:P]
            vps = PS[0:NCMP, cmp_bank["out"], P:2 * P].rearrange("p (g c) -> p g c", g=2)
            dve.wait_ge(skew_out, 32)
            link(nc.vector.tensor_copy(F[0:NCMP, 13600:13728], kps))
            ksb = F[0:NCMP, 13600:13728].rearrange("p (g c) -> p g c", g=2)
            link(nc.vector.tensor_tensor(kcn[0:NCMP, :, 0:DH], ksb, ksb, ALU.mult))
            link(nc.vector.reduce_sum(s_k[0:NCMP, :], kcn[0:NCMP, :, 0:DH], AX))
            rsqrt(st[0:NCMP, 84:86], s_k[0:NCMP, :], 1.0 / DH, 2, NCMP)
            for a in range(2):
                ins = nc.vector.tensor_tensor(kcn[0:NCMP, :, a * DH:(a + 1) * DH], ksb,
                                              st[0:NCMP, 84:86].unsqueeze(2).broadcast_to([NCMP, 2, DH]), ALU.mult)
                if a == 0:
                    link(ins)
            ins.then_inc(kcn_done, 1)
            dve.wait_ge(vc_hi, 1)
            for g in range(2):
                for a in (0, 2):
                    ins = nc.vector.tensor_tensor(VCl[0:NCMP, g, a * DH:(a + 1) * DH], vps[:, g, :],
                                                  VCh[0:NCMP, g, a * DH:(a + 1) * DH].bitcast(F32), ALU.subtract)
            ins.then_inc(vc_lo, 1)
            dve.wait_ge(kc_hi, 1)
            for g in range(2):
                ins = nc.vector.scalar_tensor_tensor(out=KCl[:, g, 0:NCMP], in0=PS[:, cmp_bank["turned"], 32 * g:32 * g + NCMP], scalar=cst[:, GQ + 3:GQ + 4],
                                                     in1=KCh[:, g, 0:NCMP].bitcast(F32), op0=ALU.mult, op1=ALU.subtract)
            ins.then_inc(kc_lo, 1)

            for tt in range(3):
                sums(2, tt)
            for t in range(T + LAG):
                n, k, w = (STEPS[t]["n"], STEPS[t]["k"], STEPS[t]["n"] + 2) if t < T else (NPAIR, 0, 0)
                if t < T:
                    bias(t)
                if 1 <= t <= T:
                    scale(t - 1)
                if t - 1 in NORM:
                    normalise(NORM[t - 1])
                for j, end in gate_end.items():
                    if t == end + 1 and j + 1 < NGATE:
                        gate_low(j + 1)
                if t >= LAG:
                    pt_low(t - LAG)
                if T - 2 <= t < T + 1:
                    m = 2 * (t - T + 2) + 1
                    dve.wait_ge(yt_hi, m + 1)
                    nc.vector.tensor_tensor(yTl[:, m, :], ytmp[:, m, :], yTh[:, m, :].bitcast(F32), ALU.subtract).then_inc(yt_lo[1], 1)
                if proj_end(t):
                    sums(*proj_end(t))
                if t in VEC:
                    vec_low(*VEC[t])
                if t < T:
                    if t in SPLIT:
                        w_low(*SPLIT[t])
                    if t in NORM:
                        rstd(NORM[t])
                    if n > 0 and k == VLAG - 1:
                        dve.wait_ge(pv_done, STEPS[last_t[n - 1]]["u"] + 1)
                        if n > 1:
                            dve.wait_ge(y_out, 16 * (n - 1))
                        else:
                            dve.wait_ge(cmp_hidden, 2)
                        nc.vector.tensor_copy(ystage, PS[:, 6, :]).then_inc(y_evac, 1)
            dve.wait_ge(yt_hi, 8)
            nc.vector.tensor_tensor(yTl[:, 7, :], PS[:, 6, :], yTh[:, 7, :].bitcast(F32), ALU.subtract).then_inc(y_evac, 1)

            for mg in range(2):
                for m in range(4):
                    dve.wait_ge(chunk_done, cidx[("bra", mg, 3)] + 1)
                    dve.wait_ge(ga_in[m], 16 * (mg + 1))
                    nc.vector.scalar_tensor_tensor(out=ga[:, m, :], in0=ga[:, m, :], scalar=1.0, in1=PS[:, m, :],
                                                   op0=ALU.add, op1=ALU.mult).then_inc(brA_done, 1)
                for m in range(4):
                    i = 4 * mg + m
                    dve.wait_ge(chunk_done, cidx[("brb", mg, 3)] + 1)
                    dve.wait_ge(gb_in[i % 2], 16 * (i // 2 + 1))
                    dve.wait_ge(brA_done, i + 1)
                    nc.vector.scalar_tensor_tensor(out=gb[:, i % 2, :], in0=gb[:, i % 2, :], scalar=1.0, in1=PS[:, 4 + m, :],
                                                   op0=ALU.add, op1=ALU.mult).then_inc(brB_done, 1)
                    dve.wait_ge(brB_done, i + 1)
                    nc.vector.tensor_tensor(ga[:, m, :], ga[:, m, :], gb[:, i % 2, :], ALU.add).then_inc(br_sum, 1)
                for m in range(4):
                    i = 4 * mg + m
                    dve.wait_ge(mT_hi, i + 1)
                    nc.vector.scalar_tensor_tensor(out=mTl[:, i, :], in0=ga[:, m, :], scalar=0.5, in1=mTh[:, i, :].bitcast(F32),
                                                   op0=ALU.mult, op1=ALU.subtract).then_inc(mT_lo, 1)
            for k in range(2):
                dve.wait_ge(pT_hi, k + 1)
                nc.vector.tensor_tensor(pTl[:, k, :], PS[:, 4 + k, :], pTh[:, k, :].bitcast(F32), ALU.subtract).then_inc(pT_lo, 1)
            dve.wait_ge(xT_done, 8)
            for mg in range(2):
                for m in range(4):
                    i = 4 * mg + m
                    dve.wait_ge(chunk_done, cidx[("wo", mg, KT - 1)] + 1)
                    nc.vector.tensor_tensor(x1T[:, i, :], PS[:, i, :], x1T[:, i, :], ALU.add).then_inc(x1_done, 1)
            for a, b, n in ((0, 1, 6), (2, 3, 8)):
                dve.wait_ge(x1_sq, n)
                link(nc.vector.tensor_tensor(sqt[:, a, :], sqt[:, a, :], sqt[:, b, :], ALU.add))
            link(nc.vector.tensor_tensor(sqt[:, 0, :], sqt[:, 0, :], sqt[:, 2, :], ALU.add))
            dve.wait_ge(ssq_done, 4)
            nc.vector.tensor_tensor(sumsq, sumsq, sqt[:, 0, :], ALU.add).then_inc(sq_summed, 1)
            dve.wait_ge(tok_sum, 1)
            rsqrt(st[:, 80:84], PS[:, 4, 0:4], 1.0 / D, 4)
            for tt in range(NT):
                ins = nc.vector.tensor_scalar(rdiag[:, tt * P:(tt + 1) * P], ident, st[:, 80 + tt:81 + tt], None, ALU.mult)
            ins.then_inc(rdiag_done, 1)
            dve.wait_ge(bc_done, 1)
            for i in range(KT):
                if i >= 2:
                    dve.wait_ge(h2_lo, i - 1)
                nc.vector.scalar_tensor_tensor(out=hst[:, i % 2, :], in0=x1T[:, i, :], scalar=cst[:, 8 + i:9 + i], in1=rbc,
                                               op0=ALU.mult, op1=ALU.mult).then_inc(h2_f, 1)
            for u in range(NF // 2):
                for q in range(2):
                    f = 2 * u + q
                    for half, (dst, sb_, sm) in enumerate(((ya, ya_bias, ya_conv), (yl, yl_bias, yl_conv))):
                        b = up_bank(u) + 2 * half + q
                        col = half * NF + f
                        dve.wait_ge(sb_, f + 1)
                        link(nc.vector.scalar_tensor_tensor(out=dst[:, f % 2, 1:S], in0=PS[:, b, 0:S - 1], scalar=cst[:, CONVW + 44 + col:CONVW + 45 + col],
                                                            in1=dst[:, f % 2, 1:S], op0=ALU.mult, op1=ALU.add))
                        nc.vector.scalar_tensor_tensor(out=dst[:, f % 2, 2:S], in0=PS[:, b, 0:S - 2], scalar=cst[:, CONVW + col:CONVW + 1 + col],
                                                       in1=dst[:, f % 2, 2:S], op0=ALU.mult, op1=ALU.add).then_inc(sm, 1)
                for q in range(2):
                    f = 2 * u + q
                    dve.wait_ge(gelu_done, f + 1)
                    dve.wait_ge(yl_conv, f + 1)
                    nc.vector.tensor_tensor(ya[:, f % 2, :], ya[:, f % 2, :], yl[:, f % 2, :], ALU.mult).then_inc(glu_done, 1)
                for q in range(2):
                    f = 2 * u + q
                    dve.wait_ge(gT_hi, f + 1)
                    nc.vector.tensor_tensor(gTl[:, f, :], ya[:, f % 2, :], gTh[:, f, :].bitcast(F32), ALU.subtract).then_inc(gT_lo, 1)
            for mg in range(2):
                for m in range(4):
                    i = 4 * mg + m
                    dve.wait_ge(chunk_done, cidx[("dn", mg, NF - 1)] + 1)
                    nc.vector.tensor_tensor(x1T[:, i, :], PS[:, 4 * mg + m, :], x1T[:, i, :], ALU.add).then_inc(x2_done, 1)
                for tt in range(NT):
                    dve.wait_ge(x2_tr, 4 * mg + tt + 1)
                    nc.vector.tensor_copy(x2n[:, tt, mg * 512:(mg + 1) * 512], PS[:, 4 * mg + tt, :]).then_inc(x2n_done, 1)
            for k in range(8):
                ng, tt = k // 4, k % 4
                dve.wait_ge(th_done, k + 1)
                dve.wait_ge(pp_in, 16 * 4 if k < 4 else 16 * 8)
                nc.vector.scalar_tensor_tensor(out=thb[:, k % 4, :], in0=thb[:, k % 4, :], scalar=1.0, in1=ppb[:, k % 4, :],
                                               op0=ALU.add, op1=ALU.mult).then_inc(th_mul, 1)
                dve.wait_ge(th_mul, k + 1)
                dve.wait_ge(x2n_done, 8)
                o = x2n[:, tt, ng * 512:(ng + 1) * 512]
                nc.vector.tensor_tensor(o, o, thb[:, k % 4, :], ALU.add).then_inc(o_done, 1)

        @block.tensor
        def _(pe):
            def three(o, ah, al, bh, bl, first, last):
                nc.tensor.matmul(o, ah, bh, start=first, stop=False)
                nc.tensor.matmul(o, ah, bl, start=False, stop=False)
                return nc.tensor.matmul(o, al, bh, start=False, stop=last)

            def turn_consts():
                pe.wait_ge(const_in, 16 * 11)
                pe.wait_ge(pool_const, 4)
                for k, (o0, nr) in enumerate(((0, CONVW), (CONVW, P), (CONVW + P, 4))):
                    nc.tensor.transpose(PS[:, 0, o0:o0 + nr], rows[0:nr, k, :], ident[0:nr, 0:nr]).then_inc(cst_turned, 1)

            def turn_input(kt):
                if kt == 0:
                    pe.wait_ge(pool_const, 4)
                if kt >= 6:
                    pe.wait_ge(hT_lo, kt - 5)
                for tt in range(NT):
                    pe.wait_ge(h_nat, tt + 1)
                    ins = nc.tensor.transpose(PS[:, turn_bank(kt), P * tt:P * (tt + 1)], xnat[:, tt, P * kt:P * (kt + 1)], ident)
                ins.then_inc(x_turned, 1)

            def project(w, tt, kts=range(KT)):
                c = ucols(w)
                if kts[0] == 0:
                    before = 4 * w + tt - (1 if w > 2 or (w, tt) == (2, 3) else 2)
                    if before >= 0:
                        pe.wait_ge(qkv_done, before + 1)
                    if w == 0:
                        pe.wait_ge(hT_lo, 5)
                for kt in kts:
                    wait_weights(pe, w, kt)
                    pe.wait_ge(hT_lo, kt + 1)
                    t_ = slice(P * tt, P * (tt + 1))
                    ins = three(PS[:, proj_bank(w, tt), 0:c], hTh[:, kt, t_], hTl[:, kt, t_], Wh[:, kt, 0:c], Wl[:, kt, 0:c], kt == 0, kt == KT - 1)
                    if tt == NT - 1 and kt < KT - 1:
                        ins.then_inc(w_used, 1)
                if kts[-1] == KT - 1:
                    ins.then_inc(proj_filled, 1)

            def turn_vector(w, x):
                if w == 0 and x >= 2:
                    pe.wait_ge(tcmp_b, x - 1)
                elif w == 1 and x < 2:
                    pe.wait_ge(tcmp_b, x + 3)
                elif w == 1:
                    pe.wait_ge(vec_lo, x - 1)
                elif w > 1:
                    pe.wait_ge(vec_lo, vec_number(w, x) - 5)
                pe.wait_ge(norm_done, w + 1)
                pe.wait_ge(norm_dve, w + 1)
                for tt in range(NT):
                    ins = nc.tensor.transpose(PS[:, vec_bank(w, x), P * tt:P * (tt + 1)], qn[:, tt, x, :], ident)
                ins.then_inc(vec_filled, 1)

            def gate(j, kts=range(KT)):
                if kts[0] == 0:
                    pe.wait_ge(g_lo[0], j + 1)
                    if j:
                        pe.wait_ge(gate_tanh, j)
                for kt in kts:
                    if kt == 4:
                        pe.wait_ge(g_lo[1], j + 1)
                    ins = three(PS[:, 7, :], Gh[:, kt, :], Gl[:, kt, :], hTh[:, kt, :], hTl[:, kt, :], kt == 0, kt == KT - 1)
                if kts[-1] == KT - 1:
                    ins.then_inc(gate_filled, 1)

            def compress(kv):
                pe.wait_ge(w1k_in, 16 * (kv + 1))
                pe.wait_ge(bp_done, kv + 1)
                pe.wait_ge(hT_lo, KT)
                o = bp[:, kv, 0:992].rearrange("p (g l n) -> p g l n", g=2, l=16)
                for c in range(16):
                    wt = w1k[:, c, :]
                    ins = nc.tensor.matmul(PS[:, cmp_bank["hidden"] + kv, 0:62].rearrange("p (g n) -> p g n", g=2), wt, o[:, :, c, :],
                                           start=(c == 0), stop=(c == 15))
                ins.then_inc(cmp_hidden, 1)

            def compress_out():
                pe.wait_ge(hid_done, 2)
                pe.wait_ge(w2c_in, 32)
                pe.wait_ge(vec_lo, 4)
                for kv in range(2):
                    for g in range(2):
                        o = (2 * kv + g) * DH
                        ins = nc.tensor.matmul(PS[0:NCMP, cmp_bank["out"], o:o + DH], hid[:, 62 * kv + 31 * g:62 * kv + 31 * (g + 1)], w2c[:, kv, :],
                                               start=True, stop=True)
                ins.then_inc(cmp_out, 1)

            def turn_compressed_keys():
                pe.wait_ge(kcn_done, 1)
                for g in range(2):
                    ins = nc.tensor.transpose(PS[:, cmp_bank["turned"], 32 * g:32 * g + NCMP], kcn[0:NCMP, g, :], ident[0:NCMP, 0:NCMP])
                ins.then_inc(cmp_turned, 1)

            def scores(t):
                s = STEPS[t]
                n, e, i = s["n"], s["e"], s["i"]
                if t < 2:
                    pe.wait_ge(hid_done, t + 1)
                if t >= 2:
                    pe.wait_ge(biased, t - 1)
                if s["k"] == 0:
                    pe.wait_ge(vec_lo, vec_base[n + 1] + nvec(n + 1) - 4)
                o = PS[:, 2 + t % 2, :]
                if s["br"] == "cmp":
                    pe.wait_ge(kc_lo, 1)
                    g = (n - 4) // 2
                    for q in range(NT):
                        nc.tensor.matmul(o[:, 32 * q:32 * q + 32], QQ[:, n % 2, e, P * q:P * (q + 1)], KCh[:, g, :], start=True, stop=False)
                        ins = nc.tensor.matmul(o[:, 32 * q:32 * q + 32], QQ[:, n % 2, e, P * q:P * (q + 1)], KCl[:, g, :], start=False, stop=True)
                else:
                    ks, ke = kslot(n, e, s["br"])
                    nk = P * (i + 1)
                    nc.tensor.matmul(o[:, 0:nk], QQ[:, n % 2, e, P * i:P * (i + 1)], Kh[:, ks, ke, 0:nk], start=True, stop=False)
                    ins = nc.tensor.matmul(o[:, 0:nk], QQ[:, n % 2, e, P * i:P * (i + 1)], Kl[:, ks, ke, 0:nk], start=False, stop=True)
                ins.then_inc(score, 1)

            def turn_probs(t):
                s = STEPS[t]
                pe.wait_ge(scaled, t + 1)
                if t == 0:
                    pe.wait_ge(vc_lo, 1)
                if t == 1:
                    pe.wait_ge(kc_lo, 1)
                if t >= 2:
                    pe.wait_ge(pt_lo, t - 1)
                if s["br"] == "cmp":
                    for q in range(NT):
                        ins = nc.tensor.transpose(PS[0:32, 4 + t % 2, P * q:P * (q + 1)], prob[:, t % 4, 32 * q:32 * q + 32], ident)
                else:
                    for j in range(s["i"] + 1):
                        ins = nc.tensor.transpose(PS[:, 4 + t % 2, P * j:P * (j + 1)], prob[:, t % 4, P * j:P * (j + 1)], ident)
                ins.then_inc(turned, 1)

            def values(t):
                s = STEPS[t]
                n, e, u = s["n"], s["e"], s["u"]
                pe.wait_ge(pt_lo, t + 1)
                opening = u == STEPS[first_t[n]]["u"]
                closing = t == last_t[n]
                if opening:
                    pe.wait_ge(v_lo, min(n + 1, 5) if n < 6 else 6)
                    if n == 0:
                        pe.wait_ge(qkv_done, 4 * 2 + 2)
                    if n > 0:
                        pe.wait_ge(y_evac, n)
                c0 = 0 if e == 0 else DH
                if s["br"] == "cmp":
                    pe.wait_ge(vc_lo, 1)
                    g = (n - 4) // 2
                    ins = three(PS[:, 6, :], VCh[0:32, g, c0:c0 + P], VCl[0:32, g, c0:c0 + P], PTh[0:32, u % 2, 0, :], PTl[0:32, u % 2, 0, :],
                                False, closing)
                else:
                    vs = vslot(n, s["br"])
                    for j in (reversed(range(NT)) if closing else range(NT)):
                        q = slice(P * j, S)
                        ins = three(PS[:, 6, q], Vh[:, vs, j, c0:c0 + P], Vl[:, vs, j, c0:c0 + P], PTh[:, u % 2, j, q], PTl[:, u % 2, j, q],
                                    opening and j == 0, closing and j == 0)
                ins.then_inc(pv_done, 1)

            for kt in range(4):
                turn_input(kt)
            turn_consts()
            for kt in range(4, KT):
                turn_input(kt)
            for tt in range(NT):
                project(0, tt)
            gate(0)
            for x in range(4):
                turn_vector(0, x)
            for tt in range(NT):
                if tt == 3:
                    compress(0)
                project(1, tt)
            gate(1)
            compress(1)
            for x in range(4):
                turn_vector(1, x)
            project(2, 0)
            compress_out()
            project(2, 1)
            turn_compressed_keys()
            project(2, 2)
            for t in range(T):
                if STEPS[t]["k"]:
                    scores(t)
                if t >= LAG:
                    turn_probs(t - LAG)
                if t >= VLAG and STEPS[t - VLAG]["last"]:
                    values(t - VLAG)
                if t in VEC:
                    turn_vector(*VEC[t])
                if t in PROJ:
                    project(*PROJ[t])
                if not STEPS[t]["k"]:
                    scores(t)
                if t in GATE:
                    gate(*GATE[t])

            def turn_x(tt):
                if tt == 2:
                    pe.wait_ge(xg_in, 16)
                else:
                    pe.wait_ge(xs_in, 16 * (tt + 1 if tt < 2 else 3))
                src = xg if tt == 2 else xs
                b = 4 + 2 * (tt % 2)
                if tt == 0:
                    pe.wait_ge(brB_done, 4)
                if tt >= 1:
                    pe.wait_ge(brB_done, 8)
                if tt >= 2:
                    pe.wait_ge(xT_done, 2 * tt - 2)
                for kt in range(KT):
                    ins = nc.tensor.transpose(PS[:, b + kt // 4, P * (kt % 4):P * (kt % 4 + 1)], src[:, P * kt:P * (kt + 1)], ident)
                ins.then_inc(xs_tr, 1)

            def turn_p():
                pe.wait_ge(xg_in, 16 * 5)
                pe.wait_ge(xT_done, 8)
                for k in range(2):
                    for tt in range(NT):
                        ins = nc.tensor.transpose(PS[:, 4 + k, P * tt:P * (tt + 1)], xg[:, tt * PLE + P * k:tt * PLE + P * (k + 1)], ident)
                    ins.then_inc(p_tr, 1)

            def token_sums():
                pe.wait_ge(sq_summed, 1)
                pe.wait_ge(x1_done, KT)
                for tt in range(NT):
                    ins = nc.tensor.matmul(PS[:, 4, tt:tt + 1], sumsq[:, P * tt:P * (tt + 1)], ones[:, 0:1], start=True, stop=True)
                ins.then_inc(tok_sum, 1)

            def spread():
                pe.wait_ge(rdiag_done, 1)
                for tt in range(NT):
                    ins = nc.tensor.matmul(PS[:, 4, P * tt:P * (tt + 1)], ones, rdiag[:, P * tt:P * (tt + 1)], start=True, stop=True)
                ins.then_inc(bc_mm, 1)

            def turn_x2(half):
                pe.wait_ge(x2_done, 4 * half + 4)
                for tt in range(NT):
                    for kt in range(4):
                        ins = nc.tensor.transpose(PS[:, 4 * half + tt, P * kt:P * (kt + 1)], x1T[:, 4 * half + kt, P * tt:P * (tt + 1)], ident)
                    ins.then_inc(x2_tr, 1)

            for c in range(NC):
                kind, a, kt = CHUNKS[c]
                if T + c < T + VLAG:
                    if STEPS[T + c - VLAG]["last"]:
                        values(T + c - VLAG)
                    if c < LAG:
                        turn_probs(T + c - LAG)
                if c == 10:
                    turn_x(0)
                if (kind, a, kt) == ("wo", 0, 1):
                    turn_x(1)
                if (kind, a, kt) == ("wo", 0, 3):
                    turn_x(2)
                if (kind, a, kt) == ("wo", 0, 5):
                    turn_x(3)
                if (kind, a, kt) == ("wo", 1, 0):
                    turn_p()
                if (kind, a, kt) == ("ple", 1, 0):
                    token_sums()
                if (kind, a, kt) == ("ple", 1, 1):
                    spread()
                if (kind, a, kt) == ("dn", 1, 8):
                    turn_x2(0)
                if (kind, a, kt) == ("pg", 0, 6):
                    turn_x2(1)
                if kind == "bra":
                    pe.wait_ge(yt_lo[kt % 2], kt // 2 + 1)
                    act_h, act_l = yTh[:, kt, :], yTl[:, kt, :]
                    b0 = 0
                    if a == 0 and kt == 0:
                        pe.wait_ge(gate_tanh, NGATE)
                        pe.wait_ge(biased, T)
                    if a == 1 and kt == 0:
                        pe.wait_ge(brA_done, 4)
                elif kind == "brb":
                    if kt < 3:
                        pe.wait_ge(yt_lo[kt % 2], 2 + kt // 2 + 1)
                    else:
                        pe.wait_ge(y_evac, 8)
                        pe.wait_ge(yt_hi, 8)
                    act_h, act_l = yTh[:, 4 + kt, :], yTl[:, 4 + kt, :]
                    b0 = 4
                    if kt == 0:
                        if a:
                            pe.wait_ge(xT_done, 2)
                        else:
                            pe.wait_ge(pt_lo, T)
                elif kind == "wo":
                    pe.wait_ge(mT_lo, kt + 1)
                    act_h, act_l = mTh[:, kt, :], mTl[:, kt, :]
                    b0 = 4 * a
                    if kt == 0:
                        pe.wait_ge(brA_done, 8)
                        if a:
                            pe.wait_ge(pT_lo, 2)
                elif kind == "ple":
                    b0 = None
                    if kt == 0 and a == 0:
                        pe.wait_ge(x1_done, 4)
                elif kind == "up":
                    pe.wait_ge(h2_lo, kt + 1)
                    act_h, act_l = h2h[:, kt, :], h2l[:, kt, :]
                    b0 = up_bank(a)
                    if kt == 0:
                        if a == 0:
                            pe.wait_ge(x1_done, 8)
                            pe.wait_ge(bc_done, 1)
                        elif a == 1:
                            pe.wait_ge(pp_ev, 8)
                        else:
                            pe.wait_ge(ya_conv, 2 * a - 2)
                            pe.wait_ge(yl_conv, 2 * a - 2)
                elif kind == "dn":
                    pe.wait_ge(gT_lo, kt + 1)
                    act_h, act_l = gTh[:, kt, :], gTl[:, kt, :]
                    b0 = 4 * a
                    if kt == 0:
                        u = 9 + a
                        pe.wait_ge(ya_conv, 2 * u + 2)
                        pe.wait_ge(yl_conv, 2 * u + 2)
                else:
                    pe.wait_ge(x2_lo, kt + 1)
                    b0 = None
                    if kt == 0:
                        pe.wait_ge(x2n_done, 4 * (a + 1))
                if kind == "pg" and a == 1:
                    continue
                pe.wait_ge(w2_lo, c + 1)
                last = kt == {"bra": 3, "brb": 3, "wo": KT - 1, "ple": 1, "up": KT - 1, "dn": NF - 1, "pg": KT - 1}[kind]
                wh, wl = W2h[:, c % RING, :], W2l[:, c % RING, :]
                for m in (0, 1, 3, 2) if kind == "brb" else range(4):
                    cs = slice(P * m, P * (m + 1))
                    if kind == "ple" and a == 1 and kt == 0:
                        pe.wait_ge(pp_ev, m + 1)
                    if kind == "brb" and a == 0 and kt == 0 and m == 2:
                        pe.wait_ge(y_evac, 8)
                    if kind in ("ple", "pg"):
                        ah, al = (pTh, pTl) if kind == "ple" else (h2h, h2l)
                        b = m
                        ins = three(PS[:, b, :], ah[:, kt, cs], al[:, kt, cs], wh, wl, kt == 0, last)
                    else:
                        ins = three(PS[:, b0 + m, :], wh[:, cs], wl[:, cs], act_h, act_l, kt == 0, last)
                ins.then_inc(chunk_done, 1)
            pe.wait_ge(w2_lo, NC)
            for tt in range(NT):
                for kt in range(KT):
                    w_ = cidx[("pg", 1, kt)] % RING
                    cs = slice(P * tt, P * (tt + 1))
                    ins = three(PS[:, 4 + tt, :], h2h[:, kt, cs], h2l[:, kt, cs], W2h[:, w_, :], W2l[:, w_, :], kt == 0, kt == KT - 1)
                ins.then_inc(tail_done, 1)


_INS = ['x', 'p', 'rel_bias', 'attn_norm', 'w_in', 'moba_q_gain', 'moba_k_gain', 'nsa_q_gain', 'nsa_k_gain',
        'cmp_pos_k', 'cmp_w1_k', 'cmp_w2_k', 'cmp_pos_v', 'cmp_w1_v', 'cmp_w2_v', 'w_br_moba', 'w_br_nsa', 'w_o',
        'ffn_norm', 'w_up', 'conv_w', 'conv_b', 'w_down', 'w_ple_gate', 'w_ple']


def kernel(**inputs):
    import numpy as _np
    import concourse.bacc as _bacc
    from concourse.bass_utils import run_bass_kernel_spmd as _run

    nc = _bacc.Bacc("TRN2", target_bir_lowering=False, num_devices=1)
    arrays, args = {}, {}
    for name in _INS:
        a = _np.ascontiguousarray(inputs[name])
        arrays[f"in_{name}_dram"] = a
        args[name] = nc.dram_tensor(f"in_{name}_dram", a.shape, mybir.dt.from_np(a.dtype), kind="ExternalInput").ap()
    out = nc.dram_tensor("out_0_dram", (1, S, D), F32, kind="ExternalOutput").ap()
    layer(nc, args, out)
    r = _run(nc, [arrays], core_ids=[0])
    return r.results[0]["out_0_dram"]
```
